# Optimizing a Trainium2 kernel written in Bass

```python
import jax, jax.numpy as jnp
from jax import lax
import numpy as np
import math
import jax
import jax.numpy as jnp

D_MODEL = 1024
BATCH = 1
SEQ = 256
DEPTH = 2

CHUNK = 64
N_META = 16
Q_BLOCK = 128
PAD = Q_BLOCK - N_META
N_A_LAYERS = DEPTH // 2
N_B_LAYERS = DEPTH - N_A_LAYERS
RMS_EPS = 1e-6
GN_EPS = 1e-5
ROPE_THETA = 10000.0
MASK_VALUE = -1e30

RET_HEADS = 4
RET_QK_DIM = D_MODEL // RET_HEADS
RET_V_DIM = 2 * D_MODEL // RET_HEADS
RET_IN = 2 * RET_HEADS * RET_QK_DIM + 2 * RET_HEADS * RET_V_DIM

MLA_HEADS = 8
MLA_NOPE = 128
MLA_ROPE = 64
MLA_V = 128
MLA_Q_RANK = 768
MLA_KV_RANK = 512

FFN_HIDDEN = ((8 * D_MODEL + 3 * 256 - 1) // (3 * 256)) * 256


def rmsnorm(x, g):
    xf = x.astype(jnp.float32)
    y = xf * lax.rsqrt(jnp.mean(xf * xf, axis=-1, keepdims=True) + RMS_EPS)
    return (y * g.astype(jnp.float32)).astype(x.dtype)

def rope_tables(pos, dim):
    inv = 1.0 / (ROPE_THETA ** (jnp.arange(0, dim, 2, dtype=jnp.float32) / dim))
    ang = pos.astype(jnp.float32)[:, None] * inv[None, :]
    return jnp.cos(ang), jnp.sin(ang)

def apply_rope(x, cos, sin):
    xf = x.astype(jnp.float32)
    half = x.shape[-1] // 2
    x1, x2 = xf[..., :half], xf[..., half:]
    c = cos[None, :, None, :]
    s = sin[None, :, None, :]
    return jnp.concatenate([x1 * c - x2 * s, x1 * s + x2 * c], axis=-1).astype(x.dtype)

def retention_mixer(hn, w_in, gn_g, w_o, cos, sin, valid):
    B, L, _ = hn.shape
    H, DK, DV, C = RET_HEADS, RET_QK_DIM, RET_V_DIM, CHUNK
    NC = L // C
    dt = hn.dtype
    proj = hn @ w_in
    q = proj[..., :H * DK].reshape(B, L, H, DK)
    k = proj[..., H * DK:2 * H * DK].reshape(B, L, H, DK)
    v = proj[..., 2 * H * DK:2 * H * DK + H * DV].reshape(B, L, H, DV)
    gate = proj[..., 2 * H * DK + H * DV:]
    q = apply_rope(q, cos, sin)
    k = apply_rope(k, cos, sin) * (DK ** -0.5) * valid[None, :, None, None]

    def to_chunks(t):
        return t.reshape(B, NC, C, H, t.shape[-1]).transpose(1, 0, 3, 2, 4)

    log_g = jnp.log1p(-jnp.exp2(-5.0 - jnp.arange(H, dtype=jnp.float32)))
    idx = jnp.arange(C, dtype=jnp.float32)
    intra = jnp.exp(log_g[:, None, None] * jnp.abs(idx[:, None] - idx[None, :])).astype(dt)
    q_dec = jnp.exp(log_g[:, None] * (idx + 1.0)).astype(dt)
    k_dec = jnp.exp(log_g[:, None] * (C - 1.0 - idx)).astype(dt)
    chunk_dec = jnp.exp(log_g * C).astype(dt)

    def step(S, qkv):
        qc, kc, vc = qkv
        sc = jnp.einsum('bhid,bhjd->bhij', qc, kc) * intra
        o = (jnp.einsum('bhij,bhjv->bhiv', sc, vc)
             + jnp.einsum('bhid,bhdv->bhiv', qc * q_dec[:, :, None], S))
        S = S * chunk_dec[:, None, None] + jnp.einsum('bhjd,bhjv->bhdv', kc * k_dec[:, :, None], vc)
        return S, o

    S0 = jnp.zeros((B, H, DK, DV), dt)
    _, o = lax.scan(step, S0, (to_chunks(q), to_chunks(k), to_chunks(v)))
    o = o.transpose(1, 0, 3, 2, 4).reshape(B, L, H, DV)
    of = o.astype(jnp.float32)
    mu = jnp.mean(of, axis=-1, keepdims=True)
    var = jnp.mean(jnp.square(of - mu), axis=-1, keepdims=True)
    on = ((of - mu) * lax.rsqrt(var + GN_EPS)).reshape(B, L, H * DV) * gn_g.astype(jnp.float32)
    return (jax.nn.silu(gate) * on.astype(dt)) @ w_o

def mla_shared_kv(h, norm_kv_g, w_kv_a, kv_a_norm_g, w_kv_b, cos, sin):
    B, L, _ = h.shape
    kv_a = rmsnorm(h, norm_kv_g) @ w_kv_a
    c_kv = rmsnorm(kv_a[..., :MLA_KV_RANK], kv_a_norm_g)
    k_rope = apply_rope(kv_a[..., MLA_KV_RANK:][:, :, None, :], cos, sin)
    kv = (c_kv @ w_kv_b).reshape(B, L, MLA_HEADS, MLA_NOPE + MLA_V)
    k = jnp.concatenate([kv[..., :MLA_NOPE],
                         jnp.broadcast_to(k_rope, (B, L, MLA_HEADS, MLA_ROPE))], axis=-1)
    return k, kv[..., MLA_NOPE:]

def mla_mixer(hn, w_q_a, q_a_norm_g, w_q_b, w_o, k, v, cos, sin, chunk_id, valid_key):
    B, L, _ = hn.shape
    cq = rmsnorm(hn @ w_q_a, q_a_norm_g)
    q = (cq @ w_q_b).reshape(B, L, MLA_HEADS, MLA_NOPE + MLA_ROPE)
    q = jnp.concatenate([q[..., :MLA_NOPE], apply_rope(q[..., MLA_NOPE:], cos, sin)], axis=-1)
    q = q * ((MLA_NOPE + MLA_ROPE) ** -0.5)
    outs = []
    for qb in range(L // Q_BLOCK):
        s, e = qb * Q_BLOCK, (qb + 1) * Q_BLOCK
        sc = jnp.einsum('bqhd,bkhd->bhqk', q[:, s:e], k[:, :e]).astype(jnp.float32)
        mask = (chunk_id[None, :e] <= chunk_id[s:e, None]) & valid_key[None, :e]
        sc = jnp.where(mask[None, None], sc, MASK_VALUE)
        p = jax.nn.softmax(sc, axis=-1).astype(v.dtype)
        outs.append(jnp.einsum('bhqk,bkhd->bqhd', p, v[:, :e]))
    o = jnp.concatenate(outs, axis=1).reshape(B, L, MLA_HEADS * MLA_V)
    return o @ w_o

def swiglu(hn, w1, w3, w2):
    return (jax.nn.silu(hn @ w1) * (hn @ w3)) @ w2

def first_inputs(seed: int = 0) -> dict:
    key = jax.random.key(seed)
    ks = jax.random.split(key, 24)
    f32 = jnp.float32
    res = (2 * DEPTH) ** -0.5

    def w(k, shape, fan_in, scale=1.0):
        return jax.random.normal(k, shape, f32) * (fan_in ** -0.5) * scale

    def gain(k, shape):
        return 1.0 + 0.02 * jax.random.normal(k, shape, f32)

    return {
        "x": jax.random.normal(ks[0], (BATCH, SEQ, D_MODEL), f32),
        "meta": jax.random.normal(ks[1], (N_META, D_MODEL), f32),
        "norm_mix_g": gain(ks[2], (DEPTH, D_MODEL)),
        "norm_ffn_g": gain(ks[3], (DEPTH, D_MODEL)),
        "ret_w_in": w(ks[4], (N_A_LAYERS, D_MODEL, RET_IN), D_MODEL),
        "ret_gn_g": gain(ks[5], (N_A_LAYERS, RET_HEADS * RET_V_DIM)),
        "ret_w_o": w(ks[6], (N_A_LAYERS, RET_HEADS * RET_V_DIM, D_MODEL), RET_HEADS * RET_V_DIM, res),
        "mla_norm_kv_g": gain(ks[7], (D_MODEL,)),
        "mla_w_kv_a": w(ks[8], (D_MODEL, MLA_KV_RANK + MLA_ROPE), D_MODEL),
        "mla_kv_a_norm_g": gain(ks[9], (MLA_KV_RANK,)),
        "mla_w_kv_b": w(ks[10], (MLA_KV_RANK, MLA_HEADS * (MLA_NOPE + MLA_V)), MLA_KV_RANK),
        "mla_w_q_a": w(ks[11], (N_B_LAYERS, D_MODEL, MLA_Q_RANK), D_MODEL),
        "mla_q_a_norm_g": gain(ks[12], (N_B_LAYERS, MLA_Q_RANK)),
        "mla_w_q_b": w(ks[13], (N_B_LAYERS, MLA_Q_RANK, MLA_HEADS * (MLA_NOPE + MLA_ROPE)), MLA_Q_RANK),
        "mla_w_o": w(ks[14], (N_B_LAYERS, MLA_HEADS * MLA_V, D_MODEL), MLA_HEADS * MLA_V, res),
        "ffn_w1": w(ks[15], (DEPTH, D_MODEL, FFN_HIDDEN), D_MODEL),
        "ffn_w3": w(ks[16], (DEPTH, D_MODEL, FFN_HIDDEN), D_MODEL),
        "ffn_w2": w(ks[17], (DEPTH, FFN_HIDDEN, D_MODEL), FFN_HIDDEN, res),
        "final_g": gain(ks[18], (D_MODEL,)),
    }

def first_block(x, meta, norm_mix_g, norm_ffn_g, ret_w_in, ret_gn_g, ret_w_o,
              mla_norm_kv_g, mla_w_kv_a, mla_kv_a_norm_g, mla_w_kv_b,
              mla_w_q_a, mla_q_a_norm_g, mla_w_q_b, mla_w_o,
              ffn_w1, ffn_w3, ffn_w2, final_g):
    B, S, D = x.shape
    L = PAD + N_META + S
    h = jnp.concatenate([jnp.zeros((B, PAD, D), x.dtype),
                         jnp.broadcast_to(meta[None].astype(x.dtype), (B, N_META, D)),
                         x], axis=1)
    slot = jnp.arange(L)
    chunk_id = slot // CHUNK
    valid_key = slot >= PAD
    valid = valid_key.astype(x.dtype)
    pos = slot - PAD
    cos_r, sin_r = rope_tables(pos, RET_QK_DIM)
    cos_m, sin_m = rope_tables(pos, MLA_ROPE)

    k_sh = None
    v_sh = None
    for layer in range(DEPTH):
        hn = rmsnorm(h, norm_mix_g[layer])
        if layer < N_A_LAYERS:
            h = h + retention_mixer(hn, ret_w_in[layer], ret_gn_g[layer], ret_w_o[layer],
                                    cos_r, sin_r, valid)
        else:
            if layer == N_A_LAYERS:
                k_sh, v_sh = mla_shared_kv(h, mla_norm_kv_g, mla_w_kv_a, mla_kv_a_norm_g,
                                           mla_w_kv_b, cos_m, sin_m)
            j = layer - N_A_LAYERS
            h = h + mla_mixer(hn, mla_w_q_a[j], mla_q_a_norm_g[j], mla_w_q_b[j], mla_w_o[j],
                              k_sh, v_sh, cos_m, sin_m, chunk_id, valid_key)
        h = h + swiglu(rmsnorm(h, norm_ffn_g[layer]), ffn_w1[layer], ffn_w3[layer], ffn_w2[layer])
    return rmsnorm(h, final_g)[:, PAD + N_META:]


DEPTH_2 = 1

H_A = 8
HD_A = 64
W_A = H_A * HD_A
MOBA_BLOCK = 256
MOBA_TOPK = 3
Q_CHUNK = 64
NUM_BUCKETS = 32
MAX_EXACT = NUM_BUCKETS // 2
MAX_DISTANCE = 128
H_B = 4
HD_B = 128
W_B = H_B * HD_B
CONV_K = 4
DN_CHUNK = 64
N_GROUPS = 4
EXPERTS_PER_GROUP = 8
TOPK_IN_GROUP = 2
D_FF_EXPERT = 256
D_IN = 3 * W_A + 4 * W_B + 2 * H_B + 2 * D_MODEL
N_MOD = 6
EPS = 1e-6
NEG = -1e30


def rms_norm(x, w):
    xf = x.astype(jnp.float32)
    y = xf * lax.rsqrt(jnp.mean(xf * xf, axis=-1, keepdims=True) + EPS)
    return (y * w.astype(jnp.float32)).astype(x.dtype)

def l2_normalize(t):
    return t * lax.rsqrt(jnp.sum(t * t, axis=-1, keepdims=True) + EPS)

def t5_bucket(dist):
    n = jnp.maximum(dist, 0)
    nf = jnp.maximum(n, 1).astype(jnp.float32)
    large = MAX_EXACT + (jnp.log(nf / MAX_EXACT) / math.log(MAX_DISTANCE / MAX_EXACT)
                         * (NUM_BUCKETS - MAX_EXACT)).astype(jnp.int32)
    large = jnp.minimum(large, NUM_BUCKETS - 1)
    return jnp.where(n < MAX_EXACT, n, large)

def moba_attention(q, k, v, rel_bias):
    B, H, S, hd = q.shape
    L = MOBA_BLOCK
    Sp = -(-S // L) * L
    pad = ((0, 0), (0, 0), (0, Sp - S), (0, 0))
    q, k, v = jnp.pad(q, pad), jnp.pad(k, pad), jnp.pad(v, pad)
    NB, NQ = Sp // L, Sp // Q_CHUNK
    topk = min(MOBA_TOPK, NB)
    scale = HD_A ** -0.5
    k_blocks = k.reshape(B, H, NB, L, hd)
    v_blocks = v.reshape(B, H, NB, L, hd)
    k_mean = jnp.mean(k_blocks.astype(jnp.float32), axis=3)
    q_blk = jnp.arange(Sp) // L
    gate = jnp.einsum('bhsd,bhnd->bhsn', q.astype(jnp.float32), k_mean)
    gate = jnp.where(jnp.arange(NB)[None, :] < q_blk[:, None], gate, NEG)
    _, sel = lax.top_k(gate, topk)
    q_c = q.reshape(B, H, NQ, Q_CHUNK, hd).transpose(2, 0, 1, 3, 4)
    sel_c = sel.reshape(B, H, NQ, Q_CHUNK, topk).transpose(2, 0, 1, 3, 4)
    bi = jnp.arange(B)[:, None, None, None]
    hi = jnp.arange(H)[None, :, None, None]
    hi5 = hi[..., None]
    offs = jnp.arange(L)

    def one_chunk(args):
        q_i, sel_i, i = args
        qb = (i * Q_CHUNK) // L
        q_pos = i * Q_CHUNK + jnp.arange(Q_CHUNK)
        k_sel = k_blocks[bi, hi, sel_i]
        v_sel = v_blocks[bi, hi, sel_i]
        dist_sel = q_pos[None, None, :, None, None] - (sel_i[..., None] * L + offs)
        bias_sel = rel_bias[t5_bucket(dist_sel), hi5].astype(jnp.float32)
        s_sel = jnp.einsum('bhqd,bhqkld->bhqkl', q_i, k_sel).astype(jnp.float32) * scale + bias_sel
        s_sel = jnp.where((sel_i < qb)[..., None], s_sel, NEG)
        k_own = lax.dynamic_index_in_dim(k_blocks, qb, axis=2, keepdims=False)
        v_own = lax.dynamic_index_in_dim(v_blocks, qb, axis=2, keepdims=False)
        dist_own = q_pos[:, None] - (qb * L + offs)[None, :]
        bias_own = rel_bias[t5_bucket(dist_own)].transpose(2, 0, 1).astype(jnp.float32)
        s_own = jnp.einsum('bhqd,bhld->bhql', q_i, k_own).astype(jnp.float32) * scale + bias_own
        s_own = jnp.where(dist_own >= 0, s_own, NEG)
        p = jax.nn.softmax(jnp.concatenate(
            [s_sel.reshape(B, H, Q_CHUNK, topk * L), s_own], axis=-1), axis=-1)
        p_sel = p[..., :topk * L].reshape(B, H, Q_CHUNK, topk, L).astype(v.dtype)
        p_own = p[..., topk * L:].astype(v.dtype)
        return (jnp.einsum('bhqkl,bhqkld->bhqd', p_sel, v_sel)
                + jnp.einsum('bhql,bhld->bhqd', p_own, v_own))

    o = lax.map(one_chunk, (q_c, sel_c, jnp.arange(NQ)))
    o = o.transpose(1, 2, 0, 3, 4).reshape(B, H, Sp, hd)
    return o[:, :, :S]

def causal_depthwise_conv(x, w):
    C = x.shape[-1]
    return lax.conv_general_dilated(
        x, w[:, None, :].astype(x.dtype), window_strides=(1,), padding=[(CONV_K - 1, 0)],
        dimension_numbers=('NWC', 'WIO', 'NWC'), feature_group_count=C)

def gated_delta_rule(q, k, v, beta, g):
    out_dtype = v.dtype
    B, S, H, DK = q.shape
    DV = v.shape[-1]
    C = DN_CHUNK
    N = S // C
    f32 = jnp.float32
    q = l2_normalize(q.astype(f32)) * (DK ** -0.5)
    k = l2_normalize(k.astype(f32))
    v = v.astype(f32)

    def chunk(t):
        return t.reshape(B, N, C, H, -1).transpose(0, 3, 1, 2, 4)

    q, k, v = chunk(q), chunk(k), chunk(v)
    beta = beta.astype(f32).reshape(B, N, C, H).transpose(0, 3, 1, 2)
    G = jnp.cumsum(g.astype(f32).reshape(B, N, C, H).transpose(0, 3, 1, 2), axis=-1)
    tril = jnp.tril(jnp.ones((C, C), bool))
    strict = jnp.tril(jnp.ones((C, C), bool), -1)
    dec = jnp.exp(jnp.where(tril, G[..., :, None] - G[..., None, :], -jnp.inf))
    kb = k * beta[..., None]
    A = jnp.eye(C, dtype=f32) + jnp.where(strict, jnp.einsum('bhnid,bhnjd->bhnij', kb, k) * dec, 0.0)
    u = lax.linalg.triangular_solve(A, v * beta[..., None], left_side=True, lower=True, unit_diagonal=True)
    w = lax.linalg.triangular_solve(A, kb * jnp.exp(G)[..., None], left_side=True, lower=True, unit_diagonal=True)
    P = jnp.einsum('bhnid,bhnjd->bhnij', q, k) * dec
    qg = q * jnp.exp(G)[..., None]
    kd = k * jnp.exp(G[..., -1:] - G)[..., None]
    gl = jnp.exp(G[..., -1])
    xs = tuple(jnp.moveaxis(t, 2, 0) for t in (u, w, qg, P, kd, gl))

    def step(state, inp):
        u_n, w_n, qg_n, P_n, kd_n, gl_n = inp
        v_new = u_n - jnp.einsum('bhck,bhkv->bhcv', w_n, state)
        o_n = jnp.einsum('bhck,bhkv->bhcv', qg_n, state) + jnp.einsum('bhcj,bhjv->bhcv', P_n, v_new)
        state = state * gl_n[..., None, None] + jnp.einsum('bhck,bhcv->bhkv', kd_n, v_new)
        return state, o_n

    _, o = lax.scan(step, jnp.zeros((B, H, DK, DV), f32), xs)
    return o.transpose(1, 0, 3, 2, 4).reshape(B, S, H, DV).astype(out_dtype)

def token_mixer(h, rel_bias, w_in, conv_w, a_log, dt_bias, onorm_w, w_up_a, w_up_b, w_out):
    B, S, _ = h.shape
    proj = h @ w_in
    sizes = (W_A, W_A, W_A, 3 * W_B, W_B, H_B, H_B, D_MODEL, D_MODEL)
    offs = np.cumsum(sizes)[:-1].tolist()
    qa, ka, va, qkv_b, z_b, b_b, a_b, gate_a, gate_b = jnp.split(proj, offs, axis=-1)
    heads_a = lambda t: t.reshape(B, S, H_A, HD_A).transpose(0, 2, 1, 3)
    y_a = moba_attention(heads_a(qa), heads_a(ka), heads_a(va), rel_bias)
    y_a = y_a.transpose(0, 2, 1, 3).reshape(B, S, W_A)
    qkv_b = jax.nn.silu(causal_depthwise_conv(qkv_b, conv_w))
    q_b, k_b, v_b = (t.reshape(B, S, H_B, HD_B) for t in jnp.split(qkv_b, 3, axis=-1))
    beta = jax.nn.sigmoid(b_b)
    g = -jnp.exp(a_log) * jax.nn.softplus(a_b + dt_bias)
    o_b = gated_delta_rule(q_b, k_b, v_b, beta, g)
    o_b = rms_norm(o_b, onorm_w) * jax.nn.silu(z_b.reshape(B, S, H_B, HD_B))
    y_b = o_b.reshape(B, S, W_B)
    m = jax.nn.sigmoid(gate_a) * (y_a @ w_up_a) + jax.nn.sigmoid(gate_b) * (y_b @ w_up_b)
    return m @ w_out

def hier_moe(h, w_rg, b_rg, w_re, b_re, w_e_gate, w_e_up, w_e_down):
    B, S, D = h.shape
    t = h.reshape(-1, D)
    T = t.shape[0]
    pg = jax.nn.softmax((t @ w_rg + b_rg).astype(jnp.float32), axis=-1)
    p_top, g_top = lax.top_k(pg, 1)
    oh_g = jax.nn.one_hot(g_top[:, 0], N_GROUPS, dtype=jnp.float32)
    le = (t @ w_re + b_re).astype(jnp.float32).reshape(T, N_GROUPS, EXPERTS_PER_GROUP)
    le_g = jnp.einsum('tge,tg->te', le, oh_g)
    v2, e2 = lax.top_k(le_g, TOPK_IN_GROUP)
    w2 = jax.nn.softmax(v2, axis=-1) * p_top
    comb_e = jnp.sum(w2[..., None] * jax.nn.one_hot(e2, EXPERTS_PER_GROUP, dtype=jnp.float32), axis=1)
    comb = (oh_g[:, :, None] * comb_e[:, None, :]).astype(t.dtype)
    y = jnp.zeros_like(t)
    for gi in range(N_GROUPS):
        a = jax.nn.silu(jnp.einsum('td,edf->tef', t, w_e_gate[gi])) * jnp.einsum('td,edf->tef', t, w_e_up[gi])
        y = y + jnp.einsum('tef,te,efd->td', a, comb[:, gi], w_e_down[gi])
    return y.reshape(B, S, D)

def second_inputs(seed: int = 0) -> dict:
    key = jax.random.key(seed)
    ks = iter(jax.random.split(key, 32))
    L, D = DEPTH_2, D_MODEL
    G, E, F = N_GROUPS, EXPERTS_PER_GROUP, D_FF_EXPERT

    def nrm(shape, std):
        return std * jax.random.normal(next(ks), shape, jnp.float32)

    x = nrm((BATCH, SEQ, D), 1.0)
    c = nrm((BATCH, D), 1.0)
    rel_bias = nrm((NUM_BUCKETS, H_A), 0.5)
    final_norm_w = 1.0 + nrm((D,), 0.02)
    norm1_w = 1.0 + nrm((L, D), 0.02)
    norm2_w = 1.0 + nrm((L, D), 0.02)
    w_mod = nrm((L, D, N_MOD * D), 0.5 * D ** -0.5)
    b_mod = nrm((L, N_MOD * D), 0.02)
    w_in = nrm((L, D, D_IN), D ** -0.5)
    conv_w = nrm((L, CONV_K, 3 * W_B), CONV_K ** -0.5)
    a_log = jnp.log(jax.random.uniform(next(ks), (L, H_B), jnp.float32, 1.0, 16.0))
    dt = jnp.exp(jax.random.uniform(next(ks), (L, H_B), jnp.float32, math.log(1e-3), math.log(1e-1)))
    dt_bias = dt + jnp.log(-jnp.expm1(-dt))
    onorm_w = 1.0 + nrm((L, HD_B), 0.02)
    w_up_a = nrm((L, W_A, D), W_A ** -0.5)
    w_up_b = nrm((L, W_B, D), W_B ** -0.5)
    w_out = nrm((L, D, D), D ** -0.5)
    w_rg = nrm((L, D, G), D ** -0.5)
    b_rg = nrm((L, G), 0.01)
    w_re = nrm((L, D, G * E), D ** -0.5)
    b_re = nrm((L, G * E), 0.01)
    w_e_gate = nrm((L, G, E, D, F), D ** -0.5)
    w_e_up = nrm((L, G, E, D, F), D ** -0.5)
    w_e_down = nrm((L, G, E, F, D), F ** -0.5)
    return {"x": x, "c": c, "rel_bias": rel_bias, "final_norm_w": final_norm_w,
            "norm1_w": norm1_w, "norm2_w": norm2_w, "w_mod": w_mod, "b_mod": b_mod,
            "w_in": w_in, "conv_w": conv_w, "a_log": a_log, "dt_bias": dt_bias,
            "onorm_w": onorm_w, "w_up_a": w_up_a, "w_up_b": w_up_b, "w_out": w_out,
            "w_rg": w_rg, "b_rg": b_rg, "w_re": w_re, "b_re": b_re,
            "w_e_gate": w_e_gate, "w_e_up": w_e_up, "w_e_down": w_e_down}

def second_block(x, c, rel_bias, final_norm_w, norm1_w, norm2_w, w_mod, b_mod, w_in, conv_w,
              a_log, dt_bias, onorm_w, w_up_a, w_up_b, w_out, w_rg, b_rg, w_re, b_re,
              w_e_gate, w_e_up, w_e_down):
    c_act = jax.nn.silu(c)
    for l in range(DEPTH_2):
        mod = (c_act @ w_mod[l] + b_mod[l])[:, None, :]
        sh1, sc1, g1, sh2, sc2, g2 = jnp.split(mod, N_MOD, axis=-1)
        h = rms_norm(x, norm1_w[l]) * (1.0 + sc1) + sh1
        x = x + g1 * token_mixer(h, rel_bias, w_in[l], conv_w[l], a_log[l], dt_bias[l],
                                 onorm_w[l], w_up_a[l], w_up_b[l], w_out[l])
        h = rms_norm(x, norm2_w[l]) * (1.0 + sc2) + sh2
        x = x + g2 * hier_moe(h, w_rg[l], b_rg[l], w_re[l], b_re[l],
                              w_e_gate[l], w_e_up[l], w_e_down[l])
    return rms_norm(x, final_norm_w)


def setup_inputs(seed=0):
    out = dict(first_inputs(seed))
    for name, value in second_inputs(seed + 1).items():
        if name != "x":
            out[name + "_2"] = value
    return out


def reference(
    x, meta, norm_mix_g, norm_ffn_g, ret_w_in, ret_gn_g, ret_w_o, mla_norm_kv_g, mla_w_kv_a,
    mla_kv_a_norm_g, mla_w_kv_b, mla_w_q_a, mla_q_a_norm_g, mla_w_q_b, mla_w_o, ffn_w1, ffn_w3,
    ffn_w2, final_g, c_2, rel_bias_2, final_norm_w_2, norm1_w_2, norm2_w_2, w_mod_2, b_mod_2,
    w_in_2, conv_w_2, a_log_2, dt_bias_2, onorm_w_2, w_up_a_2, w_up_b_2, w_out_2, w_rg_2,
    b_rg_2, w_re_2, b_re_2, w_e_gate_2, w_e_up_2, w_e_down_2,
):
    x = first_block(
        x, meta, norm_mix_g, norm_ffn_g, ret_w_in, ret_gn_g, ret_w_o, mla_norm_kv_g, mla_w_kv_a,
        mla_kv_a_norm_g, mla_w_kv_b, mla_w_q_a, mla_q_a_norm_g, mla_w_q_b, mla_w_o, ffn_w1,
        ffn_w3, ffn_w2, final_g,
    )
    return second_block(
        x, c_2, rel_bias_2, final_norm_w_2, norm1_w_2, norm2_w_2, w_mod_2, b_mod_2, w_in_2,
        conv_w_2, a_log_2, dt_bias_2, onorm_w_2, w_up_a_2, w_up_b_2, w_out_2, w_rg_2, b_rg_2,
        w_re_2, b_re_2, w_e_gate_2, w_e_up_2, w_e_down_2,
    )


_drawn_inputs = setup_inputs


def setup_inputs(seed=0):
    import zlib

    import numpy as np

    out = dict(_drawn_inputs(seed))
    spreads = {}
    factors = {'norm_mix_g': 3.749,
     'norm_ffn_g': 4.391,
     'ret_gn_g': 8.0,
     'mla_norm_kv_g': 8.0,
     'mla_kv_a_norm_g': 8.0,
     'mla_q_a_norm_g': 8.0,
     'rel_bias_2': 3.152,
     'final_norm_w_2': 7.78,
     'norm1_w_2': 8.0,
     'norm2_w_2': 4.781,
     'b_mod_2': 3.458,
     'onorm_w_2': 8.0,
     'b_rg_2': 8.0,
     'b_re_2': 23.304}
    for name, (base, spread) in spreads.items():
        noise = np.random.default_rng([zlib.crc32(name.encode()), seed]).standard_normal(out[name].shape)
        drawn = base * np.exp(spread * noise) if base else spread * noise
        out[name] = jnp.asarray(drawn.astype(out[name].dtype))
    for name, factor in factors.items():
        out[name] = (out[name] * factor).astype(out[name].dtype)
    return out
```

```python
from contextlib import ExitStack

import numpy as np

import concourse.bass as bass
from concourse import mybir

F32 = mybir.dt.float32
ALU = mybir.AluOpType
ACT = mybir.ActivationFunctionType
AX = mybir.AxisListType.X

P = 128
D = 1024
DT = D // P
META, SEQ = 16, 256
T0 = META + SEQ
TOK = [(0, META), (META, META + P), (META + P, T0)]
PAD = P - META
CHUNK = 64
RMS_EPS, GN_EPS = 1e-6, 1e-5
NEG = -1e30

RH, RDK, RDV = 4, 256, 512
MH, NOPE, ROPE = 8, 128, 64
QR, KVR = 768, 512
QT, KVT = QR // P, KVR // P
FF = 2816
FT = FF // P
AH, AHD = 8, 64
BH, BHD = 4, 128
CONV = 4
NG, EPG, EF = 4, 8, 256
NE = NG * EPG
BUCKETS = 32
MODS = 6

UB = 8
UNIT = UB * P
SLOTS = 12
BANKS = 4

VEC = {}
_at = 0
for _name, _n in [("c", DT), ("b_mod", MODS * DT), ("mix0", DT), ("ffn0", DT), ("gn", 16), ("kv", DT), ("mix1", DT),
                  ("kva", KVT), ("qa", QT), ("ffn1", DT), ("final", DT), ("n1", DT), ("n2", DT), ("final2", DT),
                  ("onorm", 1), ("conv", 12 * CONV), ("alog", 2 * BH), ("dt", 2 * BH), ("b36", 2 * 36),
                  ("wba", DT * 8), ("w36", DT * 36)]:
    VEC[_name] = _at
    _at += _n
NVEC = _at

TAB = {}
_at = 0
SC_W = T0 + SEQ + P
MLA_W = (META + P) + T0
MOBA_W = P + SEQ
for _name, _n in [("cos_r", T0), ("sin_r", T0), ("decay", RH * SC_W), ("cos_m", T0), ("sin_m", T0), ("mask", MLA_W),
                  ("ident", P), ("ones", P), ("upto", P), ("chunk", P), ("half0", P), ("half1", P),
                  ("level", 6 * P), ("bucket", 512), ("iota", 2 * 8)]:
    TAB[_name] = _at
    _at += _n
NTAB = _at

UNITS = (MODS * D * D + D * (2 * RH * RDK + 2 * RH * RDV) + RH * RDV * D + D * (KVR + P) + D * QR + KVR * MH * 256
         + QR * MH * (NOPE + ROPE) + D * D + 2 * 3 * D * FF
         + D * (3 * 512 + 3 * 512 + 512 + 2 * D) + 2 * 512 * D + D * D + NE * 3 * D * EF) // (P * UNIT)


def constants():
    f = np.float32
    tab = np.zeros((P, NTAB), f)

    def put(name, a, rows=P):
        tab[:rows, TAB[name]:TAB[name] + a.shape[1]] = a

    def rope(dim):
        inv = f(1.0) / (f(10000.0) ** (np.arange(0, dim, 2, dtype=f) / f(dim)))
        ang = (np.arange(T0, dtype=f)[None, :] * inv[:, None].astype(f)).astype(f).astype(np.float64)
        return np.cos(ang).astype(f), np.sin(ang).astype(f)

    c, s = rope(RDK)
    put("cos_r", c)
    put("sin_r", s)
    c, s = rope(ROPE)
    put("cos_m", np.concatenate([c] * 4))
    put("sin_m", np.concatenate([s, -s, s, -s]))
    pos = np.arange(T0) + PAD
    seen = (pos[:, None] // CHUNK) <= (pos[None, :] // CHUNK)
    for h in range(RH):
        log_g = np.log1p(-np.exp2(-5.0 - h))
        m = np.where(seen, np.exp(log_g * np.abs(pos[:, None] - pos[None, :])), 0.0) * RDK ** -0.5
        at = TAB["decay"] + h * SC_W
        for lo, hi in TOK:
            tab[:hi - lo, at:at + T0 - lo] = m[lo:hi, lo:]
            at += T0 - lo
    m = np.where(seen.T, 0.0, NEG)
    put("mask", np.concatenate([m[META:META + P, :META + P], m[META + P:, :]], axis=1))
    i = np.arange(P)
    same = (i[:, None] // CHUNK) == (i[None, :] // CHUNK)
    put("ident", np.eye(P))
    put("ones", np.ones((P, P)))
    put("upto", same & (i[:, None] <= i[None, :]))
    put("chunk", same)
    put("half0", np.broadcast_to(i[:, None] < CHUNK, (P, P)))
    put("half1", np.broadcast_to(i[:, None] >= CHUNK, (P, P)))
    lv = [((i[None, :] >> n) & 1 == 1) & ((i[:, None] >> n) == (i[None, :] >> n) - 1) for n in range(6)]
    put("level", np.concatenate(lv, axis=1))
    d = 255 - np.arange(512)
    n = np.maximum(d, 0)
    large = 16 + (np.log(np.maximum(n, 1).astype(f) / f(16)) / f(np.log(8.0)) * f(16)).astype(np.int32)
    b = np.where(n < 16, n, np.minimum(large, BUCKETS - 1))
    b = np.where(d < 0, BUCKETS, b)
    put("bucket", np.arange(BUCKETS + 1)[:, None] == b[None, :], BUCKETS + 1)
    put("iota", np.broadcast_to(np.tile(np.arange(8), 2), (P, 16)))
    return tab


def narrow_units(w):
    k, f = w.shape
    b = w.reshape(k // P, P, f // P, P).transpose(2, 0, 1, 3).reshape(-1, UB, P, P)
    return b.transpose(0, 2, 1, 3).reshape(-1, P, UNIT)


def wide_units(w):
    k, f = w.shape
    b = w.reshape(k // P, P, f // 512, 512).transpose(2, 0, 1, 3).reshape(-1, UB // 4, P, 512)
    return b.transpose(0, 2, 1, 3).reshape(-1, P, UNIT)


def pair_units(a, b):
    k, f = a.shape
    both = np.stack([a.reshape(k, f // P, P), b.reshape(k, f // P, P)], axis=2)
    return narrow_units(both.reshape(k, 2 * f))


def weight_stream(i):
    r = i["ret_w_in"][0]
    qk = [r[:, base + h * RDK:base + (h + 1) * RDK] for h in range(RH) for base in (0, RH * RDK)]
    kva = i["mla_w_kv_a"]
    kvb = i["mla_w_kv_b"].reshape(KVR, MH, 2, P)
    qb = i["mla_w_q_b"][0].reshape(QR, MH, NOPE + ROPE)
    w = i["w_in_2"][0]
    out = [narrow_units(i["w_mod_2"][0]), narrow_units(np.concatenate(qk, axis=1)), wide_units(r[:, 2048:4096]),
           narrow_units(r[:, 4096:]), narrow_units(i["ret_w_o"][0]),
           pair_units(i["ffn_w1"][0], i["ffn_w3"][0]), narrow_units(i["ffn_w2"][0]),
           narrow_units(np.concatenate([kva, kva[:, KVR:]], axis=1)), narrow_units(i["mla_w_q_a"][0]),
           narrow_units(kvb[:, :, 0].reshape(KVR, D)), wide_units(kvb[:, :, 1].reshape(KVR, D)),
           narrow_units(qb[:, :, :NOPE].reshape(QR, D)), narrow_units(qb[:, :, NOPE:].reshape(QR, MH * ROPE)),
           narrow_units(i["mla_w_o"][0]),
           pair_units(i["ffn_w1"][1], i["ffn_w3"][1]), narrow_units(i["ffn_w2"][1]),
           narrow_units(w[:, 1536:3072]), narrow_units(w[:, :1024]), wide_units(w[:, 1024:1536]),
           narrow_units(w[:, 3072:3584]), narrow_units(w[:, 3592:])]
    out.append(narrow_units(np.concatenate([i["w_up_a_2"][0].reshape(512, DT, P), i["w_up_b_2"][0].reshape(512, DT, P)],
                                           axis=0).reshape(D, D)))
    out.append(narrow_units(i["w_out_2"][0]))
    gate, up = i["w_e_gate_2"][0].reshape(NE, D, EF), i["w_e_up_2"][0].reshape(NE, D, EF)
    down = i["w_e_down_2"][0].reshape(NE, EF, D)
    for e in range(NE):
        out.append(pair_units(gate[e], up[e]))
        if e:
            out.append(narrow_units(down[e - 1]))
    out.append(narrow_units(down[NE - 1]))
    return np.concatenate(out, axis=0)


def vectors(i):
    cols = lambda a: np.asarray(a).reshape(-1, P).T
    rep = lambda a: np.broadcast_to(np.asarray(a).reshape(1, -1), (P, np.asarray(a).size))
    conv = i["conv_w_2"][0].reshape(CONV, 12, P).transpose(2, 1, 0).reshape(P, 12 * CONV)
    rows = lambda w: w.reshape(DT, P, -1).transpose(1, 0, 2).reshape(P, -1)
    w36 = np.concatenate([i["w_rg_2"][0], i["w_re_2"][0]], axis=1)
    b36 = np.concatenate([i["b_rg_2"][0], i["b_re_2"][0]])
    parts = [cols(i["c_2"]), cols(i["b_mod_2"][0]), cols(i["norm_mix_g"][0]), cols(i["norm_ffn_g"][0]),
             cols(i["ret_gn_g"][0]), cols(i["mla_norm_kv_g"]), cols(i["norm_mix_g"][1]), cols(i["mla_kv_a_norm_g"]),
             cols(i["mla_q_a_norm_g"][0]), cols(i["norm_ffn_g"][1]), cols(i["final_g"]), cols(i["norm1_w_2"][0]),
             cols(i["norm2_w_2"][0]), cols(i["final_norm_w_2"]), cols(i["onorm_w_2"][0]), conv,
             rep(np.tile(i["a_log_2"][0], 2)), rep(np.tile(i["dt_bias_2"][0], 2)), rep(np.tile(b36, 2)),
             rows(i["w_in_2"][0][:, 3584:3592]), rows(w36)]
    return np.concatenate(parts, axis=1)


def build(nc, weights, vectors_in, tables_in, tokens_in, rel_bias, skew, out):
    with ExitStack() as ctx:
        def sb(name, *shape):
            return ctx.enter_context(nc.sbuf_tensor(name, list(shape), F32))

        def sem(name):
            return ctx.enter_context(nc.semaphore(name))

        ring = sb("ring", P, SLOTS, UNIT)
        vec = sb("vec", P, NVEC)
        tab = sb("tab", P, NTAB)
        h = sb("h", P, DT, T0)
        hn = sb("hn", P, DT, T0)
        sq = sb("sq", P, DT, T0)
        rms = sb("rms", P, T0)
        rstd = sb("rstd", P, T0)
        mod = sb("mod", P, MODS * DT)
        relb = sb("relb", P, AH)
        small = sb("small", P, 160)
        stats = sb("stats", P, 8 * (MH + AH))
        eps_t = sb("eps_t", P, 4)
        zero_w = sb("zero_w", P, P)
        rt = sb("rt", P, 448)
        arena = sb("arena", P, 23400)

        cursor = [0]

        def carve(*shape, at=None):
            if at is not None:
                cursor[0] = at
            n = int(np.prod(shape))
            a = arena[:, cursor[0]:cursor[0] + n]
            cursor[0] += n
            assert cursor[0] <= 23400, cursor[0]
            if len(shape) == 2:
                a = a.rearrange("p (a b) -> p a b", a=shape[0])
            return a

        qk = carve(4 * RH, T0, at=0)
        gate_r = carve(4 * RH, T0)
        o_r = carve(4 * RH, T0)
        sc_r = carve(2, SC_W)
        rope_t = carve(4, T0)
        v_r_at = cursor[0]
        v_r = carve(3, RH * RDV)
        ff_act = carve(FT, T0, at=v_r_at)
        ff_gate = carve(2, T0)
        ckv = carve(KVT, T0, at=0)
        kvn = carve(DT, T0)
        krope = carve(1, T0)
        k_m = carve(MH, T0)
        v_m = carve(3, MH * P)
        cq = carve(QT, SEQ)
        q_m = carve(MH, SEQ)
        qrope = carve(4, SEQ)
        mrope_t = carve(2, T0)
        p_m = carve(2, MLA_W)
        pt_m = carve(1, 3 * P)
        pt_meta = carve(1, SEQ)
        o_m = carve(MH, SEQ)
        raw_b = carve(12, SEQ + CONV - 1, at=0)
        cb = carve(12, SEQ)
        q_a = carve(8, SEQ)
        v_a = carve(2, 512)
        z_b = carve(BH, SEQ)
        gates = carve(16, SEQ)
        o_b = carve(BH, SEQ)
        delta_at = cursor[0]
        NP = 2 * BH
        LT = carve(NP, P)
        X = carve(NP, P)
        Y = carve(NP, P)
        TM = carve(NP, P)
        PT = carve(NP, P)
        decT = carve(NP, P)
        ML = carve(NP, P)

        def problems(a):
            return a.rearrange("p a (t b) -> p (a t) b", t=2)

        qg = problems(cb[:, 0:BH, :])
        k_tok = problems(cb[:, BH:2 * BH, :])
        kd = problems(cb[:, 2 * BH:3 * BH, :])
        wT = k_tok
        raw_flat = raw_b.rearrange("p a b -> p (a b)")
        v_tok = raw_flat[:, 0:NP * P].rearrange("p (a b) -> p a b", a=NP)
        u_tok = raw_flat[:, NP * P:2 * NP * P].rearrange("p (a b) -> p a b", a=NP)
        st = decT[:, 0:BH, :]
        vn = decT[:, BH:2 * BH, :]
        sq_flat = sq[:, :, :].rearrange("p a b -> p (a b)")
        l2sq = sq_flat[:, 0:8 * SEQ]
        obsq = sq_flat[:, 0:BH * SEQ]
        bias_a = tab[:, 0:AH * MOBA_W].rearrange("p (a b) -> p a b", a=AH)
        bias_w = v_r.rearrange("p a b -> p (a b)")[:, 0:AH * 512].rearrange("p (a b) -> p a b", a=AH)
        o_a = carve(4, SEQ, at=delta_at)
        p_a = carve(2, MOBA_W)
        pt_a = carve(1, 3 * P)
        m_up = carve(DT, SEQ)
        up_t = carve(2, SEQ)
        combB = carve(NE, SEQ, at=0)
        e_gate = carve(2, SEQ)
        e_act = carve(4, SEQ)
        e_tmp = carve(2, SEQ)
        combT_t = carve(1, SEQ)
        combT = combT_t[0:NE, 0, :]
        RT, cur = {}, 0
        for name, k in [("logits", 2 * 36), ("gmax", 2), ("g_diff", 8), ("g_exp", 8), ("g_sum", 2), ("g_top", 2),
                        ("g_hit", 8), ("g_first", 2), ("g_one", 8), ("prod", 64), ("le", 16), ("m1", 2), ("hit1", 16),
                        ("first1", 2), ("one1", 16), ("le2", 16), ("m2", 2), ("hit2", 16), ("first2", 2), ("one2", 16),
                        ("t_diff", 2), ("t_exp", 2), ("t_sum", 2), ("w1", 2), ("w2", 2), ("ce", 16), ("comb", 64)]:
            RT[name] = (cur, k)
            cur += k

        def router(name, groups=None):
            a, k = RT[name]
            v = rt[:, a:a + k]
            return v if groups is None else v.rearrange("p (a b) -> p a b", a=groups)

        comb = router("comb", 2)
        SM = dict(c=0, g=16, beta=24, b=40, a=48, sp=56, ea=64, G=72, R=80, H=88, eG=104, eR=112, eH=120, abs=136, bg=144)
        G_COL = [(p % 2) * BH + p // 2 for p in range(2 * BH)]

        def M(name, k=0, n=1):
            return small[:, SM[name] + k:SM[name] + k + n]

        bank = [ctx.enter_context(nc.psum_tensor(f"bank{n}", [P, 512], F32)) for n in range(8)]

        def V(name, k=0, n=1):
            return vec[:, VEC[name] + k:VEC[name] + k + n]

        def C(name, k=0, n=P, rows=P):
            return tab[0:rows, TAB[name] + k:TAB[name] + k + n]

        ident, ones = C("ident"), C("ones")

        slot_loaded = [sem(f"slot_loaded{s}") for s in range(SLOTS)]
        unit_begun = sem("unit_begun")
        tile_done = sem("tile_done")
        evacuated = [sem(f"evacuated{b}") for b in range(BANKS)]
        vec_loaded, tab_loaded, tok_loaded = sem("vec_loaded"), sem("tab_loaded"), sem("tok_loaded")
        rel_loaded = sem("rel_loaded")
        squared, summed, rooted, normed = sem("squared"), sem("summed"), sem("rooted"), sem("normed")
        dve_step, act_step = sem("dve_step"), sem("act_step")

        made = {}

        def S(name):
            if name not in made:
                made[name] = sem(name)
            return made[name]

        def done(n):
            return n + 1

        def freed(n):
            return n // BANKS + 1

        def wait_stored(eng, n):
            eng.wait_ge(evacuated[n % BANKS], freed(n))

        at = {}
        n = 0
        for name, count in [("mod", 1), ("qk", 4 * RH)]:
            at[name] = n
            n += count
        at["v"] = n
        n += 3 * RH
        for hh in range(RH):
            at["gate", hh] = n
            at["av", hh] = n + 4
            n += 8
        for name, count in [("wo0", DT), ("ffn0", 2 * FT), ("down0", DT), ("kva", KVT + 1), ("qa", QT), ("kn", MH),
                            ("vm", 6), ("qn", MH), ("qr", 4), ("am", MH), ("wo1", DT), ("ffn1", 2 * FT),
                            ("down1", DT), ("qkvb", 12), ("qka", 8), ("va", 2), ("z", BH), ("gates", 16),
                            ("aa", AH), ("up", 2 * DT), ("wout", DT), ("exp", 4 * NE)]:
            at[name] = n
            n += count

        norm_k = [("mix0", DT), ("ffn0", DT), ("mix1", DT), ("ckv", KVT), ("cq", QT), ("ffn1", DT), ("final", DT),
                  ("n1", DT), ("n2", DT), ("final2", DT)]
        norm_no = {name: j for j, (name, _) in enumerate(norm_k)}
        norm_sq, norm_out = {}, {}
        a = b = 0
        for name, k in norm_k:
            norm_sq[name], norm_out[name] = a, b
            a += k
            b += k + (DT if name == "mix1" else 0)
        XC = slice(META, T0)
        ALL = slice(0, T0)

        block = ctx.enter_context(nc.Block())

        @block.sync
        def _(sp):
            def load(slot, unit):
                sp.dma_start(ring[:, slot, :], unit).then_inc(slot_loaded[slot], 16)

            for s in range(SLOTS):
                load(s, weights[s])
            rounds = UNITS // SLOTS
            with sp.Fori(1, rounds) as r:
                for s in range(SLOTS):
                    sp.wait_ge(unit_begun, (r - 1) * SLOTS + s + 2)
                    load(s, weights[bass.ds(r * SLOTS + s, 1)].rearrange("a p n -> (a p) n"))
            for u in range(rounds * SLOTS, UNITS):
                sp.wait_ge(unit_begun, u - SLOTS + 2)
                load(u % SLOTS, weights[u])
            for k in range(DT):
                sp.wait_ge(normed, norm_out["final2"] + k + 1)
                sp.dma_start(out[:, k, :], hn[:, k, 0:SEQ]).then_inc(S("out_stored"), 16)
            sp.wait_ge(S("out_stored"), 16 * DT)

        @block.gpsimd
        def _(pool):
            nc.gpsimd.memset(relb[:, :], NEG).then_inc(S("rel_zeroed"), 1)
            pool.wait_ge(S("rel_zeroed"), 1)
            pool.dma_start(relb[0:BUCKETS, :], rel_bias).then_inc(rel_loaded, 16)
            pool.wait_ge(S("bias_row"), AH)
            pool.dma_start(skew.rearrange("a p x -> p a x"), bias_w).then_inc(S("skew_written"), 16)
            pool.wait_ge(S("skew_written"), 16)
            pool.wait_ge(S("ret_out"), 4 * RH)
            flat = P * 512
            for a in range(AH):
                for off, lo, n in ((255, 0, P), (127, P, SEQ)):
                    pool.dma_start(bias_a[:, a, lo:lo + n],
                                   bass.AP(skew.tensor, a * flat + off, [[511, P], [1, n]])).then_inc(S("bias_loaded"), 16)
            pool.wait_ge(S("bias_loaded"), 16 * 2 * AH)

        @block.tensor
        def _(pe):
            mm = nc.tensor.matmul
            pos = [0, 0]

            def weight(k_offset=0, turn=None, per_turn=0):
                blk = pos[0]
                pos[0] += 1
                unit, place = divmod(blk, UB)
                slot = unit % SLOTS
                if place == 0:
                    want = 16 * (unit // SLOTS + 1)
                    pe.wait_ge(slot_loaded[slot], want if turn is None else turn * (16 * per_turn) + want)
                return ring[:, slot, place * P:(place + 1) * P], place == 0

            def narrow(K, moving, cols, ready=None, turn=None, tiles_per_turn=0, rounds_per_turn=0):
                t = pos[1]
                pos[1] += 1
                dst = bank[t % BANKS]
                if t >= BANKS:
                    want = freed(t - BANKS)
                    pe.wait_ge(evacuated[t % BANKS],
                               want if turn is None else turn * (tiles_per_turn // BANKS) + want)
                for k in range(K):
                    if ready:
                        ready(k)
                    w, first = weight(turn=turn, per_turn=rounds_per_turn)
                    last = mm(dst[:, 0:cols], w, moving(k), start=k == 0, stop=k == K - 1)
                    if first:
                        last.then_inc(unit_begun, 1)
                last.then_inc(tile_done, 1)

            def wide(K, stationary, tiles, ready=None):
                t = pos[1]
                pos[1] += len(tiles)
                for j in range(len(tiles)):
                    if t + j >= BANKS:
                        wait_stored(pe, t + j - BANKS)
                for k in range(K):
                    if ready:
                        ready(k)
                    unit, half = divmod(pos[0] // 4, 2)
                    pos[0] += 4
                    slot = unit % SLOTS
                    if half == 0:
                        pe.wait_ge(slot_loaded[slot], 16 * (unit // SLOTS + 1))
                    for j, (lo, hi) in enumerate(tiles):
                        last = mm(bank[(t + j) % BANKS][0:hi - lo, :], stationary(k)[:, lo:hi],
                                  ring[:, slot, half * 512:(half + 1) * 512], start=k == 0, stop=k == K - 1)
                        if half == 0 and j == 0:
                            last.then_inc(unit_begun, 1)
                        if k == K - 1:
                            last.then_inc(tile_done, 1)

            def norm_sum(name, K, cols):
                for k in range(K):
                    pe.wait_ge(squared, norm_sq[name] + k + 1)
                    last = mm(bank[7][:, 0:cols], ones, sq[:, k, 0:cols], start=k == 0, stop=k == K - 1)
                last.then_inc(summed, 1)

            def normed_ready(name, extra=0):
                return lambda k: pe.wait_ge(normed, norm_out[name] + extra + k + 1)

            pe.wait_ge(S("c_silu"), 1)
            pe.wait_ge(tab_loaded, 16)
            with pe.Fori(0, MODS * DT // SLOTS) as r:
                for s in range(SLOTS):
                    pe.wait_ge(slot_loaded[s], r * 16 + 16)
                    for k in range(DT):
                        last = mm(bank[0][:, bass.ds(r * SLOTS + s, 1)], ring[:, s, k * P:(k + 1) * P],
                                  small[:, k:k + 1], start=k == 0, stop=k == DT - 1, skip_group_check=True)
                        if k == 0:
                            last.then_inc(unit_begun, 1)
            pos[0] += MODS * DT * UB
            pos[1] += 1
            mm(bank[0][:, 64:65], ones, small[:, 0:1], start=True, stop=True,
               skip_group_check=True).then_inc(tile_done, 1)

            pe.wait_ge(rel_loaded, 16)
            for a in range(AH):
                if a >= 2:
                    pe.wait_ge(S("bias_row"), a - 1)
                mm(bank[4 + a % 2][:, :], relb[0:BUCKETS + 1, a:a + 1].to_broadcast([BUCKETS + 1, P]),
                   C("bucket", 0, 512, BUCKETS + 1), start=True, stop=True).then_inc(S("bias_sum"), 1)

            norm_sum("mix0", DT, T0)
            ready = normed_ready("mix0")
            for t in range(4 * RH):
                narrow(DT, lambda k: hn[:, k, :], T0, ready if t == 0 else None)
            for g in range(RH):
                wide(DT, lambda k: hn[:, k, :], TOK)

            def ret_mean(hh):
                for d in range(4):
                    wait_stored(pe, at["av", hh] + d)
                    last = mm(bank[6][:, 0:T0], ones, o_r[:, 4 * hh + d, :], start=d == 0, stop=d == 3)
                last.then_inc(S("gn_mean"), 1)

            def ret_var(hh):
                pe.wait_ge(S("gn_squared"), hh + 1)
                for d in range(4):
                    last = mm(bank[7][:, 0:T0], ones, sq[:, d, :], start=d == 0, stop=d == 3)
                last.then_inc(S("gn_var"), 1)

            for hh in range(RH):
                pe.wait_ge(S("roped"), 2 * hh + 2)
                if hh:
                    pe.wait_ge(S("decayed"), hh)
                for half in range(2):
                    mm(bank[4][0:META, 0:T0], qk[:, 4 * hh + 2 + half, 0:META], qk[:, 4 * hh + half, :],
                       start=half == 0, stop=half == 1)
                for j, (lo, hi) in enumerate(TOK[1:]):
                    for half in range(2):
                        last = mm(bank[5][:, j * SEQ:j * SEQ + T0 - lo], qk[:, 4 * hh + 2 + half, lo:hi],
                                  qk[:, 4 * hh + half, lo:T0], start=half == 0, stop=half == 1)
                last.then_inc(S("ret_scored"), 1)
                if hh:
                    ret_mean(hh - 1)
                for t in range(4):
                    if hh and t == 2:
                        ret_var(hh - 1)
                    narrow(DT, lambda k: hn[:, k, :], T0)
                pe.wait_ge(S("decayed"), hh + 1)
                if hh == 0:
                    wait_stored(pe, at["v"] + 3 * RH - 1)
                for d in range(4):
                    t = pos[1]
                    pos[1] += 1
                    wait_stored(pe, t - BANKS)
                    dst, col, c0 = bank[t % BANKS], hh * RDV + d * P, 0
                    for j, (lo, hi) in enumerate(TOK):
                        last = mm(dst[:, lo:T0], v_r[0:hi - lo, j, col:col + P], sc_r[0:hi - lo, hh % 2, c0:c0 + T0 - lo],
                                  start=j == 0, stop=j == 2, skip_group_check=True)
                        c0 += T0 - lo
                    last.then_inc(tile_done, 1)
            ret_mean(RH - 1)
            ret_var(RH - 1)
            for t in range(DT):
                narrow(4 * RH, lambda k: o_r[:, k, :], T0,
                       (lambda k: pe.wait_ge(S("ret_out"), k + 1)) if t == 0 else None)

            def feed_forward(layer, src, cols):
                name = f"ffn{layer}"
                norm_sum(name, DT, cols)
                ready = normed_ready(name)
                for k in range(DT):
                    ready(k)
                turns = 2 * FT // SLOTS
                start = list(pos)
                with pe.Fori(0, turns) as r:
                    for t in range(SLOTS):
                        narrow(DT, lambda k: src(hn, k), cols, turn=r, tiles_per_turn=SLOTS, rounds_per_turn=1)
                pos[0] = start[0] + turns * SLOTS * UB
                pos[1] = start[1] + turns * SLOTS
                for t in range(turns * SLOTS, 2 * FT):
                    narrow(DT, lambda k: src(hn, k), cols)
                for t in range(DT):
                    narrow(FT, lambda k: ff_act[:, k, 0:cols], cols,
                           (lambda k: wait_stored(pe, at[name] + 2 * k + 1)) if t == 0 else None)

            feed_forward(0, lambda a, k: a[:, k, :], T0)

            norm_sum("mix1", DT, T0)
            for t in range(KVT + 1):
                narrow(DT, lambda k: kvn[:, k, :], T0, normed_ready("mix1") if t == 0 else None)
            for t in range(QT):
                narrow(DT, lambda k: hn[:, k, XC], SEQ, normed_ready("mix1", DT) if t == 0 else None)
            norm_sum("ckv", KVT, T0)
            norm_sum("cq", QT, SEQ)
            for t in range(MH):
                narrow(KVT, lambda k: ckv[:, k, :], T0, normed_ready("ckv") if t == 0 else None)
            for g in range(2):
                wide(KVT, lambda k: ckv[:, k, :], TOK)
            for t in range(MH + 4):
                narrow(QT, lambda k: cq[:, k, :], SEQ, normed_ready("cq") if t == 0 else None)

            def attention(tag, heads, score, put):
                for i in range(heads + 1):
                    if i < heads:
                        score(i, bank[4 + i % 2]).then_inc(S(tag + "_scored"), 1)
                    if i >= 1:
                        j = i - 1
                        pe.wait_ge(S(tag + "_p"), i)
                        if j:
                            pe.wait_ge(S(tag + "_pt"), j)
                        put(j)

            def mla_score(i, dst):
                if i == 0:
                    pe.wait_ge(S("q_roped"), 5)
                    wait_stored(pe, at["qn"] + MH - 1)
                if i >= 2:
                    pe.wait_ge(S("mla_p"), i - 1)
                r = 64 * (i % 2)
                for lo, hi, q0 in [(0, META + P, 0), (META + P, MLA_W, P)]:
                    w = hi - lo
                    mm(dst[:, lo:hi], q_m[:, i, q0:q0 + P], k_m[:, i, 0:w], start=True, stop=False)
                    last = mm(dst[:, lo:hi], qrope[r:r + ROPE, i // 2, q0:q0 + P], krope[r:r + ROPE, 0, 0:w],
                              start=False, stop=True)
                return last

            def values(tag, j, pv, v_cols, meta, rows):
                key0 = META if meta else 0
                second = key0 + P
                nc.tensor.transpose(bank[6][:, 0:P], pv[:, key0:key0 + P], ident)
                nc.tensor.transpose(bank[6][:, P:2 * P], pv[:, second + key0:second + key0 + P], ident)
                last = nc.tensor.transpose(bank[6][:, 2 * P:3 * P], pv[:, second + key0 + P:second + key0 + 2 * P], ident)
                last.then_inc(S(tag + "_turned"), 1)
                if meta:
                    if j:
                        pe.wait_ge(S(tag + "_ptm"), j)
                    nc.tensor.transpose(bank[7][0:META, 0:P], pv[:, 0:META], ident)
                    nc.tensor.transpose(bank[7][0:META, P:2 * P], pv[:, second:second + META],
                                        ident).then_inc(S(tag + "_turnedm"), 1)
                t = pos[1]
                pos[1] += 1
                wait_stored(pe, t - BANKS)
                dst = bank[t % BANKS]
                pe.wait_ge(S(tag + "_pt"), j + 1)
                pt = pt_m if meta else pt_a
                v = v_m if meta else v_a
                o = 1 if meta else 0
                mm(dst[rows, 0:SEQ], v[:, o, v_cols], pt[:, 0, 0:SEQ], start=True, stop=False, skip_group_check=True)
                last = mm(dst[rows, P:SEQ], v[:, o + 1, v_cols], pt[:, 0, SEQ:3 * P], start=False, stop=not meta,
                          skip_group_check=True)
                if meta:
                    pe.wait_ge(S(tag + "_ptm"), j + 1)
                    last = mm(dst[rows, 0:SEQ], v[0:META, 0, v_cols], pt_meta[0:META, 0, :], start=False, stop=True,
                              skip_group_check=True)
                last.then_inc(tile_done, 1)

            def mla_values(j):
                if j == 0:
                    wait_stored(pe, at["vm"] + 5)
                values("mla", j, p_m[:, j % 2, :], slice(j * P, (j + 1) * P), True, slice(0, P))

            attention("mla", MH, mla_score, mla_values)
            for t in range(DT):
                narrow(MH, lambda k: o_m[:, k, :], SEQ,
                       (lambda k: wait_stored(pe, at["am"] + k)) if t == 0 else None)
            feed_forward(1, lambda a, k: a[:, k, XC], SEQ)
            norm_sum("final", DT, SEQ)

            norm_sum("n1", DT, SEQ)
            hb = lambda k: hn[:, k, 0:SEQ]
            for k in range(DT):
                pe.wait_ge(S("hb_ready"), k + 1)
            for tt in range(2):
                for k in range(DT):
                    last = mm(bank[4][:, 8 * tt:8 * tt + 8], hn[:, k, tt * P:(tt + 1) * P], V("wba", 8 * k, 8),
                              start=k == 0, stop=k == DT - 1)
            last.then_inc(S("ba_done"), 1)
            for t in range(12):
                narrow(DT, hb, SEQ)
            pe.wait_ge(S("g_ready"), 1)
            g = M("g", 0, 8)
            for j, name in enumerate(("upto", "chunk", "half0", "half1")):
                last = mm(bank[5][:, 8 * j:8 * j + 8], C(name), g, start=True, stop=True)
            last.then_inc(S("g_summed"), 1)
            pe.wait_ge(S("g_stored"), 1)
            for p in range(NP):
                last = mm(bank[6 + p // 4][:, (p % 4) * P:(p % 4 + 1) * P],
                          M("g", G_COL[p]).to_broadcast([P, P]), C("upto"), start=True, stop=True)
            last.then_inc(S("row_g"), 1)
            for p in range(NP):
                last = mm(bank[4 + p // 4][:, (p % 4) * P:(p % 4 + 1) * P],
                          M("beta", G_COL[p]).to_broadcast([P, P]), ident, start=True, stop=True)
            last.then_inc(S("row_beta"), 1)
            for t in range(8):
                narrow(DT, hb, SEQ)
            wide(DT, hb, [(0, P), (P, SEQ)])
            pe.wait_ge(S("l2_squared"), 8)
            pe.wait_ge(S("beta_rows"), 1)
            pe.wait_ge(S("exp_rows"), 1)
            for j in range(4):
                last = mm(bank[4 + j][:, :], ones, l2sq[:, j * 512:(j + 1) * 512], start=True, stop=True)
            last.then_inc(S("l2_summed"), 1)
            for t in range(BH):
                narrow(DT, hb, SEQ)
            pe.wait_ge(S("l2_done"), 1)
            for p in range(NP):
                kp = cb[:, BH + p // 2, (p % 2) * P:(p % 2 + 1) * P]
                last = mm(bank[4 + p // 4][:, (p % 4) * P:(p % 4 + 1) * P], kp, kp, start=True, stop=True)
            last.then_inc(S("gram_done"), 1)
            for p in range(NP):
                kp = cb[:, BH + p // 2, (p % 2) * P:(p % 2 + 1) * P]
                last = mm(bank[6 + p // 4][:, (p % 4) * P:(p % 4 + 1) * P], kp,
                          cb[:, p // 2, (p % 2) * P:(p % 2 + 1) * P], start=True, stop=True)
            last.then_inc(S("qk_done"), 1)
            narrow(DT, hb, SEQ)
            narrow(DT, hb, SEQ)
            pe.wait_ge(S("lt_ready"), 1)
            for p in range(NP):
                last = nc.tensor.transpose(bank[4 + p // 4][:, (p % 4) * P:(p % 4 + 1) * P],
                                           cb[:, BH + p // 2, (p % 2) * P:(p % 2 + 1) * P], ident)
            last.then_inc(S("k_turned"), 1)
            pe.wait_ge(S("pt_ready"), 1)
            for p in range(NP):
                last = nc.tensor.transpose(bank[6 + p // 4][:, (p % 4) * P:(p % 4 + 1) * P],
                                           cb[:, 2 * BH + p // 2, (p % 2) * P:(p % 2 + 1) * P], ident)
            last.then_inc(S("v_turned"), 1)
            narrow(DT, hb, SEQ)
            narrow(DT, hb, SEQ)
            pe.wait_ge(S("tok_ready"), 1)
            for lv in range(6):
                pe.wait_ge(S("ml_ready"), lv + 1)
                for half in range(2):
                    if lv and half == 0:
                        pe.wait_ge(S("inv_ready"), lv)
                    for p in range(4 * half, 4 * half + 4):
                        last = mm(bank[4 + half][:, (p % 4) * P:(p % 4 + 1) * P], ML[:, p, :],
                                  X[:, p, :] if lv else ident, start=True, stop=True)
                last.then_inc(S("mx_done"), 1)
                narrow(DT, hb, SEQ)
                if lv == 0:
                    continue
                pe.wait_ge(S("t_stored"), lv)
                for half in range(2):
                    for p in range(4 * half, 4 * half + 4):
                        last = mm(bank[6 + half][:, (p % 4) * P:(p % 4 + 1) * P], TM[:, p, :], Y[:, p, :],
                                  start=True, stop=True)
                last.then_inc(S("dy_done"), 1)
                if lv < 5:
                    for half in range(2):
                        for p in range(4 * half, 4 * half + 4):
                            last = mm(bank[4 + half][:, (p % 4) * P:(p % 4 + 1) * P], Y[:, p, :], TM[:, p, :],
                                      start=True, stop=True)
                    last.then_inc(S("dx_done"), 1)
                narrow(DT, hb, SEQ)
            pe.wait_ge(S("inv_ready"), 6)
            for p in range(NP):
                last = mm(bank[4 + p // 4][:, (p % 4) * P:(p % 4 + 1) * P], Y[:, p, :], v_tok[:, p, :],
                          start=True, stop=True)
            last.then_inc(S("u_done"), 1)
            for p in range(NP):
                last = mm(bank[6 + p // 4][:, (p % 4) * P:(p % 4 + 1) * P], k_tok[:, p, :], Y[:, p, :],
                          start=True, stop=True)
            last.then_inc(S("w_done"), 1)
            narrow(DT, hb, SEQ)
            for c in range(4):
                R, tt = CHUNK * (c % 2), c // 2
                rows = slice(R, R + CHUNK)
                if c == 0:
                    pe.wait_ge(S("u_stored"), 1)
                    pe.wait_ge(S("w_stored"), 1)
                if c:
                    pe.wait_ge(S("state_ready"), c)
                    for a in range(BH):
                        last = mm(bank[4][rows, a * P:(a + 1) * P], wT[:, 2 * a + tt, rows], st[:, a, :],
                                  start=True, stop=True)
                    last.then_inc(S("ws_done"), 1)
                pe.wait_ge(S("vn_ready"), c + 1)
                if c:
                    pe.wait_ge(S("ob_stored"), c)
                for a in range(BH):
                    dst = bank[5][:, a * CHUNK:(a + 1) * CHUNK]
                    if c:
                        mm(dst, st[:, a, :], qg[:, 2 * a + tt, rows], start=True, stop=False)
                    last = mm(dst, vn[rows, a, :], PT[rows, 2 * a + tt, rows], start=c == 0, stop=True)
                last.then_inc(S("ob_done"), 1)
                if c < 3:
                    for a in range(BH):
                        last = mm(bank[6][:, a * P:(a + 1) * P], kd[rows, 2 * a + tt, :], vn[rows, a, :],
                                  start=True, stop=True)
                    last.then_inc(S("ds_done"), 1)
            assert pos[1] == at["aa"]
            pe.wait_ge(S("ob_squared"), 1)
            for j in range(2):
                last = mm(bank[4 + j][:, :], ones, obsq[:, j * 512:(j + 1) * 512], start=True, stop=True)
            last.then_inc(S("ob_summed"), 1)

            def moba_score(i, dst):
                if i == 0:
                    wait_stored(pe, at["qka"] + 7)
                    pe.wait_ge(S("ob_rooted"), 1)
                if i >= 2:
                    pe.wait_ge(S("moba_p"), i - 1)
                r = slice(AHD * (i % 2), AHD * (i % 2) + AHD)
                mm(dst[:, 0:P], q_a[r, i // 2, 0:P], q_a[r, 4 + i // 2, 0:P], start=True, stop=True)
                return mm(dst[:, P:MOBA_W], q_a[r, i // 2, P:SEQ], q_a[r, 4 + i // 2, :], start=True, stop=True)

            def moba_values(j):
                if j == 0:
                    wait_stored(pe, at["va"] + 1)
                values("moba", j, p_a[:, j % 2, :], slice(j // 2 * P, (j // 2 + 1) * P), False, slice(0, P))

            attention("moba", AH, moba_score, moba_values)
            for k in range(4):
                wait_stored(pe, at["aa"] + 2 * k + 1)
            for t in range(DT):
                narrow(4, lambda k: o_a[:, k, :], SEQ)
                narrow(4, lambda k: o_b[:, k, :], SEQ,
                       (lambda k: pe.wait_ge(S("ob_ready"), 1)) if t == 0 else None)
            for t in range(DT):
                narrow(DT, lambda k: m_up[:, k, :], SEQ,
                       (lambda k: pe.wait_ge(S("m_ready"), k + 1)) if t == 0 else None)

            norm_sum("n2", DT, SEQ)
            for k in range(DT):
                pe.wait_ge(S("hb_ready"), DT + k + 1)
            for tt in range(2):
                for k in range(DT):
                    last = mm(bank[4][:, 36 * tt:36 * tt + 36], hn[:, k, tt * P:(tt + 1) * P], V("w36", 36 * k, 36),
                              start=k == 0, stop=k == DT - 1)
            last.then_inc(S("logits_done"), 1)

            def expert_in(turn=None):
                for t in range(4):
                    narrow(DT, hb, SEQ, turn=turn, tiles_per_turn=8, rounds_per_turn=1)

            def expert_out(parity, want, turn=None, final=False):
                pe.wait_ge(S("e_act"), want if turn is None else turn * 4 + want)
                for t in range(DT):
                    for k in range(2):
                        w, first = weight(turn=turn, per_turn=1)
                        last = mm(bank[4 + t // 2][:, (t % 2) * SEQ:(t % 2 + 1) * SEQ], w, e_act[:, 2 * parity + k, :],
                                  start=False, stop=final and t % 2 == 1 and k == 1, skip_group_check=True)
                        if first:
                            last.then_inc(unit_begun, 1)
                return last

            expert_in()
            pe.wait_ge(S("comb_ready"), 1)
            for tt in range(2):
                last = nc.tensor.transpose(bank[4][0:NE, tt * P:(tt + 1) * P], comb[:, tt, :], ident)
            last.then_inc(S("comb_turned"), 1)
            pe.wait_ge(S("combT_stored"), 1)
            for e in range(0, NE, 2):
                b = 4 + (e // 2) % 4
                if e >= 8:
                    pe.wait_ge(S("comb_row"), e // 2 - 3)
                for j in range(2):
                    last = mm(bank[b][:, j * SEQ:(j + 1) * SEQ], tab[0:NE, TAB["ident"] + e + j:TAB["ident"] + e + j + 1]
                              .to_broadcast([NE, P]), combT, start=True, stop=True)
                last.then_inc(S("comb_sum"), 1)
            pe.wait_ge(S("comb_row"), NE // 2)
            for b in range(4, 8):
                mm(bank[b][:, :], zero_w[:, :], C("bucket", 0, 512), start=True, stop=False, skip_group_check=True)
            turns = NE // 2 - 1
            start = list(pos)
            with pe.Fori(0, turns) as r:
                for j in range(2):
                    expert_in(turn=r)
                    expert_out(j, 2 * (j + 1), turn=r)
            pos[0] = start[0] + turns * SLOTS * UB
            pos[1] = start[1] + turns * 8
            expert_in()
            expert_out(0, 2 * (NE - 1))
            expert_out(1, 2 * NE, final=True).then_inc(S("moe_done"), 1)
            pe.wait_ge(S("moe_added"), DT)
            norm_sum("final2", DT, SEQ)

        @block.scalar
        def _(act):
            fn = nc.scalar.activation
            act.dma_start(vec[:, :], vectors_in).then_inc(vec_loaded, 16)
            act.dma_start(h[:, :, :], tokens_in).then_inc(tok_loaded, 16)
            act.dma_start(tab[:, :], tables_in).then_inc(tab_loaded, 16)
            tile = [0]

            def take():
                t = tile[0]
                tile[0] += 1
                act.wait_ge(tile_done, done(t))
                return bank[t % BANKS], evacuated[t % BANKS]

            def norm(name, src, K, cols, width, ready, eps=RMS_EPS):
                for k in range(K):
                    ready(k)
                    fn(sq[:, k, 0:cols], src(k), ACT.Square).then_inc(squared, 1)
                act.wait_ge(summed, norm_no[name] + 1)
                if norm_no[name]:
                    act.wait_ge(normed, norm_out[norm_k[norm_no[name] - 1][0]] + 1)
                fn(rms[:, 0:cols], bank[7][:, 0:cols], ACT.Sqrt, bias=eps_col(eps), scale=1.0 / width).then_inc(rooted, 1)

            def eps_col(eps):
                return eps_t[:, 0:1] if eps == RMS_EPS else eps_t[:, 1:2]

            act.wait_ge(vec_loaded, 16)
            fn(small[:, 0:DT], V("c", 0, DT), ACT.Silu).then_inc(S("c_silu"), 1)
            act.wait_ge(tok_loaded, 16)
            act.wait_ge(S("eps_set"), 1)
            norm("mix0", lambda k: h[:, k, :], DT, T0, D, lambda k: None)
            tile[0] = at["v"]
            act.wait_ge(S("skew_written"), 16)
            for g in range(RH):
                for j, (lo, hi) in enumerate(TOK):
                    src, free = take()
                    fn(v_r[0:hi - lo, j, g * RDV:(g + 1) * RDV], src[0:hi - lo, :], ACT.Copy).then_inc(free, 1)

            def gn_root(hh):
                act.wait_ge(S("gn_var"), hh + 1)
                fn(rms[:, :], bank[7][:, 0:T0], ACT.Sqrt, bias=eps_col(GN_EPS), scale=1.0 / RDV).then_inc(S("gn_root"), 1)

            def gn_square(hh):
                act.wait_ge(S("gn_centred"), hh + 1)
                fn(sq[:, 0:4, :], o_r[:, 4 * hh:4 * hh + 4, :], ACT.Square).then_inc(S("gn_squared"), 1)

            for hh in range(RH):
                if hh:
                    gn_square(hh - 1)
                for t in range(4):
                    if hh and t == 2:
                        gn_root(hh - 1)
                    src, free = take()
                    fn(gate_r[:, 4 * hh + t, :], src[:, 0:T0], ACT.Silu).then_inc(free, 1)
                for d in range(4):
                    src, free = take()
                    fn(o_r[:, 4 * hh + d, :], src[:, 0:T0], ACT.Copy).then_inc(free, 1)
            gn_square(RH - 1)
            gn_root(RH - 1)

            def feed_forward(layer, first_tile, cols, src):
                name = f"ffn{layer}"
                res = at["wo0"] if layer == 0 else at["wo1"]
                norm(name, src, DT, cols, D, lambda k: wait_stored(act, res + k))
                assert at[name] == first_tile
                turns = 2 * FT // SLOTS

                def gate(pair, turn=None):
                    t = first_tile + 2 * pair
                    more = lambda n, per: n if turn is None else turn * per + n
                    act.wait_ge(tile_done, more(done(t), SLOTS))
                    act.wait_ge(evacuated[(t + 1) % BANKS], more(freed(t + 1) - 1, SLOTS // BANKS))
                    fn(ff_gate[:, pair % 2, 0:cols], bank[t % BANKS][:, 0:cols], ACT.Silu).then_inc(evacuated[t % BANKS], 1)

                with act.Fori(0, turns) as r:
                    for j in range(SLOTS // 2):
                        gate(j, r)
                for pair in range(turns * SLOTS // 2, FT):
                    gate(pair)

            feed_forward(0, at["ffn0"], T0, lambda k: h[:, k, :])

            norm("mix1", lambda k: h[:, k, :], DT, T0, D, lambda k: wait_stored(act, at["down0"] + k))
            tile[0] = at["kva"]
            for t in range(KVT):
                src, free = take()
                fn(ckv[:, t, :], src[:, 0:T0], ACT.Copy).then_inc(free, 1)
            tile[0] = at["qa"]
            for t in range(QT):
                src, free = take()
                fn(cq[:, t, :], src[:, 0:SEQ], ACT.Copy).then_inc(free, 1)
            norm("ckv", lambda k: ckv[:, k, :], KVT, T0, KVR, lambda k: wait_stored(act, at["kva"] + k))
            norm("cq", lambda k: cq[:, k, :], QT, SEQ, QR, lambda k: wait_stored(act, at["qa"] + k))
            for t in range(MH):
                src, free = take()
                fn(k_m[:, t, :], src[:, 0:T0], ACT.Copy).then_inc(free, 1)
            for g in range(2):
                for j, (lo, hi) in enumerate(TOK):
                    src, free = take()
                    fn(v_m[0:hi - lo, j, g * 512:(g + 1) * 512], src[0:hi - lo, :], ACT.Copy).then_inc(free, 1)
            for t in range(MH):
                src, free = take()
                fn(q_m[:, t, :], src[:, 0:SEQ], ACT.Copy).then_inc(free, 1)

            def attention(tag, heads, probs, parts, stat, pt, store):
                for i in range(heads + 1):
                    if i < heads:
                        act.wait_ge(S(tag + "_max"), i + 1)
                        s = stat(i)
                        for j, (lo, hi) in enumerate(parts):
                            a = probs[:, i % 2, lo:hi]
                            last = fn(a, a, ACT.Exp, bias=s[:, 2 + j:3 + j], accum_out=s[:, 4 + j:5 + j])
                        last.then_inc(S(tag + "_exp"), 1)
                    if i >= 1:
                        j = i - 1
                        act.wait_ge(S(tag + "_turned"), j + 1)
                        fn(pt[:, 0, :], bank[6][:, 0:3 * P], ACT.Copy).then_inc(S(tag + "_pt"), 1)
                        store(j)

            tile[0] = at["am"]

            def mla_store(j):
                src, free = take()
                fn(o_m[:, j, :], src[:, 0:SEQ], ACT.Copy).then_inc(free, 1)

            attention("mla", MH, p_m, [(0, META + P), (META + P, MLA_W)], lambda i: stats[:, 8 * i:8 * i + 8],
                      pt_m, mla_store)
            feed_forward(1, at["ffn1"], SEQ, lambda k: h[:, k, XC])
            norm("final", lambda k: h[:, k, XC], DT, SEQ, D, lambda k: wait_stored(act, at["down1"] + k))

            def shifted(name, shift, ready):
                norm(name, lambda k: h[:, k, XC], DT, SEQ, D, ready)
                for k in range(DT):
                    act.wait_ge(normed, norm_out[name] + k + 1)
                    fn(hn[:, k, 0:SEQ], hn[:, k, 0:SEQ], ACT.Identity,
                       bias=mod[:, shift * DT + k:shift * DT + k + 1]).then_inc(S("hb_ready"), 1)

            wait_stored(act, at["mod"])
            shifted("n1", 0, lambda k: act.wait_ge(normed, norm_out["final"] + k + 1))
            act.wait_ge(S("ba_split"), 1)
            fn(M("beta", 0, 8), M("b", 0, 8), ACT.Sigmoid).then_inc(S("beta_ready"), 1)
            fn(M("sp", 0, 8), M("abs", 0, 8), ACT.Exp, scale=-1.0)
            fn(M("ea", 0, 8), V("alog", 0, 8), ACT.Exp).then_inc(act_step, 1)
            act.wait_ge(act_step, 1)
            fn(M("sp", 0, 8), M("sp", 0, 8), ACT.Ln, bias=eps_t[:, 2:3]).then_inc(S("softplus_ln"), 1)
            tile[0] = at["qkvb"]
            for t in range(12):
                src, free = take()
                fn(raw_b[:, t, CONV - 1:], src[:, 0:SEQ], ACT.Copy).then_inc(free, 1)
            act.wait_ge(S("g_stored"), 1)
            fn(M("eG", 0, 32), M("G", 0, 32), ACT.Exp).then_inc(S("g_exp"), 1)
            act.wait_ge(S("row_g"), 1)
            for j in range(2):
                last = fn(TM[:, 4 * j:4 * j + 4, :], bank[6 + j][:, :].rearrange("p (a b) -> p a b", a=4), ACT.Exp)
            last.then_inc(S("exp_rows"), 1)
            act.wait_ge(S("dec_diff"), 1)
            fn(decT[:, :, :], decT[:, :, :], ACT.Exp).then_inc(S("dec_exp"), 1)
            tile[0] = at["qka"]
            for t in range(8):
                src, free = take()
                fn(q_a[:, t, :], src[:, 0:SEQ], ACT.Copy).then_inc(free, 1)
            for t in range(2):
                src, free = take()
                fn(v_a[:, t, :], src[:, :], ACT.Copy).then_inc(free, 1)
            for t in range(12):
                act.wait_ge(S("conv_done"), t + 1)
                fn(cb[:, t, :], cb[:, t, :], ACT.Silu).then_inc(S("conv_silu"), 1)
            for t in range(8):
                act.wait_ge(S("conv_silu"), t + 1)
                fn(l2sq[:, t * SEQ:(t + 1) * SEQ], cb[:, t, :], ACT.Square).then_inc(S("l2_squared"), 1)
            act.wait_ge(S("l2_summed"), 1)
            for j in range(4):
                last = fn(l2sq[:, j * 512:(j + 1) * 512], bank[4 + j][:, :], ACT.Sqrt, bias=eps_t[:, 0:1])
            last.then_inc(S("l2_root"), 1)
            for t in range(BH):
                src, free = take()
                fn(z_b[:, t, :], src[:, 0:SEQ], ACT.Silu).then_inc(free, 1)

            def gate():
                t = tile[0] - at["gates"]
                src, free = take()
                fn(gates[:, t, :], src[:, 0:SEQ], ACT.Sigmoid).then_inc(free, 1)

            gate()
            gate()
            gate()
            gate()
            for lv in range(6):
                if lv:
                    act.wait_ge(S("mx_done"), lv + 1)
                    for j in range(2):
                        last = fn(TM[:, 4 * j:4 * j + 4, :], bank[4 + j][:, :].rearrange("p (a b) -> p a b", a=4),
                                  ACT.Copy)
                    last.then_inc(S("t_stored"), 1)
                gate()
                if lv:
                    gate()
            act.wait_ge(S("u_done"), 1)
            for j in range(2):
                last = fn(u_tok[:, 4 * j:4 * j + 4, :], bank[4 + j][:, :].rearrange("p (a b) -> p a b", a=4), ACT.Copy)
            last.then_inc(S("u_stored"), 1)
            act.wait_ge(S("w_done"), 1)
            for j in range(2):
                last = fn(wT[:, 4 * j:4 * j + 4, :], bank[6 + j][:, :].rearrange("p (a b) -> p a b", a=4), ACT.Copy)
            last.then_inc(S("w_stored"), 1)
            gate()
            assert tile[0] == at["aa"]
            for c in range(4):
                act.wait_ge(S("ob_done"), c + 1)
                fn(o_b[:, :, c * CHUNK:(c + 1) * CHUNK], bank[5][:, 0:BH * CHUNK].rearrange("p (a b) -> p a b", a=BH),
                   ACT.Copy).then_inc(S("ob_stored"), 1)
            act.wait_ge(S("ob_stored"), 4)
            fn(obsq, o_b.rearrange("p a b -> p (a b)"), ACT.Square).then_inc(S("ob_squared"), 1)
            act.wait_ge(S("ob_summed"), 1)
            for j in range(2):
                last = fn(obsq[:, j * 512:(j + 1) * 512], bank[4 + j][:, :], ACT.Sqrt, bias=eps_t[:, 0:1], scale=1.0 / BHD)
            last.then_inc(S("ob_rooted"), 1)
            tile[0] = at["aa"]

            def moba_store(j):
                src, free = take()
                r = slice(AHD * (j % 2), AHD * (j % 2) + AHD)
                fn(o_a[r, j // 2, :], src[r, 0:SEQ], ACT.Copy).then_inc(free, 1)

            attention("moba", AH, p_a, [(0, P), (P, MOBA_W)], lambda i: stats[:, 64 + 8 * i:72 + 8 * i], pt_a, moba_store)

            shifted("n2", 3, lambda k: wait_stored(act, at["wout"] + k))

            def gates_of(first, turn=None):
                for f in range(2):
                    t = first + 2 * f
                    act.wait_ge(tile_done, done(t) if turn is None else turn * 8 + done(t))
                    before = freed(t + 1) - 1
                    act.wait_ge(evacuated[(t + 1) % BANKS], before if turn is None else turn * 2 + before)
                    fn(e_gate[:, f, :], bank[t % BANKS][:, 0:SEQ], ACT.Silu).then_inc(evacuated[t % BANKS], 1)

            act.wait_ge(S("group_diff"), 1)
            fn(router("g_exp"), router("g_diff"), ACT.Exp).then_inc(S("group_exp"), 1)
            act.wait_ge(S("top_diff"), 1)
            fn(router("t_exp"), router("t_diff"), ACT.Exp).then_inc(S("top_exp"), 1)
            act.wait_ge(S("comb_turned"), 1)
            fn(combT, bank[4][0:NE, 0:SEQ], ACT.Copy).then_inc(S("combT_stored"), 1)
            for e in range(0, NE, 2):
                act.wait_ge(S("comb_sum"), e // 2 + 1)
                fn(combB[:, e:e + 2, :], bank[4 + (e // 2) % 4][:, :].rearrange("p (a b) -> p a b", a=2),
                   ACT.Copy).then_inc(S("comb_row"), 1)
            gates_of(at["exp"])
            with act.Fori(0, NE // 2 - 1) as r:
                for j in range(2):
                    gates_of(at["exp"] + 4 * (j + 1), r)
            gates_of(at["exp"] + 4 * (NE - 1))
            norm("final2", lambda k: h[:, k, XC], DT, SEQ, D, lambda k: act.wait_ge(S("moe_added"), k + 1))

        @block.vector
        def _(dve):
            tt_, ts_, stt = nc.vector.tensor_tensor, nc.vector.tensor_scalar, nc.vector.scalar_tensor_tensor
            steps = [0]

            def link(ins):
                steps[0] += 1
                ins.then_inc(dve_step, 1)
                dve.wait_ge(dve_step, steps[0])

            def take(t):
                dve.wait_ge(tile_done, done(t))
                return bank[t % BANKS], evacuated[t % BANKS]

            def spread(a, n):
                return a.unsqueeze(1).to_broadcast([a.shape[0], n, a.shape[1]])

            def norm_scale(name, cols):
                dve.wait_ge(rooted, norm_no[name] + 1)
                if norm_no[name]:
                    dve.wait_ge(normed, norm_out[name])
                link(nc.vector.reciprocal(rstd[:, 0:cols], rms[:, 0:cols]))

            def norm_apply(src, dst, gain, K, cols):
                for k in range(K):
                    stt(dst(k), src(k), gain(k), cols, ALU.mult, ALU.mult).then_inc(normed, 1)

            nc.vector.memset(eps_t[:, 0:1], RMS_EPS)
            nc.vector.memset(eps_t[:, 2:3], 1.0)
            nc.vector.memset(zero_w[:, :], 0.0)
            nc.vector.memset(eps_t[:, 1:2], GN_EPS).then_inc(S("eps_set"), 1)
            dve.wait_ge(tab_loaded, 16)
            dve.wait_ge(vec_loaded, 16)
            src, free = take(at["mod"])
            link(tt_(mod[:, :], src[:, 0:MODS * DT], V("b_mod", 0, MODS * DT), ALU.add))
            for part, gain in ((1, "n1"), (4, "n2")):
                a = mod[:, part * DT:(part + 1) * DT]
                last = stt(a, a, 1.0, V(gain, 0, DT), ALU.add, ALU.mult)
            last.then_inc(free, 1)
            for a in range(AH):
                dve.wait_ge(S("bias_sum"), a + 1)
                nc.vector.tensor_copy(bias_w[:, a, :], bank[4 + a % 2][:, :]).then_inc(S("bias_row"), 1)
            norm_scale("mix0", T0)
            norm_apply(lambda k: h[:, k, :], lambda k: hn[:, k, :], lambda k: V("mix0", k), DT, rstd[:, :])
            for pair in range(2 * RH):
                t = at["qk"] + 2 * pair
                a, free = take(t)
                if pair:
                    dve.wait_ge(S("roped"), pair)
                tt_(rope_t[:, 0, :], a[:, 0:T0], C("cos_r", 0, T0), ALU.mult)
                tt_(rope_t[:, 1, :], a[:, 0:T0], C("sin_r", 0, T0), ALU.mult).then_inc(free, 1)
                a, free = take(t + 1)
                tt_(rope_t[:, 2, :], a[:, 0:T0], C("sin_r", 0, T0), ALU.mult)
                tt_(rope_t[:, 3, :], a[:, 0:T0], C("cos_r", 0, T0), ALU.mult).then_inc(free, 1)
                wait_stored(dve, t + 1)
                tt_(qk[:, 2 * pair, :], rope_t[:, 0, :], rope_t[:, 2, :], ALU.subtract)
                tt_(qk[:, 2 * pair + 1, :], rope_t[:, 1, :], rope_t[:, 3, :], ALU.add).then_inc(S("roped"), 1)

            def gn_centre(hh):
                dve.wait_ge(S("gn_mean"), hh + 1)
                a = o_r[:, 4 * hh:4 * hh + 4, :]
                stt(a, spread(bank[6][:, 0:T0], 4), -1.0 / RDV, a, ALU.mult, ALU.add).then_inc(S("gn_centred"), 1)

            def gn_apply(hh):
                dve.wait_ge(S("gn_root"), hh + 1)
                link(nc.vector.reciprocal(rstd[:, :], rms[:, :]))
                a = o_r[:, 4 * hh:4 * hh + 4, :]
                dve.wait_ge(S("gn_squared"), hh + 1)
                link(tt_(a, a, spread(rstd[:, :], 4), ALU.mult))
                for d in range(4):
                    t = 4 * hh + d
                    wait_stored(dve, at["gate", hh] + d)
                    stt(o_r[:, t, :], o_r[:, t, :], V("gn", t), gate_r[:, t, :], ALU.mult,
                        ALU.mult).then_inc(S("ret_out"), 1)

            for hh in range(RH):
                dve.wait_ge(S("ret_scored"), hh + 1)
                if hh >= 2:
                    dve.wait_ge(tile_done, done(at["av", hh - 2] + 3))
                col = TAB["decay"] + hh * SC_W
                tt_(sc_r[0:META, hh % 2, 0:T0], bank[4][0:META, 0:T0], tab[0:META, col:col + T0], ALU.mult)
                tt_(sc_r[:, hh % 2, T0:], bank[5][:, 0:SEQ + P], tab[:, col + T0:col + SC_W],
                    ALU.mult).then_inc(S("decayed"), 1)
                if hh:
                    gn_centre(hh - 1)
                    gn_apply(hh - 1)
            gn_centre(RH - 1)
            gn_apply(RH - 1)

            def add_tiles(first, cols, dst):
                for k in range(DT):
                    src, free = take(first + k)
                    tt_(dst(k), dst(k), src[:, 0:cols], ALU.add).then_inc(free, 1)

            add_tiles(at["wo0"], T0, lambda k: h[:, k, :])

            def feed_forward(layer, cols, src, dst):
                name = f"ffn{layer}"
                norm_scale(name, cols)
                norm_apply(src, dst, lambda k: V(name, k), DT, rstd[:, 0:cols])
                first = at[name]
                turns = 2 * FT // SLOTS

                def product(pair, turn=None):
                    t = first + 2 * pair + 1
                    more = lambda n, per: n if turn is None else turn * per + n
                    dve.wait_ge(tile_done, more(done(t), SLOTS))
                    dve.wait_ge(evacuated[(t - 1) % BANKS], more(freed(t - 1), SLOTS // BANKS))
                    dst = ff_act[:, pair, 0:cols] if turn is None else \
                        ff_act[:, bass.ds(turn * (SLOTS // 2) + pair, 1), 0:cols].rearrange("p a b -> p (a b)")
                    tt_(dst, ff_gate[:, pair % 2, 0:cols], bank[t % BANKS][:, 0:cols],
                        ALU.mult).then_inc(evacuated[t % BANKS], 1)

                with dve.Fori(0, turns) as r:
                    for j in range(SLOTS // 2):
                        product(j, r)
                for pair in range(turns * SLOTS // 2, FT):
                    product(pair)

            feed_forward(0, T0, lambda k: h[:, k, :], lambda k: hn[:, k, :])
            add_tiles(at["down0"], T0, lambda k: h[:, k, :])

            norm_scale("mix1", T0)
            norm_apply(lambda k: h[:, k, :], lambda k: kvn[:, k, :], lambda k: V("kv", k), DT, rstd[:, :])
            norm_apply(lambda k: h[:, k, :], lambda k: hn[:, k, :], lambda k: V("mix1", k), DT, rstd[:, :])

            def rotate(src, free, dst, c0, cols):
                c, s = C("cos_m", c0, cols), C("sin_m", c0, cols)
                tt_(mrope_t[:, 0, 0:cols], src[:, 0:cols], c, ALU.mult)
                for q in range(4):
                    of, to = slice(32 * q, 32 * q + 32), slice(32 * (q ^ 1), 32 * (q ^ 1) + 32)
                    last = tt_(mrope_t[to, 1, 0:cols], src[of, 0:cols], s[of], ALU.mult)
                last.then_inc(free[0], 1)
                dve.wait_ge(*free)
                tt_(dst, mrope_t[:, 0, 0:cols], mrope_t[:, 1, 0:cols], ALU.add).then_inc(S("q_roped"), 1)
                rotated[0] += 1
                dve.wait_ge(S("q_roped"), rotated[0])

            rotated = [0]

            def rotate_tile(t, dst, c0, cols):
                src, sem_free = take(t)
                rotate(src, (sem_free, freed(t)), dst, c0, cols)

            rotate_tile(at["kva"] + KVT, krope[:, 0, :], 0, T0)
            norm_scale("ckv", T0)
            norm_apply(lambda k: ckv[:, k, :], lambda k: ckv[:, k, :], lambda k: V("kva", k), KVT, rstd[:, :])
            norm_scale("cq", SEQ)
            norm_apply(lambda k: cq[:, k, :], lambda k: cq[:, k, :], lambda k: V("qa", k), QT, rstd[:, 0:SEQ])
            for t in range(4):
                rotate_tile(at["qr"] + t, qrope[:, t, :], META, SEQ)

            def attention(tag, heads, front, probs, parts, stat, turned=None):
                for i in range(heads + 1):
                    if i < heads:
                        dve.wait_ge(S(tag + "_scored"), i + 1)
                        if i >= 2:
                            dve.wait_ge(S(tag + "_turned"), i - 1)
                        link(front(i, bank[4 + i % 2], probs[:, i % 2, :]))
                        s = stat(i)
                        for j, (lo, hi) in enumerate(parts):
                            last = nc.vector.tensor_reduce(s[:, j:j + 1], probs[:, i % 2, lo:hi], AX, ALU.max)
                        link(last)
                        ts_(s[:, 2:4], s[:, 0:2], -1.0, None, ALU.mult).then_inc(S(tag + "_max"), 1)
                    if i >= 1:
                        j = i - 1
                        dve.wait_ge(S(tag + "_exp"), i)
                        s = stat(j)
                        link(nc.vector.reciprocal(s[:, 6:8], s[:, 4:6]))
                        for n, (lo, hi) in enumerate(parts):
                            a = probs[:, j % 2, lo:hi]
                            last = ts_(a, a, s[:, 6 + n:7 + n], None, ALU.mult)
                        last.then_inc(S(tag + "_p"), 1)
                        if turned:
                            turned(j)

            scale = (NOPE + ROPE) ** -0.5

            def mla_front(i, src, dst):
                return stt(dst, src[:, 0:MLA_W], scale, C("mask", 0, MLA_W), ALU.mult, ALU.add)

            def mla_turned(j):
                dve.wait_ge(S("mla_turnedm"), j + 1)
                if j:
                    dve.wait_ge(tile_done, done(at["am"] + j - 1))
                nc.vector.tensor_copy(pt_meta[0:META, 0, :], bank[7][0:META, 0:SEQ]).then_inc(S("mla_ptm"), 1)

            attention("mla", MH, mla_front, p_m, [(0, META + P), (META + P, MLA_W)],
                      lambda i: stats[:, 8 * i:8 * i + 8], mla_turned)
            add_tiles(at["wo1"], SEQ, lambda k: h[:, k, XC])
            feed_forward(1, SEQ, lambda k: h[:, k, XC], lambda k: hn[:, k, XC])
            add_tiles(at["down1"], SEQ, lambda k: h[:, k, XC])
            norm_scale("final", SEQ)
            norm_apply(lambda k: h[:, k, XC], lambda k: h[:, k, XC], lambda k: V("final", k), DT, rstd[:, 0:SEQ])

            norm_scale("n1", SEQ)
            norm_apply(lambda k: h[:, k, XC], lambda k: hn[:, k, 0:SEQ],
                       lambda k: mod[:, DT + k:DT + k + 1], DT, rstd[:, 0:SEQ])
            nc.vector.memset(raw_b[:, :, 0:CONV - 1], 0.0)
            dve.wait_ge(S("ba_done"), 1)
            ba = bank[4][:, 0:16].rearrange("p (t c) -> p t c", t=2)
            two = lambda a: a.rearrange("p (t c) -> p t c", t=2)
            nc.vector.tensor_copy(two(M("b", 0, 8)), ba[:, :, 0:BH])
            link(tt_(two(M("a", 0, 8)), ba[:, :, BH:2 * BH], two(V("dt", 0, 8)), ALU.add))
            stt(M("abs", 0, 8), M("a", 0, 8), -1.0, M("a", 0, 8), ALU.mult, ALU.max).then_inc(S("ba_split"), 1)
            dve.wait_ge(S("beta_ready"), 1)
            dve.wait_ge(S("softplus_ln"), 1)
            link(stt(M("sp", 0, 8), M("a", 0, 8), 0.0, M("sp", 0, 8), ALU.max, ALU.add))
            stt(M("g", 0, 8), M("sp", 0, 8), -1.0, M("ea", 0, 8), ALU.mult, ALU.mult).then_inc(S("g_ready"), 1)
            dve.wait_ge(S("g_summed"), 1)
            link(nc.vector.tensor_copy(M("G", 0, 8), bank[5][:, 0:8]))
            tt_(M("R", 0, 8), bank[5][:, 8:16], M("G", 0, 8), ALU.subtract)
            nc.vector.tensor_copy(M("H", 0, 16), bank[5][:, 16:32]).then_inc(S("g_stored"), 1)
            dve.wait_ge(S("g_exp"), 1)
            link(tt_(M("bg", 0, 8), M("beta", 0, 8), M("eG", 0, 8), ALU.mult))
            dve.wait_ge(S("exp_rows"), 1)
            for p in range(NP):
                last = ts_(decT[:, p, :], bank[6 + p // 4][:, (p % 4) * P:(p % 4 + 1) * P], M("G", G_COL[p]), 0.0,
                           ALU.subtract, ALU.min)
            last.then_inc(S("dec_diff"), 1)
            dve.wait_ge(S("dec_exp"), 1)
            link(tt_(decT[:, :, :], decT[:, :, :], spread(C("upto"), NP), ALU.mult))
            dve.wait_ge(S("row_beta"), 1)

            def half(a, j):
                return a[:, 4 * j:4 * j + 4, :]

            def psum(b):
                return bank[b][:, :].rearrange("p (a b) -> p a b", a=4)

            for j in range(2):
                last = tt_(half(LT, j), half(decT, j), psum(4 + j), ALU.mult)
            last.then_inc(S("beta_rows"), 1)
            for t0 in range(0, 12, 4):
                for j in range(CONV):
                    for t in range(t0, t0 + 4):
                        if j == 0:
                            wait_stored(dve, at["qkvb"] + t)
                        x, w = raw_b[:, t, j:j + SEQ], V("conv", t * CONV + j)
                        if j == 0:
                            last = ts_(cb[:, t, :], x, w, None, ALU.mult)
                        else:
                            last = stt(cb[:, t, :], x, w, cb[:, t, :], ALU.mult, ALU.add)
                            if j == CONV - 1:
                                last.then_inc(S("conv_done"), 1)
                    if j < CONV - 1:
                        link(last)
            dve.wait_ge(S("l2_root"), 1)
            link(nc.vector.reciprocal(l2sq, l2sq))
            flat = cb.rearrange("p a b -> p (a b)")
            stt(flat[:, 0:BH * SEQ], flat[:, 0:BH * SEQ], BHD ** -0.5, l2sq[:, 0:BH * SEQ], ALU.mult, ALU.mult)
            tt_(flat[:, BH * SEQ:2 * BH * SEQ], flat[:, BH * SEQ:2 * BH * SEQ], l2sq[:, BH * SEQ:], ALU.mult)\
                .then_inc(S("l2_done"), 1)
            dve.wait_ge(S("gram_done"), 1)
            for j in range(2):
                last = tt_(half(LT, j), half(LT, j), psum(4 + j), ALU.mult)
            last.then_inc(S("lt_ready"), 1)
            dve.wait_ge(S("qk_done"), 1)
            for j in range(2):
                last = tt_(half(PT, j), half(decT, j), psum(6 + j), ALU.mult)
            last.then_inc(S("pt_ready"), 1)
            tt_(qg, qg, TM[:, :, :], ALU.mult)
            dve.wait_ge(S("k_turned"), 1)
            dve.wait_ge(S("v_turned"), 1)
            dve.wait_ge(S("conv_silu"), 12)
            for dst, first, name in ((k_tok, 4, "bg"), (kd, 4, "eR"), (v_tok, 6, "beta")):
                per = M(name, 0, 8).rearrange("p (t a) -> p a t", t=2)
                for j in range(2):
                    last = tt_(half(dst, j).rearrange("p (a t) b -> p a t b", t=2),
                               psum(first + j).rearrange("p (a t) b -> p a t b", t=2),
                               per[:, 2 * j:2 * j + 2, :].unsqueeze(3).to_broadcast([P, 2, 2, P]), ALU.mult)
            last.then_inc(S("tok_ready"), 1)

            def level(lv):
                tt_(ML[:, :, :], LT[:, :, :], spread(C("level", lv * P), NP), ALU.mult).then_inc(S("ml_ready"), 1)

            dve.wait_ge(S("lt_ready"), 1)
            level(0)
            for lv in range(6):
                dve.wait_ge(S("mx_done"), lv + 1)
                if lv == 0:
                    dve.wait_ge(S("ml_ready"), 1)
                    tt_(Y[:, :, :], spread(ident, NP), ML[:, :, :], ALU.subtract)
                    for j in range(2):
                        last = tt_(half(X, j), spread(ident, 4), psum(4 + j), ALU.subtract)
                    last.then_inc(S("inv_ready"), 1)
                    dve.wait_ge(S("inv_ready"), 1)
                    level(1)
                    continue
                if lv < 5:
                    level(lv + 1)
                dve.wait_ge(S("dy_done"), lv)
                if lv < 5:
                    dve.wait_ge(S("dx_done"), lv)
                for j in range(2):
                    last = tt_(half(Y, j), half(Y, j), psum(6 + j), ALU.subtract)
                if lv < 5:
                    for j in range(2):
                        last = tt_(half(X, j), half(X, j), psum(4 + j), ALU.subtract)
                last.then_inc(S("inv_ready"), 1)
            dve.wait_ge(S("u_stored"), 1)
            for c in range(4):
                R, tt = CHUNK * (c % 2), c // 2
                rows = slice(R, R + CHUNK)
                u = u_tok.rearrange("p (a t) b -> p a t b", t=2)[rows, :, tt, :]
                if c == 0:
                    nc.vector.tensor_copy(vn[rows], u).then_inc(S("vn_ready"), 1)
                else:
                    dve.wait_ge(S("ws_done"), c)
                    tt_(vn[rows], u, psum(4)[rows], ALU.subtract).then_inc(S("vn_ready"), 1)
                if c == 3:
                    break
                dve.wait_ge(S("ds_done"), c + 1)
                if c == 0:
                    nc.vector.tensor_copy(st, psum(6)).then_inc(S("state_ready"), 1)
                    continue
                for a in range(BH):
                    last = stt(st[:, a, :], st[:, a, :], M("eH", 8 * (c % 2) + tt * BH + a), psum(6)[:, a, :],
                               ALU.mult, ALU.add)
                last.then_inc(S("state_ready"), 1)
            dve.wait_ge(S("ob_rooted"), 1)
            ob = o_b.rearrange("p a b -> p (a b)")
            link(nc.vector.reciprocal(obsq, obsq))
            link(tt_(ob, ob, obsq, ALU.mult))
            wait_stored(dve, at["z"] + BH - 1)
            stt(ob, z_b.rearrange("p a b -> p (a b)"), V("onorm"), ob, ALU.mult, ALU.mult).then_inc(S("ob_ready"), 1)

            dve.wait_ge(S("bias_loaded"), 16 * 2 * AH)

            def moba_front(i, src, dst):
                return stt(dst, src[:, 0:MOBA_W], AHD ** -0.5, bias_a[:, i, :], ALU.mult, ALU.add)

            attention("moba", AH, moba_front, p_a, [(0, P), (P, MOBA_W)], lambda i: stats[:, 64 + 8 * i:72 + 8 * i])
            for k in range(DT):
                t = at["up"] + 2 * k
                src, free = take(t)
                if k == 0:
                    wait_stored(dve, at["gates"] + 15)
                else:
                    dve.wait_ge(S("m_ready"), k)
                tt_(up_t[:, 0, :], gates[:, k, :], src[:, 0:SEQ], ALU.mult).then_inc(free, 1)
                src, free = take(t + 1)
                tt_(up_t[:, 1, :], gates[:, DT + k, :], src[:, 0:SEQ], ALU.mult).then_inc(free, 1)
                wait_stored(dve, t + 1)
                tt_(m_up[:, k, :], up_t[:, 0, :], up_t[:, 1, :], ALU.add).then_inc(S("m_ready"), 1)
            for k in range(DT):
                src, free = take(at["wout"] + k)
                stt(h[:, k, XC], src[:, 0:SEQ], mod[:, 2 * DT + k:2 * DT + k + 1], h[:, k, XC],
                    ALU.mult, ALU.add).then_inc(free, 1)
            norm_scale("n2", SEQ)
            norm_apply(lambda k: h[:, k, XC], lambda k: hn[:, k, 0:SEQ],
                       lambda k: mod[:, 4 * DT + k:4 * DT + k + 1], DT, rstd[:, 0:SEQ])

            dve.wait_ge(S("logits_done"), 1)
            red = nc.vector.tensor_reduce

            def per_token(a, n):
                return a.unsqueeze(2).to_broadcast([P, 2, n])

            def first_of_max(values, n, top, hit, first, one, shape):
                link(red(router(top), values, AX, ALU.max))
                link(tt_(shape(hit), values, per_token(router(top), n), ALU.is_equal))
                iota = C("iota", 0, 16).rearrange("p (a b) -> p a b", a=2)[:, :, 0:n]
                link(stt(shape(hit), shape(hit), -64.0, iota, ALU.mult, ALU.add))
                link(red(router(first), shape(hit), AX, ALU.min))
                link(tt_(shape(one), shape(hit), per_token(router(first), n), ALU.is_equal))

            lg = router("logits", 2)
            link(tt_(lg, bank[4][:, 0:72].rearrange("p (a b) -> p a b", a=2),
                     V("b36", 0, 72).rearrange("p (a b) -> p a b", a=2), ALU.add))
            first_of_max(lg[:, :, 0:NG], NG, "gmax", "g_hit", "g_first", "g_one", lambda a: router(a, 2))
            tt_(router("g_diff", 2), lg[:, :, 0:NG], per_token(router("gmax"), NG), ALU.subtract)\
                .then_inc(S("group_diff"), 1)
            for tt in range(2):
                prod = router("prod")[:, tt * 32:tt * 32 + 32].rearrange("p (g e) -> p g e", g=NG)
                last = tt_(prod, lg[:, tt, NG:].rearrange("p (g e) -> p g e", g=NG),
                           router("g_one", 2)[:, tt, :].unsqueeze(2).to_broadcast([P, NG, EPG]), ALU.mult)
            link(last)
            for tt in range(2):
                prod = router("prod")[:, tt * 32:tt * 32 + 32].rearrange("p (g e) -> p e g", g=NG)
                last = red(router("le", 2)[:, tt, :], prod, AX, ALU.add)
            link(last)
            first_of_max(router("le", 2), EPG, "m1", "hit1", "first1", "one1", lambda a: router(a, 2))
            link(stt(router("le2"), router("one1"), NEG, router("le"), ALU.mult, ALU.add))
            first_of_max(router("le2", 2), EPG, "m2", "hit2", "first2", "one2", lambda a: router(a, 2))
            tt_(router("t_diff"), router("m2"), router("m1"), ALU.subtract).then_inc(S("top_diff"), 1)
            dve.wait_ge(S("group_exp"), 1)
            link(red(router("g_sum"), router("g_exp", 2), AX, ALU.add))
            nc.vector.reciprocal(router("g_top"), router("g_sum"))
            dve.wait_ge(S("top_exp"), 1)
            link(ts_(router("t_sum"), router("t_exp"), 1.0, None, ALU.add))
            link(nc.vector.reciprocal(router("t_sum"), router("t_sum")))
            link(tt_(router("w1"), router("t_sum"), router("g_top"), ALU.mult))
            link(tt_(router("w2"), router("w1"), router("t_exp"), ALU.mult))
            tt_(router("hit1", 2), router("one1", 2), per_token(router("w1"), EPG), ALU.mult)
            link(tt_(router("hit2", 2), router("one2", 2), per_token(router("w2"), EPG), ALU.mult))
            link(tt_(router("ce"), router("hit1"), router("hit2"), ALU.add))
            for tt in range(2):
                last = tt_(comb[:, tt, :].rearrange("p (g e) -> p g e", g=NG),
                           router("ce", 2)[:, tt, :].unsqueeze(1).to_broadcast([P, NG, EPG]),
                           router("g_one", 2)[:, tt, :].unsqueeze(2).to_broadcast([P, NG, EPG]), ALU.mult)
            last.then_inc(S("comb_ready"), 1)
            dve.wait_ge(S("comb_row"), NE // 2)

            def expert(first, parity, e=None, turn=None):
                for f in range(2):
                    t = first + 2 * f + 1
                    more = lambda n, per: n if turn is None else turn * per + n
                    dve.wait_ge(tile_done, more(done(t), 8))
                    dve.wait_ge(evacuated[(t - 1) % BANKS], more(freed(t - 1), 2))
                    if e:
                        dve.wait_ge(S("e_act"), more(2 * e, 4))
                    tt_(e_tmp[:, f, :], e_gate[:, f, :], bank[t % BANKS][:, 0:SEQ], ALU.mult)\
                        .then_inc(evacuated[t % BANKS], 1)
                for f in range(2):
                    t = first + 2 * f + 1
                    dve.wait_ge(evacuated[t % BANKS], more(freed(t), 2))
                    share = combB[:, e, :] if turn is None else \
                        combB[:, bass.ds(turn * 2 + e, 1), :].rearrange("p a b -> p (a b)")
                    tt_(e_act[:, 2 * parity + f, :], e_tmp[:, f, :], share, ALU.mult).then_inc(S("e_act"), 1)

            expert(at["exp"], 0, e=0)
            with dve.Fori(0, NE // 2 - 1) as r:
                for j in range(2):
                    expert(at["exp"] + 4 * (j + 1), (j + 1) % 2, e=j + 1, turn=r)
            expert(at["exp"] + 4 * (NE - 1), 1, e=NE - 1)
            dve.wait_ge(S("moe_done"), 1)
            for k in range(DT):
                stt(h[:, k, XC], bank[4 + k // 2][:, (k % 2) * SEQ:(k % 2 + 1) * SEQ],
                    mod[:, 5 * DT + k:5 * DT + k + 1], h[:, k, XC], ALU.mult, ALU.add).then_inc(S("moe_added"), 1)
            norm_scale("final2", SEQ)
            norm_apply(lambda k: h[:, k, XC], lambda k: hn[:, k, 0:SEQ], lambda k: V("final2", k), DT, rstd[:, 0:SEQ])


def kernel(**inputs):
    import concourse.bacc as bacc
    from concourse.bass_utils import run_bass_kernel_spmd

    i = {name: np.asarray(a) for name, a in inputs.items()}
    tokens = np.concatenate([i["meta"], i["x"][0]], axis=0)
    arrays = {
        "weights": weight_stream(i),
        "vectors": np.ascontiguousarray(vectors(i)),
        "tables": constants(),
        "tokens": np.ascontiguousarray(tokens.T.reshape(DT, P, T0).transpose(1, 0, 2)),
        "rel_bias": np.ascontiguousarray(i["rel_bias_2"]),
    }
    nc = bacc.Bacc("TRN2", target_bir_lowering=False, num_devices=1)
    args = [nc.dram_tensor(name, a.shape, F32, kind="ExternalInput").ap() for name, a in arrays.items()]
    skew = nc.dram_tensor("skew", (AH, P, 512), F32, kind="Internal").ap()
    out = nc.dram_tensor("out", (P, DT, SEQ), F32, kind="ExternalOutput").ap()
    build(nc, *args, skew, out)
    r = run_bass_kernel_spmd(nc, [arrays], core_ids=[0])
    got = np.asarray(r.results[0]["out"])
    return np.ascontiguousarray(got.transpose(2, 1, 0).reshape(1, SEQ, D))
```

```python
from contextlib import ExitStack

import numpy as np

import concourse.bass as bass
from concourse import mybir

F32 = mybir.dt.float32
ALU = mybir.AluOpType
ACT = mybir.ActivationFunctionType
AX = mybir.AxisListType.X

P = 128
D = 1024
DT = D // P
META, SEQ = 16, 256
T0 = META + SEQ
TOK = [(0, META), (META, META + P), (META + P, T0)]
PAD = P - META
CHUNK = 64
RMS_EPS, GN_EPS = 1e-6, 1e-5
NEG = -1e30

RH, RDK, RDV = 4, 256, 512
MH, NOPE, ROPE = 8, 128, 64
QR, KVR = 768, 512
QT, KVT = QR // P, KVR // P
FF = 2816
FT = FF // P
AH, AHD = 8, 64
BH, BHD = 4, 128
CONV = 4
NG, EPG, EF = 4, 8, 256
NE = NG * EPG
BUCKETS = 32
CAP = 64
PAIRS = NE // 2
FAR = 1000.0
MODS = 6

UB = 8
UNIT = UB * P
SLOTS = 12
BANKS = 4

VEC = {}
_at = 0
for _name, _n in [("c", DT), ("b_mod", MODS * DT), ("mix0", DT), ("ffn0", DT), ("gn", 16), ("kv", DT), ("mix1", DT),
                  ("kva", KVT), ("qa", QT), ("ffn1", DT), ("final", DT), ("n1", DT), ("n2", DT), ("final2", DT),
                  ("onorm", 1), ("conv", 12 * CONV), ("alog", 2 * BH), ("dt", 2 * BH), ("b36", 2 * 36),
                  ("wba", DT * 8), ("w36", DT * 36)]:
    VEC[_name] = _at
    _at += _n
NVEC = _at

TAB = {}
_at = 0
SC_W = T0 + SEQ + P
MLA_W = (META + P) + T0
MOBA_W = P + SEQ
for _name, _n in [("cos_r", T0), ("sin_r", T0), ("decay", RH * SC_W), ("cos_m", T0), ("sin_m", T0), ("mask", MLA_W),
                  ("ident", P), ("ones", P), ("upto", P), ("chunk", P), ("half0", P), ("half1", P),
                  ("level", 6 * P), ("bucket", 512), ("iota", 2 * 8), ("before", P), ("slot", CAP)]:
    TAB[_name] = _at
    _at += _n
NTAB = _at

UNITS = (MODS * D * D + D * (2 * RH * RDK + 2 * RH * RDV) + RH * RDV * D + D * (KVR + P) + D * QR + KVR * MH * 256
         + QR * MH * (NOPE + ROPE) + D * D + 2 * 3 * D * FF
         + D * (3 * 512 + 3 * 512 + 512 + 2 * D) + 2 * 512 * D + D * D + NE * 3 * D * EF) // (P * UNIT)


def constants():
    f = np.float32
    tab = np.zeros((P, NTAB), f)

    def put(name, a, rows=P):
        tab[:rows, TAB[name]:TAB[name] + a.shape[1]] = a

    def rope(dim):
        inv = f(1.0) / (f(10000.0) ** (np.arange(0, dim, 2, dtype=f) / f(dim)))
        ang = (np.arange(T0, dtype=f)[None, :] * inv[:, None].astype(f)).astype(f).astype(np.float64)
        return np.cos(ang).astype(f), np.sin(ang).astype(f)

    c, s = rope(RDK)
    put("cos_r", c)
    put("sin_r", s)
    c, s = rope(ROPE)
    put("cos_m", np.concatenate([c] * 4))
    put("sin_m", np.concatenate([s, -s, s, -s]))
    pos = np.arange(T0) + PAD
    seen = (pos[:, None] // CHUNK) <= (pos[None, :] // CHUNK)
    for h in range(RH):
        log_g = np.log1p(-np.exp2(-5.0 - h))
        m = np.where(seen, np.exp(log_g * np.abs(pos[:, None] - pos[None, :])), 0.0) * RDK ** -0.5
        at = TAB["decay"] + h * SC_W
        for lo, hi in TOK:
            tab[:hi - lo, at:at + T0 - lo] = m[lo:hi, lo:]
            at += T0 - lo
    m = np.where(seen.T, 0.0, NEG)
    put("mask", np.concatenate([m[META:META + P, :META + P], m[META + P:, :]], axis=1))
    i = np.arange(P)
    same = (i[:, None] // CHUNK) == (i[None, :] // CHUNK)
    put("ident", np.eye(P))
    put("ones", np.ones((P, P)))
    put("upto", same & (i[:, None] <= i[None, :]))
    put("chunk", same)
    put("half0", np.broadcast_to(i[:, None] < CHUNK, (P, P)))
    put("half1", np.broadcast_to(i[:, None] >= CHUNK, (P, P)))
    lv = [((i[None, :] >> n) & 1 == 1) & ((i[:, None] >> n) == (i[None, :] >> n) - 1) for n in range(6)]
    put("level", np.concatenate(lv, axis=1))
    d = 255 - np.arange(512)
    n = np.maximum(d, 0)
    large = 16 + (np.log(np.maximum(n, 1).astype(f) / f(16)) / f(np.log(8.0)) * f(16)).astype(np.int32)
    b = np.where(n < 16, n, np.minimum(large, BUCKETS - 1))
    b = np.where(d < 0, BUCKETS, b)
    put("bucket", np.arange(BUCKETS + 1)[:, None] == b[None, :], BUCKETS + 1)
    put("iota", np.broadcast_to(np.tile(np.arange(8), 2), (P, 16)))
    put("before", i[:, None] < i[None, :])
    put("slot", np.broadcast_to(np.arange(CAP), (P, CAP)))
    return tab


def narrow_units(w):
    k, f = w.shape
    b = w.reshape(k // P, P, f // P, P).transpose(2, 0, 1, 3).reshape(-1, UB, P, P)
    return b.transpose(0, 2, 1, 3).reshape(-1, P, UNIT)


def wide_units(w):
    k, f = w.shape
    b = w.reshape(k // P, P, f // 512, 512).transpose(2, 0, 1, 3).reshape(-1, UB // 4, P, 512)
    return b.transpose(0, 2, 1, 3).reshape(-1, P, UNIT)


def pair_units(a, b):
    k, f = a.shape
    both = np.stack([a.reshape(k, f // P, P), b.reshape(k, f // P, P)], axis=2)
    return narrow_units(both.reshape(k, 2 * f))


def weight_stream(i):
    r = i["ret_w_in"][0]
    qk = [r[:, base + h * RDK:base + (h + 1) * RDK] for h in range(RH) for base in (0, RH * RDK)]
    kva = i["mla_w_kv_a"]
    kvb = i["mla_w_kv_b"].reshape(KVR, MH, 2, P)
    qb = i["mla_w_q_b"][0].reshape(QR, MH, NOPE + ROPE)
    w = i["w_in_2"][0]
    out = [narrow_units(i["w_mod_2"][0]), narrow_units(np.concatenate(qk, axis=1)), wide_units(r[:, 2048:4096]),
           narrow_units(r[:, 4096:]), narrow_units(i["ret_w_o"][0]),
           pair_units(i["ffn_w1"][0], i["ffn_w3"][0]), narrow_units(i["ffn_w2"][0]),
           narrow_units(np.concatenate([kva, kva[:, KVR:]], axis=1)), narrow_units(i["mla_w_q_a"][0]),
           narrow_units(kvb[:, :, 0].reshape(KVR, D)), wide_units(kvb[:, :, 1].reshape(KVR, D)),
           narrow_units(qb[:, :, :NOPE].reshape(QR, D)), narrow_units(qb[:, :, NOPE:].reshape(QR, MH * ROPE)),
           narrow_units(i["mla_w_o"][0]),
           pair_units(i["ffn_w1"][1], i["ffn_w3"][1]), narrow_units(i["ffn_w2"][1]),
           narrow_units(w[:, 1536:3072]), narrow_units(w[:, :1024]), wide_units(w[:, 1024:1536]),
           narrow_units(w[:, 3072:3584]), narrow_units(w[:, 3592:])]
    out.append(narrow_units(np.concatenate([i["w_up_a_2"][0].reshape(512, DT, P), i["w_up_b_2"][0].reshape(512, DT, P)],
                                           axis=0).reshape(D, D)))
    out.append(narrow_units(i["w_out_2"][0]))
    gate, up = i["w_e_gate_2"][0].reshape(NE, D, EF), i["w_e_up_2"][0].reshape(NE, D, EF)
    down = i["w_e_down_2"][0].reshape(NE, EF, D)
    for e in range(0, NE, 2):
        out += [pair_units(gate[e], up[e]), pair_units(gate[e + 1], up[e + 1])]
        both = down[e:e + 2].reshape(2, EF // P, P, DT, P).transpose(3, 0, 1, 2, 4).reshape(-1, UB, P, P)
        out.append(both.transpose(0, 2, 1, 3).reshape(-1, P, UNIT))
    return np.concatenate(out, axis=0)


def vectors(i):
    cols = lambda a: np.asarray(a).reshape(-1, P).T
    rep = lambda a: np.broadcast_to(np.asarray(a).reshape(1, -1), (P, np.asarray(a).size))
    conv = i["conv_w_2"][0].reshape(CONV, 12, P).transpose(2, 1, 0).reshape(P, 12 * CONV)
    rows = lambda w: w.reshape(DT, P, -1).transpose(1, 0, 2).reshape(P, -1)
    w36 = np.concatenate([i["w_rg_2"][0], i["w_re_2"][0]], axis=1)
    b36 = np.concatenate([i["b_rg_2"][0], i["b_re_2"][0]])
    parts = [cols(i["c_2"]), cols(i["b_mod_2"][0]), cols(i["norm_mix_g"][0]), cols(i["norm_ffn_g"][0]),
             cols(i["ret_gn_g"][0]), cols(i["mla_norm_kv_g"]), cols(i["norm_mix_g"][1]), cols(i["mla_kv_a_norm_g"]),
             cols(i["mla_q_a_norm_g"][0]), cols(i["norm_ffn_g"][1]), cols(i["final_g"]), cols(i["norm1_w_2"][0]),
             cols(i["norm2_w_2"][0]), cols(i["final_norm_w_2"]), cols(i["onorm_w_2"][0]), conv,
             rep(np.tile(i["a_log_2"][0], 2)), rep(np.tile(i["dt_bias_2"][0], 2)), rep(np.tile(b36, 2)),
             rows(i["w_in_2"][0][:, 3584:3592]), rows(w36)]
    return np.concatenate(parts, axis=1)


def build(nc, weights, vectors_in, tables_in, tokens_in, rel_bias, skew, out):
    with ExitStack() as ctx:
        def sb(name, *shape):
            return ctx.enter_context(nc.sbuf_tensor(name, list(shape), F32))

        def sem(name):
            return ctx.enter_context(nc.semaphore(name))

        ring = sb("ring", P, SLOTS, UNIT)
        vec = sb("vec", P, NVEC)
        tab = sb("tab", P, NTAB)
        h = sb("h", P, DT, T0)
        hn = sb("hn", P, DT, T0)
        sq = sb("sq", P, DT, T0)
        rms = sb("rms", P, T0)
        rstd = sb("rstd", P, T0)
        mod = sb("mod", P, MODS * DT)
        relb = sb("relb", P, AH)
        small = sb("small", P, 160)
        stats = sb("stats", P, 8 * (MH + AH))
        eps_t = sb("eps_t", P, 4)
        zero_w = sb("zero_w", P, P)
        rt = sb("rt", P, 640)
        rounds_t = ctx.enter_context(nc.sbuf_tensor("rounds_t", [P, 1], mybir.dt.int32))
        arena = sb("arena", P, 23400)

        cursor = [0]

        def carve(*shape, at=None):
            if at is not None:
                cursor[0] = at
            n = int(np.prod(shape))
            a = arena[:, cursor[0]:cursor[0] + n]
            cursor[0] += n
            assert cursor[0] <= 23400, cursor[0]
            if len(shape) == 2:
                a = a.rearrange("p (a b) -> p a b", a=shape[0])
            return a

        qk = carve(4 * RH, T0, at=0)
        gate_r = carve(4 * RH, T0)
        o_r = carve(4 * RH, T0)
        sc_r = carve(2, SC_W)
        rope_t = carve(4, T0)
        v_r_at = cursor[0]
        v_r = carve(3, RH * RDV)
        ff_act = carve(FT, T0, at=v_r_at)
        ff_gate = carve(2, T0)
        ckv = carve(KVT, T0, at=0)
        kvn = carve(DT, T0)
        krope = carve(1, T0)
        k_m = carve(MH, T0)
        v_m = carve(3, MH * P)
        cq = carve(QT, SEQ)
        q_m = carve(MH, SEQ)
        qrope = carve(4, SEQ)
        mrope_t = carve(2, T0)
        p_m = carve(2, MLA_W)
        pt_m = carve(1, 3 * P)
        pt_meta = carve(1, SEQ)
        o_m = carve(MH, SEQ)
        raw_b = carve(12, SEQ + CONV - 1, at=0)
        cb = carve(12, SEQ)
        q_a = carve(8, SEQ)
        v_a = carve(2, 512)
        z_b = carve(BH, SEQ)
        gates = carve(16, SEQ)
        o_b = carve(BH, SEQ)
        delta_at = cursor[0]
        NP = 2 * BH
        LT = carve(NP, P)
        X = carve(NP, P)
        Y = carve(NP, P)
        TM = carve(NP, P)
        PT = carve(NP, P)
        decT = carve(NP, P)
        ML = carve(NP, P)

        def problems(a):
            return a.rearrange("p a (t b) -> p (a t) b", t=2)

        qg = problems(cb[:, 0:BH, :])
        k_tok = problems(cb[:, BH:2 * BH, :])
        kd = problems(cb[:, 2 * BH:3 * BH, :])
        wT = k_tok
        raw_flat = raw_b.rearrange("p a b -> p (a b)")
        v_tok = raw_flat[:, 0:NP * P].rearrange("p (a b) -> p a b", a=NP)
        u_tok = raw_flat[:, NP * P:2 * NP * P].rearrange("p (a b) -> p a b", a=NP)
        st = decT[:, 0:BH, :]
        vn = decT[:, BH:2 * BH, :]
        sq_flat = sq[:, :, :].rearrange("p a b -> p (a b)")
        l2sq = sq_flat[:, 0:8 * SEQ]
        obsq = sq_flat[:, 0:BH * SEQ]
        bias_a = tab[:, 0:AH * MOBA_W].rearrange("p (a b) -> p a b", a=AH)
        bias_w = v_r.rearrange("p a b -> p (a b)")[:, 0:AH * 512].rearrange("p (a b) -> p a b", a=AH)
        o_a = carve(4, SEQ, at=delta_at)
        p_a = carve(2, MOBA_W)
        pt_a = carve(1, 3 * P)
        m_up = carve(DT, SEQ)
        up_t = carve(2, SEQ)
        h_tok = carve(2, D, at=0)
        sel = carve(2, P)
        sel_w = carve(2, P)
        sel_t = carve(1, SEQ)
        e_in = carve(DT, P)
        e_gate = carve(4, CAP)
        e_act = carve(4, CAP)
        e_out = carve(DT, P)
        e_out_t = carve(DT, P)
        RT, cur = {}, 0
        for name, k in [("logits", 2 * 36), ("gmax", 2), ("g_diff", 8), ("g_exp", 8), ("g_sum", 2), ("g_top", 2),
                        ("g_hit", 8), ("g_first", 2), ("g_one", 8), ("prod", 64), ("le", 16), ("m1", 2), ("hit1", 16),
                        ("first1", 2), ("one1", 16), ("le2", 16), ("m2", 2), ("hit2", 16), ("first2", 2), ("one2", 16),
                        ("t_diff", 2), ("t_exp", 2), ("t_sum", 2), ("w1", 2), ("w2", 2), ("ce", 16), ("comb", 64), ("hit", 16),
                        ("used", 64), ("rank", 64), ("most", 1), ("over", 1)]:
            RT[name] = (cur, k)
            cur += k

        def router(name, groups=None):
            a, k = RT[name]
            v = rt[:, a:a + k]
            return v if groups is None else v.rearrange("p (a b) -> p a b", a=groups)

        comb = router("comb", 2)
        SM = dict(c=0, g=16, beta=24, b=40, a=48, sp=56, ea=64, G=72, R=80, H=88, eG=104, eR=112, eH=120, abs=136, bg=144)
        G_COL = [(p % 2) * BH + p // 2 for p in range(2 * BH)]

        def M(name, k=0, n=1):
            return small[:, SM[name] + k:SM[name] + k + n]

        bank = [ctx.enter_context(nc.psum_tensor(f"bank{n}", [P, 512], F32)) for n in range(8)]

        def V(name, k=0, n=1):
            return vec[:, VEC[name] + k:VEC[name] + k + n]

        def C(name, k=0, n=P, rows=P):
            return tab[0:rows, TAB[name] + k:TAB[name] + k + n]

        ident, ones = C("ident"), C("ones")

        slot_loaded = [sem(f"slot_loaded{s}") for s in range(SLOTS)]
        unit_begun = sem("unit_begun")
        tile_done = sem("tile_done")
        evacuated = [sem(f"evacuated{b}") for b in range(BANKS)]
        vec_loaded, tab_loaded, tok_loaded = sem("vec_loaded"), sem("tab_loaded"), sem("tok_loaded")
        rel_loaded = sem("rel_loaded")
        squared, summed, rooted, normed = sem("squared"), sem("summed"), sem("rooted"), sem("normed")
        dve_step, act_step = sem("dve_step"), sem("act_step")

        made = {}

        def S(name):
            if name not in made:
                made[name] = sem(name)
            return made[name]

        def done(n):
            return n + 1

        def freed(n):
            return n // BANKS + 1

        def wait_stored(eng, n):
            eng.wait_ge(evacuated[n % BANKS], freed(n))

        at = {}
        n = 0
        for name, count in [("qk", 4 * RH)]:
            at[name] = n
            n += count
        at["v"] = n
        n += 3 * RH
        for hh in range(RH):
            at["gate", hh] = n
            at["av", hh] = n + 4
            n += 8
        for name, count in [("wo0", DT), ("ffn0", 2 * FT), ("down0", DT), ("kva", KVT + 1), ("qa", QT), ("kn", MH),
                            ("vm", 6), ("qn", MH), ("qr", 4), ("am", MH), ("wo1", DT), ("ffn1", 2 * FT),
                            ("down1", DT), ("qkvb", 12), ("qka", 8), ("va", 2), ("z", BH), ("gates", 16),
                            ("aa", AH), ("up", 2 * DT), ("wout", DT)]:
            at[name] = n
            n += count

        norm_k = [("mix0", DT), ("ffn0", DT), ("mix1", DT), ("ckv", KVT), ("cq", QT), ("ffn1", DT), ("final", DT),
                  ("n1", DT), ("n2", DT), ("final2", DT)]
        norm_no = {name: j for j, (name, _) in enumerate(norm_k)}
        norm_sq, norm_out = {}, {}
        a = b = 0
        for name, k in norm_k:
            norm_sq[name], norm_out[name] = a, b
            a += k
            b += k + (DT if name == "mix1" else 0)
        XC = slice(META, T0)
        ALL = slice(0, T0)

        block = ctx.enter_context(nc.Block())

        @block.sync
        def _(sp):
            def load(slot, unit):
                sp.dma_start(ring[:, slot, :], unit).then_inc(slot_loaded[slot], 16)

            for s in range(SLOTS):
                load(s, weights[s])
            rounds = UNITS // SLOTS
            with sp.Fori(1, rounds) as r:
                for s in range(SLOTS):
                    sp.wait_ge(unit_begun, (r - 1) * SLOTS + s + 2)
                    load(s, weights[bass.ds(r * SLOTS + s, 1)].rearrange("a p n -> (a p) n"))
            for u in range(rounds * SLOTS, UNITS):
                sp.wait_ge(unit_begun, u - SLOTS + 2)
                load(u % SLOTS, weights[u])
            sp.wait_ge(S("rounds_ready"), 1)
            more = sp.value_load(rounds_t[0:1, 0:1], min_val=1, max_val=SEQ // CAP)
            first = UNITS - PAIRS * SLOTS
            with sp.If(more > 1):
                with sp.Fori(1, more) as r:
                    with sp.Fori(0, PAIRS) as pair:
                        for s in range(SLOTS):
                            sp.wait_ge(unit_begun, (r * PAIRS + pair) * SLOTS + (first + s - SLOTS + 2))
                            load((first + s) % SLOTS,
                                 weights[bass.ds(pair * SLOTS + (first + s), 1)].rearrange("a p n -> (a p) n"))
            for k in range(DT):
                sp.wait_ge(normed, norm_out["final2"] + k + 1)
                sp.dma_start(out[:, k, :], hn[:, k, 0:SEQ]).then_inc(S("out_stored"), 16)
            sp.wait_ge(S("out_stored"), 16 * DT)

        @block.gpsimd
        def _(pool):
            nc.gpsimd.memset(relb[:, :], NEG).then_inc(S("rel_zeroed"), 1)
            pool.wait_ge(S("rel_zeroed"), 1)
            pool.dma_start(relb[0:BUCKETS, :], rel_bias).then_inc(rel_loaded, 16)
            pool.wait_ge(S("bias_row"), AH)
            pool.dma_start(skew.rearrange("a p x -> p a x"), bias_w).then_inc(S("skew_written"), 16)
            pool.wait_ge(S("skew_written"), 16)
            pool.wait_ge(S("ret_out"), 4 * RH)
            flat = P * 512
            for a in range(AH):
                for off, lo, n in ((255, 0, P), (127, P, SEQ)):
                    pool.dma_start(bias_a[:, a, lo:lo + n],
                                   bass.AP(skew.tensor, a * flat + off, [[511, P], [1, n]])).then_inc(S("bias_loaded"), 16)
            pool.wait_ge(S("bias_loaded"), 16 * 2 * AH)

        @block.tensor
        def _(pe):
            mm = nc.tensor.matmul
            pos = [0, 0]

            def weight(k_offset=0, turn=None, per_turn=0):
                blk = pos[0]
                pos[0] += 1
                unit, place = divmod(blk, UB)
                slot = unit % SLOTS
                if place == 0:
                    want = 16 * (unit // SLOTS + 1)
                    pe.wait_ge(slot_loaded[slot], want if turn is None else turn * (16 * per_turn) + want)
                return ring[:, slot, place * P:(place + 1) * P], place == 0

            def narrow(K, moving, cols, ready=None, turn=None, tiles_per_turn=0, rounds_per_turn=0):
                t = pos[1]
                pos[1] += 1
                dst = bank[t % BANKS]
                if t >= BANKS:
                    want = freed(t - BANKS)
                    pe.wait_ge(evacuated[t % BANKS],
                               want if turn is None else turn * (tiles_per_turn // BANKS) + want)
                for k in range(K):
                    if ready:
                        ready(k)
                    w, first = weight(turn=turn, per_turn=rounds_per_turn)
                    last = mm(dst[:, 0:cols], w, moving(k), start=k == 0, stop=k == K - 1)
                    if first:
                        last.then_inc(unit_begun, 1)
                last.then_inc(tile_done, 1)

            def wide(K, stationary, tiles, ready=None):
                t = pos[1]
                pos[1] += len(tiles)
                for j in range(len(tiles)):
                    if t + j >= BANKS:
                        wait_stored(pe, t + j - BANKS)
                for k in range(K):
                    if ready:
                        ready(k)
                    unit, half = divmod(pos[0] // 4, 2)
                    pos[0] += 4
                    slot = unit % SLOTS
                    if half == 0:
                        pe.wait_ge(slot_loaded[slot], 16 * (unit // SLOTS + 1))
                    for j, (lo, hi) in enumerate(tiles):
                        last = mm(bank[(t + j) % BANKS][0:hi - lo, :], stationary(k)[:, lo:hi],
                                  ring[:, slot, half * 512:(half + 1) * 512], start=k == 0, stop=k == K - 1)
                        if half == 0 and j == 0:
                            last.then_inc(unit_begun, 1)
                        if k == K - 1:
                            last.then_inc(tile_done, 1)

            def norm_sum(name, K, cols):
                for k in range(K):
                    pe.wait_ge(squared, norm_sq[name] + k + 1)
                    last = mm(bank[7][:, 0:cols], ones, sq[:, k, 0:cols], start=k == 0, stop=k == K - 1)
                last.then_inc(summed, 1)

            def normed_ready(name, extra=0):
                return lambda k: pe.wait_ge(normed, norm_out[name] + extra + k + 1)

            pe.wait_ge(S("c_silu"), 1)
            pe.wait_ge(tab_loaded, 16)
            with pe.Fori(0, MODS * DT // (2 * SLOTS)) as r:
                for b in range(2):
                    pe.wait_ge(S("mod_stored"), r * 2 + b + 1)
                    for s in range(SLOTS):
                        pe.wait_ge(slot_loaded[s], r * 32 + 16 * (b + 1))
                        for k in range(DT):
                            last = mm(bank[b][:, s:s + 1], ring[:, s, k * P:(k + 1) * P],
                                      small[:, k:k + 1], start=k == 0, stop=k == DT - 1, skip_group_check=True)
                            if k == 0:
                                last.then_inc(unit_begun, 1)
                    last.then_inc(S("mod_summed"), 1)
            pos[0] += MODS * DT * UB

            pe.wait_ge(rel_loaded, 16)
            for a in range(AH):
                if a >= 2:
                    pe.wait_ge(S("bias_row"), a - 1)
                mm(bank[4 + a % 2][:, :], relb[0:BUCKETS + 1, a:a + 1].to_broadcast([BUCKETS + 1, P]),
                   C("bucket", 0, 512, BUCKETS + 1), start=True, stop=True).then_inc(S("bias_sum"), 1)

            norm_sum("mix0", DT, T0)
            ready = normed_ready("mix0")
            for t in range(4 * RH):
                narrow(DT, lambda k: hn[:, k, :], T0, ready if t == 0 else None)
            for g in range(RH):
                wide(DT, lambda k: hn[:, k, :], TOK)

            def ret_mean(hh):
                for d in range(4):
                    wait_stored(pe, at["av", hh] + d)
                    last = mm(bank[6][:, 0:T0], ones, o_r[:, 4 * hh + d, :], start=d == 0, stop=d == 3)
                last.then_inc(S("gn_mean"), 1)

            def ret_var(hh):
                pe.wait_ge(S("gn_squared"), hh + 1)
                for d in range(4):
                    last = mm(bank[7][:, 0:T0], ones, sq[:, d, :], start=d == 0, stop=d == 3)
                last.then_inc(S("gn_var"), 1)

            for hh in range(RH):
                pe.wait_ge(S("roped"), 2 * hh + 2)
                if hh:
                    pe.wait_ge(S("decayed"), hh)
                for half in range(2):
                    mm(bank[4][0:META, 0:T0], qk[:, 4 * hh + 2 + half, 0:META], qk[:, 4 * hh + half, :],
                       start=half == 0, stop=half == 1)
                for j, (lo, hi) in enumerate(TOK[1:]):
                    for half in range(2):
                        last = mm(bank[5][:, j * SEQ:j * SEQ + T0 - lo], qk[:, 4 * hh + 2 + half, lo:hi],
                                  qk[:, 4 * hh + half, lo:T0], start=half == 0, stop=half == 1)
                last.then_inc(S("ret_scored"), 1)
                if hh:
                    ret_mean(hh - 1)
                for t in range(4):
                    if hh and t == 2:
                        ret_var(hh - 1)
                    narrow(DT, lambda k: hn[:, k, :], T0)
                pe.wait_ge(S("decayed"), hh + 1)
                if hh == 0:
                    wait_stored(pe, at["v"] + 3 * RH - 1)
                for d in range(4):
                    t = pos[1]
                    pos[1] += 1
                    wait_stored(pe, t - BANKS)
                    dst, col, c0 = bank[t % BANKS], hh * RDV + d * P, 0
                    for j, (lo, hi) in enumerate(TOK):
                        last = mm(dst[:, lo:T0], v_r[0:hi - lo, j, col:col + P], sc_r[0:hi - lo, hh % 2, c0:c0 + T0 - lo],
                                  start=j == 0, stop=j == 2, skip_group_check=True)
                        c0 += T0 - lo
                    last.then_inc(tile_done, 1)
            ret_mean(RH - 1)
            ret_var(RH - 1)
            for t in range(DT):
                narrow(4 * RH, lambda k: o_r[:, k, :], T0,
                       (lambda k: pe.wait_ge(S("ret_out"), k + 1)) if t == 0 else None)

            def feed_forward(layer, src, cols):
                name = f"ffn{layer}"
                norm_sum(name, DT, cols)
                ready = normed_ready(name)
                for k in range(DT):
                    ready(k)
                turns = 2 * FT // SLOTS
                start = list(pos)
                with pe.Fori(0, turns) as r:
                    for t in range(SLOTS):
                        narrow(DT, lambda k: src(hn, k), cols, turn=r, tiles_per_turn=SLOTS, rounds_per_turn=1)
                pos[0] = start[0] + turns * SLOTS * UB
                pos[1] = start[1] + turns * SLOTS
                for t in range(turns * SLOTS, 2 * FT):
                    narrow(DT, lambda k: src(hn, k), cols)
                for t in range(DT):
                    narrow(FT, lambda k: ff_act[:, k, 0:cols], cols,
                           (lambda k: wait_stored(pe, at[name] + 2 * k + 1)) if t == 0 else None)

            feed_forward(0, lambda a, k: a[:, k, :], T0)

            norm_sum("mix1", DT, T0)
            for t in range(KVT + 1):
                narrow(DT, lambda k: kvn[:, k, :], T0, normed_ready("mix1") if t == 0 else None)
            for t in range(QT):
                narrow(DT, lambda k: hn[:, k, XC], SEQ, normed_ready("mix1", DT) if t == 0 else None)
            norm_sum("ckv", KVT, T0)
            norm_sum("cq", QT, SEQ)
            for t in range(MH):
                narrow(KVT, lambda k: ckv[:, k, :], T0, normed_ready("ckv") if t == 0 else None)
            for g in range(2):
                wide(KVT, lambda k: ckv[:, k, :], TOK)
            for t in range(MH + 4):
                narrow(QT, lambda k: cq[:, k, :], SEQ, normed_ready("cq") if t == 0 else None)

            def attention(tag, heads, score, put):
                for i in range(heads + 1):
                    if i < heads:
                        score(i, bank[4 + i % 2]).then_inc(S(tag + "_scored"), 1)
                    if i >= 1:
                        j = i - 1
                        pe.wait_ge(S(tag + "_p"), i)
                        if j:
                            pe.wait_ge(S(tag + "_pt"), j)
                        put(j)

            def mla_score(i, dst):
                if i == 0:
                    pe.wait_ge(S("q_roped"), 5)
                    wait_stored(pe, at["qn"] + MH - 1)
                if i >= 2:
                    pe.wait_ge(S("mla_p"), i - 1)
                r = 64 * (i % 2)
                for lo, hi, q0 in [(0, META + P, 0), (META + P, MLA_W, P)]:
                    w = hi - lo
                    mm(dst[:, lo:hi], q_m[:, i, q0:q0 + P], k_m[:, i, 0:w], start=True, stop=False)
                    last = mm(dst[:, lo:hi], qrope[r:r + ROPE, i // 2, q0:q0 + P], krope[r:r + ROPE, 0, 0:w],
                              start=False, stop=True)
                return last

            def values(tag, j, pv, v_cols, meta, rows):
                key0 = META if meta else 0
                second = key0 + P
                nc.tensor.transpose(bank[6][:, 0:P], pv[:, key0:key0 + P], ident)
                nc.tensor.transpose(bank[6][:, P:2 * P], pv[:, second + key0:second + key0 + P], ident)
                last = nc.tensor.transpose(bank[6][:, 2 * P:3 * P], pv[:, second + key0 + P:second + key0 + 2 * P], ident)
                last.then_inc(S(tag + "_turned"), 1)
                if meta:
                    if j:
                        pe.wait_ge(S(tag + "_ptm"), j)
                    nc.tensor.transpose(bank[7][0:META, 0:P], pv[:, 0:META], ident)
                    nc.tensor.transpose(bank[7][0:META, P:2 * P], pv[:, second:second + META],
                                        ident).then_inc(S(tag + "_turnedm"), 1)
                t = pos[1]
                pos[1] += 1
                wait_stored(pe, t - BANKS)
                dst = bank[t % BANKS]
                pe.wait_ge(S(tag + "_pt"), j + 1)
                pt = pt_m if meta else pt_a
                v = v_m if meta else v_a
                o = 1 if meta else 0
                mm(dst[rows, 0:SEQ], v[:, o, v_cols], pt[:, 0, 0:SEQ], start=True, stop=False, skip_group_check=True)
                last = mm(dst[rows, P:SEQ], v[:, o + 1, v_cols], pt[:, 0, SEQ:3 * P], start=False, stop=not meta,
                          skip_group_check=True)
                if meta:
                    pe.wait_ge(S(tag + "_ptm"), j + 1)
                    last = mm(dst[rows, 0:SEQ], v[0:META, 0, v_cols], pt_meta[0:META, 0, :], start=False, stop=True,
                              skip_group_check=True)
                last.then_inc(tile_done, 1)

            def mla_values(j):
                if j == 0:
                    wait_stored(pe, at["vm"] + 5)
                values("mla", j, p_m[:, j % 2, :], slice(j * P, (j + 1) * P), True, slice(0, P))

            attention("mla", MH, mla_score, mla_values)
            for t in range(DT):
                narrow(MH, lambda k: o_m[:, k, :], SEQ,
                       (lambda k: wait_stored(pe, at["am"] + k)) if t == 0 else None)
            feed_forward(1, lambda a, k: a[:, k, XC], SEQ)
            norm_sum("final", DT, SEQ)

            norm_sum("n1", DT, SEQ)
            hb = lambda k: hn[:, k, 0:SEQ]
            for k in range(DT):
                pe.wait_ge(S("hb_ready"), k + 1)
            for tt in range(2):
                for k in range(DT):
                    last = mm(bank[4][:, 8 * tt:8 * tt + 8], hn[:, k, tt * P:(tt + 1) * P], V("wba", 8 * k, 8),
                              start=k == 0, stop=k == DT - 1)
            last.then_inc(S("ba_done"), 1)
            for t in range(12):
                narrow(DT, hb, SEQ)
            pe.wait_ge(S("g_ready"), 1)
            g = M("g", 0, 8)
            for j, name in enumerate(("upto", "chunk", "half0", "half1")):
                last = mm(bank[5][:, 8 * j:8 * j + 8], C(name), g, start=True, stop=True)
            last.then_inc(S("g_summed"), 1)
            pe.wait_ge(S("g_stored"), 1)
            for p in range(NP):
                last = mm(bank[6 + p // 4][:, (p % 4) * P:(p % 4 + 1) * P],
                          M("g", G_COL[p]).to_broadcast([P, P]), C("upto"), start=True, stop=True)
            last.then_inc(S("row_g"), 1)
            for p in range(NP):
                last = mm(bank[4 + p // 4][:, (p % 4) * P:(p % 4 + 1) * P],
                          M("beta", G_COL[p]).to_broadcast([P, P]), ident, start=True, stop=True)
            last.then_inc(S("row_beta"), 1)
            for t in range(8):
                narrow(DT, hb, SEQ)
            wide(DT, hb, [(0, P), (P, SEQ)])
            pe.wait_ge(S("l2_squared"), 8)
            pe.wait_ge(S("beta_rows"), 1)
            pe.wait_ge(S("exp_rows"), 1)
            for j in range(4):
                last = mm(bank[4 + j][:, :], ones, l2sq[:, j * 512:(j + 1) * 512], start=True, stop=True)
            last.then_inc(S("l2_summed"), 1)
            for t in range(BH):
                narrow(DT, hb, SEQ)
            pe.wait_ge(S("l2_done"), 1)
            for p in range(NP):
                kp = cb[:, BH + p // 2, (p % 2) * P:(p % 2 + 1) * P]
                last = mm(bank[4 + p // 4][:, (p % 4) * P:(p % 4 + 1) * P], kp, kp, start=True, stop=True)
            last.then_inc(S("gram_done"), 1)
            for p in range(NP):
                kp = cb[:, BH + p // 2, (p % 2) * P:(p % 2 + 1) * P]
                last = mm(bank[6 + p // 4][:, (p % 4) * P:(p % 4 + 1) * P], kp,
                          cb[:, p // 2, (p % 2) * P:(p % 2 + 1) * P], start=True, stop=True)
            last.then_inc(S("qk_done"), 1)
            narrow(DT, hb, SEQ)
            narrow(DT, hb, SEQ)
            pe.wait_ge(S("lt_ready"), 1)
            for p in range(NP):
                last = nc.tensor.transpose(bank[4 + p // 4][:, (p % 4) * P:(p % 4 + 1) * P],
                                           cb[:, BH + p // 2, (p % 2) * P:(p % 2 + 1) * P], ident)
            last.then_inc(S("k_turned"), 1)
            pe.wait_ge(S("pt_ready"), 1)
            for p in range(NP):
                last = nc.tensor.transpose(bank[6 + p // 4][:, (p % 4) * P:(p % 4 + 1) * P],
                                           cb[:, 2 * BH + p // 2, (p % 2) * P:(p % 2 + 1) * P], ident)
            last.then_inc(S("v_turned"), 1)
            narrow(DT, hb, SEQ)
            narrow(DT, hb, SEQ)
            pe.wait_ge(S("tok_ready"), 1)
            for lv in range(6):
                pe.wait_ge(S("ml_ready"), lv + 1)
                for half in range(2):
                    if lv and half == 0:
                        pe.wait_ge(S("inv_ready"), lv)
                    for p in range(4 * half, 4 * half + 4):
                        last = mm(bank[4 + half][:, (p % 4) * P:(p % 4 + 1) * P], ML[:, p, :],
                                  X[:, p, :] if lv else ident, start=True, stop=True)
                last.then_inc(S("mx_done"), 1)
                narrow(DT, hb, SEQ)
                if lv == 0:
                    continue
                pe.wait_ge(S("t_stored"), lv)
                for half in range(2):
                    for p in range(4 * half, 4 * half + 4):
                        last = mm(bank[6 + half][:, (p % 4) * P:(p % 4 + 1) * P], TM[:, p, :], Y[:, p, :],
                                  start=True, stop=True)
                last.then_inc(S("dy_done"), 1)
                if lv < 5:
                    for half in range(2):
                        for p in range(4 * half, 4 * half + 4):
                            last = mm(bank[4 + half][:, (p % 4) * P:(p % 4 + 1) * P], Y[:, p, :], TM[:, p, :],
                                      start=True, stop=True)
                    last.then_inc(S("dx_done"), 1)
                narrow(DT, hb, SEQ)
            pe.wait_ge(S("inv_ready"), 6)
            for p in range(NP):
                last = mm(bank[4 + p // 4][:, (p % 4) * P:(p % 4 + 1) * P], Y[:, p, :], v_tok[:, p, :],
                          start=True, stop=True)
            last.then_inc(S("u_done"), 1)
            for p in range(NP):
                last = mm(bank[6 + p // 4][:, (p % 4) * P:(p % 4 + 1) * P], k_tok[:, p, :], Y[:, p, :],
                          start=True, stop=True)
            last.then_inc(S("w_done"), 1)
            narrow(DT, hb, SEQ)
            for c in range(4):
                R, tt = CHUNK * (c % 2), c // 2
                rows = slice(R, R + CHUNK)
                if c == 0:
                    pe.wait_ge(S("u_stored"), 1)
                    pe.wait_ge(S("w_stored"), 1)
                if c:
                    pe.wait_ge(S("state_ready"), c)
                    for a in range(BH):
                        last = mm(bank[4][rows, a * P:(a + 1) * P], wT[:, 2 * a + tt, rows], st[:, a, :],
                                  start=True, stop=True)
                    last.then_inc(S("ws_done"), 1)
                pe.wait_ge(S("vn_ready"), c + 1)
                if c:
                    pe.wait_ge(S("ob_stored"), c)
                for a in range(BH):
                    dst = bank[5][:, a * CHUNK:(a + 1) * CHUNK]
                    if c:
                        mm(dst, st[:, a, :], qg[:, 2 * a + tt, rows], start=True, stop=False)
                    last = mm(dst, vn[rows, a, :], PT[rows, 2 * a + tt, rows], start=c == 0, stop=True)
                last.then_inc(S("ob_done"), 1)
                if c < 3:
                    for a in range(BH):
                        last = mm(bank[6][:, a * P:(a + 1) * P], kd[rows, 2 * a + tt, :], vn[rows, a, :],
                                  start=True, stop=True)
                    last.then_inc(S("ds_done"), 1)
            assert pos[1] == at["aa"]
            pe.wait_ge(S("ob_squared"), 1)
            for j in range(2):
                last = mm(bank[4 + j][:, :], ones, obsq[:, j * 512:(j + 1) * 512], start=True, stop=True)
            last.then_inc(S("ob_summed"), 1)

            def moba_score(i, dst):
                if i == 0:
                    wait_stored(pe, at["qka"] + 7)
                    pe.wait_ge(S("ob_rooted"), 1)
                if i >= 2:
                    pe.wait_ge(S("moba_p"), i - 1)
                r = slice(AHD * (i % 2), AHD * (i % 2) + AHD)
                mm(dst[:, 0:P], q_a[r, i // 2, 0:P], q_a[r, 4 + i // 2, 0:P], start=True, stop=True)
                return mm(dst[:, P:MOBA_W], q_a[r, i // 2, P:SEQ], q_a[r, 4 + i // 2, :], start=True, stop=True)

            def moba_values(j):
                if j == 0:
                    wait_stored(pe, at["va"] + 1)
                values("moba", j, p_a[:, j % 2, :], slice(j // 2 * P, (j // 2 + 1) * P), False, slice(0, P))

            attention("moba", AH, moba_score, moba_values)
            for k in range(4):
                wait_stored(pe, at["aa"] + 2 * k + 1)
            for t in range(DT):
                narrow(4, lambda k: o_a[:, k, :], SEQ)
                narrow(4, lambda k: o_b[:, k, :], SEQ,
                       (lambda k: pe.wait_ge(S("ob_ready"), 1)) if t == 0 else None)
            for t in range(DT):
                narrow(DT, lambda k: m_up[:, k, :], SEQ,
                       (lambda k: pe.wait_ge(S("m_ready"), k + 1)) if t == 0 else None)

            norm_sum("n2", DT, SEQ)
            for k in range(DT):
                pe.wait_ge(S("hb_ready"), DT + k + 1)
            for tt in range(2):
                for k in range(DT):
                    last = mm(bank[4][:, 36 * tt:36 * tt + 36], hn[:, k, tt * P:(tt + 1) * P], V("w36", 36 * k, 36),
                              start=k == 0, stop=k == DT - 1)
            last.then_inc(S("logits_done"), 1)

            for t in range(pos[1] - BANKS, pos[1]):
                wait_stored(pe, t)
            for tt in range(2):
                for k in range(DT):
                    last = nc.tensor.transpose(bank[2 * tt + k // 4][:, (k % 4) * P:(k % 4 + 1) * P],
                                               hn[:, k, tt * P:(tt + 1) * P], ident)
                last.then_inc(S("h_turned"), 1)
            pe.wait_ge(S("used_ready"), 1)
            used = router("used", 2)
            mm(bank[4][:, 0:NE], C("before"), used[:, 0, :], start=True, stop=True)
            mm(bank[4][:, NE:2 * NE], C("before"), used[:, 1, :], start=True, stop=False)
            mm(bank[4][:, NE:2 * NE], ones, used[:, 0, :], start=False, stop=True)
            for tt in range(2):
                last = mm(bank[4][:, 2 * NE:3 * NE], ones, used[:, tt, :], start=tt == 0, stop=tt == 1)
            last.then_inc(S("ranked"), 1)
            pe.wait_ge(S("h_tok_stored"), 4)
            pe.wait_ge(S("rounds_ready"), 1)
            for b in range(4, 8):
                mm(bank[b][:, :], zero_w[:, :], C("bucket", 0, 512), start=True, stop=False, skip_group_check=True)
            for b in (2, 3):
                mm(bank[b][:, :], zero_w[:, :], C("bucket", 0, 512), start=True, stop=True)\
                    .then_inc(S("down_done"), 1)

            def turn_out(g):
                pe.wait_ge(S("out_stored_a"), g + 1)
                pe.wait_ge(S("out_stored_v"), g + 1)
                for t in range(DT):
                    last = nc.tensor.transpose(bank[2 + t // 4][:, (t % 4) * P:(t % 4 + 1) * P], e_out[:, t, :], ident)
                last.then_inc(S("out_turned"), 1)

            def scatter(g, final=False):
                pe.wait_ge(S("turned_stored_a"), g + 1)
                pe.wait_ge(S("turned_stored_v"), g + 1)
                pe.wait_ge(S("sel_t_stored"), g + 1)
                for t in range(DT):
                    last = mm(bank[4 + t // 2][:, (t % 2) * SEQ:(t % 2 + 1) * SEQ], e_out_t[:, t, :], sel_t[:, 0, :],
                              start=False, stop=final and t % 2 == 1, skip_group_check=True)
                return last

            pe_rounds = pe.value_load(rounds_t[0:1, 0:1], min_val=1, max_val=SEQ // CAP)
            with pe.Fori(0, pe_rounds) as r:
                with pe.Fori(0, PAIRS) as pair:
                    start = list(pos)
                    g = r * PAIRS + pair
                    pe.wait_ge(S("sel_ready"), g + 1)
                    pe.wait_ge(S("e_act_ready"), g + 1)
                    pe.wait_ge(S("sel_t_stored"), g + 1)
                    for k in range(DT):
                        for tt in range(2):
                            last = mm(bank[k // 4][:, (k % 4) * P:(k % 4 + 1) * P], h_tok[:, tt, k * P:(k + 1) * P],
                                      sel[:, tt, :], start=tt == 0, stop=tt == 1)
                        if k % 4 == 3:
                            last.then_inc(S("gathered"), 1)
                    turn_out(g)
                    pe.wait_ge(S("in_stored_a"), g + 1)
                    pe.wait_ge(S("in_stored_v"), g + 1)
                    for t in range(8):
                        for k in range(DT):
                            w, fresh = weight(turn=g, per_turn=1)
                            last = mm(bank[0][:, t * CAP:(t + 1) * CAP], w,
                                      e_in[:, k, (t // 4) * CAP:(t // 4 + 1) * CAP], start=k == 0, stop=k == DT - 1)
                            if fresh:
                                last.then_inc(unit_begun, 1)
                    last.then_inc(S("gate_up_done"), 1)
                    scatter(g)
                    for tt in range(2):
                        last = nc.tensor.transpose(bank[1][:, tt * P:(tt + 1) * P], sel_w[:, tt, :], ident)
                    last.then_inc(S("sel_turned"), 1)
                    pe.wait_ge(S("e_act_ready"), g + 2)
                    for t in range(DT):
                        for j in range(2):
                            for k in range(2):
                                w, fresh = weight(turn=g, per_turn=1)
                                c0 = (t % 4) * P + j * CAP
                                last = mm(bank[2 + t // 4][:, c0:c0 + CAP], w, e_act[:, 2 * j + k, :],
                                          start=k == 0, stop=k == 1)
                                if fresh:
                                    last.then_inc(unit_begun, 1)
                        if t % 4 == 3:
                            last.then_inc(S("down_done"), 1)
                    assert pos[0] - start[0] == SLOTS * UB
            turn_out(pe_rounds * PAIRS)
            scatter(pe_rounds * PAIRS, final=True).then_inc(S("moe_done"), 1)
            pe.wait_ge(S("moe_added"), DT)
            norm_sum("final2", DT, SEQ)

        @block.scalar
        def _(act):
            fn = nc.scalar.activation
            act.dma_start(vec[:, :], vectors_in).then_inc(vec_loaded, 16)
            act.dma_start(h[:, :, :], tokens_in).then_inc(tok_loaded, 16)
            act.dma_start(tab[:, :], tables_in).then_inc(tab_loaded, 16)
            tile = [0]

            def take():
                t = tile[0]
                tile[0] += 1
                act.wait_ge(tile_done, done(t))
                return bank[t % BANKS], evacuated[t % BANKS]

            def norm(name, src, K, cols, width, ready, eps=RMS_EPS):
                for k in range(K):
                    ready(k)
                    fn(sq[:, k, 0:cols], src(k), ACT.Square).then_inc(squared, 1)
                act.wait_ge(summed, norm_no[name] + 1)
                if norm_no[name]:
                    act.wait_ge(normed, norm_out[norm_k[norm_no[name] - 1][0]] + 1)
                fn(rms[:, 0:cols], bank[7][:, 0:cols], ACT.Sqrt, bias=eps_col(eps), scale=1.0 / width).then_inc(rooted, 1)

            def eps_col(eps):
                return eps_t[:, 0:1] if eps == RMS_EPS else eps_t[:, 1:2]

            act.wait_ge(vec_loaded, 16)
            fn(small[:, 0:DT], V("c", 0, DT), ACT.Silu).then_inc(S("c_silu"), 1)
            act.wait_ge(tok_loaded, 16)
            act.wait_ge(S("eps_set"), 1)
            norm("mix0", lambda k: h[:, k, :], DT, T0, D, lambda k: None)
            tile[0] = at["v"]
            act.wait_ge(S("skew_written"), 16)
            for g in range(RH):
                for j, (lo, hi) in enumerate(TOK):
                    src, free = take()
                    fn(v_r[0:hi - lo, j, g * RDV:(g + 1) * RDV], src[0:hi - lo, :], ACT.Copy).then_inc(free, 1)

            def gn_root(hh):
                act.wait_ge(S("gn_var"), hh + 1)
                fn(rms[:, :], bank[7][:, 0:T0], ACT.Sqrt, bias=eps_col(GN_EPS), scale=1.0 / RDV).then_inc(S("gn_root"), 1)

            def gn_square(hh):
                act.wait_ge(S("gn_centred"), hh + 1)
                fn(sq[:, 0:4, :], o_r[:, 4 * hh:4 * hh + 4, :], ACT.Square).then_inc(S("gn_squared"), 1)

            for hh in range(RH):
                if hh:
                    gn_square(hh - 1)
                for t in range(4):
                    if hh and t == 2:
                        gn_root(hh - 1)
                    src, free = take()
                    fn(gate_r[:, 4 * hh + t, :], src[:, 0:T0], ACT.Silu).then_inc(free, 1)
                for d in range(4):
                    src, free = take()
                    fn(o_r[:, 4 * hh + d, :], src[:, 0:T0], ACT.Copy).then_inc(free, 1)
            gn_square(RH - 1)
            gn_root(RH - 1)

            def feed_forward(layer, first_tile, cols, src):
                name = f"ffn{layer}"
                res = at["wo0"] if layer == 0 else at["wo1"]
                norm(name, src, DT, cols, D, lambda k: wait_stored(act, res + k))
                assert at[name] == first_tile
                turns = 2 * FT // SLOTS

                def gate(pair, turn=None):
                    t = first_tile + 2 * pair
                    more = lambda n, per: n if turn is None else turn * per + n
                    act.wait_ge(tile_done, more(done(t), SLOTS))
                    act.wait_ge(evacuated[(t + 1) % BANKS], more(freed(t + 1) - 1, SLOTS // BANKS))
                    fn(ff_gate[:, pair % 2, 0:cols], bank[t % BANKS][:, 0:cols], ACT.Silu).then_inc(evacuated[t % BANKS], 1)

                with act.Fori(0, turns) as r:
                    for j in range(SLOTS // 2):
                        gate(j, r)
                for pair in range(turns * SLOTS // 2, FT):
                    gate(pair)

            feed_forward(0, at["ffn0"], T0, lambda k: h[:, k, :])

            norm("mix1", lambda k: h[:, k, :], DT, T0, D, lambda k: wait_stored(act, at["down0"] + k))
            tile[0] = at["kva"]
            for t in range(KVT):
                src, free = take()
                fn(ckv[:, t, :], src[:, 0:T0], ACT.Copy).then_inc(free, 1)
            tile[0] = at["qa"]
            for t in range(QT):
                src, free = take()
                fn(cq[:, t, :], src[:, 0:SEQ], ACT.Copy).then_inc(free, 1)
            norm("ckv", lambda k: ckv[:, k, :], KVT, T0, KVR, lambda k: wait_stored(act, at["kva"] + k))
            norm("cq", lambda k: cq[:, k, :], QT, SEQ, QR, lambda k: wait_stored(act, at["qa"] + k))
            for t in range(MH):
                src, free = take()
                fn(k_m[:, t, :], src[:, 0:T0], ACT.Copy).then_inc(free, 1)
            for g in range(2):
                for j, (lo, hi) in enumerate(TOK):
                    src, free = take()
                    fn(v_m[0:hi - lo, j, g * 512:(g + 1) * 512], src[0:hi - lo, :], ACT.Copy).then_inc(free, 1)
            for t in range(MH):
                src, free = take()
                fn(q_m[:, t, :], src[:, 0:SEQ], ACT.Copy).then_inc(free, 1)

            def attention(tag, heads, probs, parts, stat, pt, store):
                for i in range(heads + 1):
                    if i < heads:
                        act.wait_ge(S(tag + "_max"), i + 1)
                        s = stat(i)
                        for j, (lo, hi) in enumerate(parts):
                            a = probs[:, i % 2, lo:hi]
                            last = fn(a, a, ACT.Exp, bias=s[:, 2 + j:3 + j], accum_out=s[:, 4 + j:5 + j])
                        last.then_inc(S(tag + "_exp"), 1)
                    if i >= 1:
                        j = i - 1
                        act.wait_ge(S(tag + "_turned"), j + 1)
                        fn(pt[:, 0, :], bank[6][:, 0:3 * P], ACT.Copy).then_inc(S(tag + "_pt"), 1)
                        store(j)

            tile[0] = at["am"]

            def mla_store(j):
                src, free = take()
                fn(o_m[:, j, :], src[:, 0:SEQ], ACT.Copy).then_inc(free, 1)

            attention("mla", MH, p_m, [(0, META + P), (META + P, MLA_W)], lambda i: stats[:, 8 * i:8 * i + 8],
                      pt_m, mla_store)
            feed_forward(1, at["ffn1"], SEQ, lambda k: h[:, k, XC])
            norm("final", lambda k: h[:, k, XC], DT, SEQ, D, lambda k: wait_stored(act, at["down1"] + k))

            def shifted(name, shift, ready):
                norm(name, lambda k: h[:, k, XC], DT, SEQ, D, ready)
                for k in range(DT):
                    act.wait_ge(normed, norm_out[name] + k + 1)
                    fn(hn[:, k, 0:SEQ], hn[:, k, 0:SEQ], ACT.Identity,
                       bias=mod[:, shift * DT + k:shift * DT + k + 1]).then_inc(S("hb_ready"), 1)

            act.wait_ge(S("mod_ready"), 2)
            shifted("n1", 0, lambda k: act.wait_ge(normed, norm_out["final"] + k + 1))
            act.wait_ge(S("ba_split"), 1)
            fn(M("beta", 0, 8), M("b", 0, 8), ACT.Sigmoid).then_inc(S("beta_ready"), 1)
            fn(M("sp", 0, 8), M("abs", 0, 8), ACT.Exp, scale=-1.0)
            fn(M("ea", 0, 8), V("alog", 0, 8), ACT.Exp).then_inc(act_step, 1)
            act.wait_ge(act_step, 1)
            fn(M("sp", 0, 8), M("sp", 0, 8), ACT.Ln, bias=eps_t[:, 2:3]).then_inc(S("softplus_ln"), 1)
            tile[0] = at["qkvb"]
            for t in range(12):
                src, free = take()
                fn(raw_b[:, t, CONV - 1:], src[:, 0:SEQ], ACT.Copy).then_inc(free, 1)
            act.wait_ge(S("g_stored"), 1)
            fn(M("eG", 0, 32), M("G", 0, 32), ACT.Exp).then_inc(S("g_exp"), 1)
            act.wait_ge(S("row_g"), 1)
            for j in range(2):
                last = fn(TM[:, 4 * j:4 * j + 4, :], bank[6 + j][:, :].rearrange("p (a b) -> p a b", a=4), ACT.Exp)
            last.then_inc(S("exp_rows"), 1)
            act.wait_ge(S("dec_diff"), 1)
            fn(decT[:, :, :], decT[:, :, :], ACT.Exp).then_inc(S("dec_exp"), 1)
            tile[0] = at["qka"]
            for t in range(8):
                src, free = take()
                fn(q_a[:, t, :], src[:, 0:SEQ], ACT.Copy).then_inc(free, 1)
            for t in range(2):
                src, free = take()
                fn(v_a[:, t, :], src[:, :], ACT.Copy).then_inc(free, 1)
            for t in range(12):
                act.wait_ge(S("conv_done"), t + 1)
                fn(cb[:, t, :], cb[:, t, :], ACT.Silu).then_inc(S("conv_silu"), 1)
            for t in range(8):
                act.wait_ge(S("conv_silu"), t + 1)
                fn(l2sq[:, t * SEQ:(t + 1) * SEQ], cb[:, t, :], ACT.Square).then_inc(S("l2_squared"), 1)
            act.wait_ge(S("l2_summed"), 1)
            for j in range(4):
                last = fn(l2sq[:, j * 512:(j + 1) * 512], bank[4 + j][:, :], ACT.Sqrt, bias=eps_t[:, 0:1])
            last.then_inc(S("l2_root"), 1)
            for t in range(BH):
                src, free = take()
                fn(z_b[:, t, :], src[:, 0:SEQ], ACT.Silu).then_inc(free, 1)

            def gate():
                t = tile[0] - at["gates"]
                src, free = take()
                fn(gates[:, t, :], src[:, 0:SEQ], ACT.Sigmoid).then_inc(free, 1)

            gate()
            gate()
            gate()
            gate()
            for lv in range(6):
                if lv:
                    act.wait_ge(S("mx_done"), lv + 1)
                    for j in range(2):
                        last = fn(TM[:, 4 * j:4 * j + 4, :], bank[4 + j][:, :].rearrange("p (a b) -> p a b", a=4),
                                  ACT.Copy)
                    last.then_inc(S("t_stored"), 1)
                gate()
                if lv:
                    gate()
            act.wait_ge(S("u_done"), 1)
            for j in range(2):
                last = fn(u_tok[:, 4 * j:4 * j + 4, :], bank[4 + j][:, :].rearrange("p (a b) -> p a b", a=4), ACT.Copy)
            last.then_inc(S("u_stored"), 1)
            act.wait_ge(S("w_done"), 1)
            for j in range(2):
                last = fn(wT[:, 4 * j:4 * j + 4, :], bank[6 + j][:, :].rearrange("p (a b) -> p a b", a=4), ACT.Copy)
            last.then_inc(S("w_stored"), 1)
            gate()
            assert tile[0] == at["aa"]
            for c in range(4):
                act.wait_ge(S("ob_done"), c + 1)
                fn(o_b[:, :, c * CHUNK:(c + 1) * CHUNK], bank[5][:, 0:BH * CHUNK].rearrange("p (a b) -> p a b", a=BH),
                   ACT.Copy).then_inc(S("ob_stored"), 1)
            act.wait_ge(S("ob_stored"), 4)
            fn(obsq, o_b.rearrange("p a b -> p (a b)"), ACT.Square).then_inc(S("ob_squared"), 1)
            act.wait_ge(S("ob_summed"), 1)
            for j in range(2):
                last = fn(obsq[:, j * 512:(j + 1) * 512], bank[4 + j][:, :], ACT.Sqrt, bias=eps_t[:, 0:1], scale=1.0 / BHD)
            last.then_inc(S("ob_rooted"), 1)
            tile[0] = at["aa"]

            def moba_store(j):
                src, free = take()
                r = slice(AHD * (j % 2), AHD * (j % 2) + AHD)
                fn(o_a[r, j // 2, :], src[r, 0:SEQ], ACT.Copy).then_inc(free, 1)

            attention("moba", AH, p_a, [(0, P), (P, MOBA_W)], lambda i: stats[:, 64 + 8 * i:72 + 8 * i], pt_a, moba_store)

            shifted("n2", 3, lambda k: wait_stored(act, at["wout"] + k))

            act.wait_ge(S("group_diff"), 1)
            fn(router("g_exp"), router("g_diff"), ACT.Exp).then_inc(S("group_exp"), 1)
            act.wait_ge(S("top_diff"), 1)
            fn(router("t_exp"), router("t_diff"), ACT.Exp).then_inc(S("top_exp"), 1)
            for b in range(4):
                act.wait_ge(S("h_turned"), b // 2 + 1)
                fn(h_tok[:, b // 2, (b % 2) * 512:(b % 2 + 1) * 512], bank[b][:, :], ACT.Copy)\
                    .then_inc(S("h_tok_stored"), 1)

            def four(a, at):
                return a[:, at:at + 4, :].rearrange("p a b -> p (a b)")

            def out_halves(g):
                act.wait_ge(S("down_done"), g * 2 + 1)
                fn(four(e_out, 0), bank[2][:, :], ACT.Copy).then_inc(S("out_stored_a"), 1)

            def turned_halves(g):
                act.wait_ge(S("out_turned"), g + 1)
                fn(four(e_out_t, 0), bank[2][:, :], ACT.Copy).then_inc(S("turned_stored_a"), 1)

            act.wait_ge(S("rounds_ready"), 1)
            act_rounds = act.value_load(rounds_t[0:1, 0:1], min_val=1, max_val=SEQ // CAP)
            with act.Fori(0, act_rounds) as r:
                with act.Fori(0, PAIRS) as pair:
                    g = r * PAIRS + pair
                    out_halves(g)
                    act.wait_ge(S("gathered"), g * 2 + 1)
                    fn(four(e_in, 0), bank[0][:, :], ACT.Copy).then_inc(S("in_stored_a"), 1)
                    turned_halves(g)
                    act.wait_ge(S("gate_up_done"), g + 1)
                    fn(e_gate[:, :, :], bank[0][:, :].rearrange("p (a b c) -> p a b c", a=4, b=2)[:, :, 0, :],
                       ACT.Silu).then_inc(S("e_gate_ready"), 1)
            out_halves(act_rounds * PAIRS)
            turned_halves(act_rounds * PAIRS)
            norm("final2", lambda k: h[:, k, XC], DT, SEQ, D, lambda k: act.wait_ge(S("moe_added"), k + 1))

        @block.vector
        def _(dve):
            tt_, ts_, stt = nc.vector.tensor_tensor, nc.vector.tensor_scalar, nc.vector.scalar_tensor_tensor
            steps = [0]

            def link(ins):
                steps[0] += 1
                ins.then_inc(dve_step, 1)
                dve.wait_ge(dve_step, steps[0])

            def take(t):
                dve.wait_ge(tile_done, done(t))
                return bank[t % BANKS], evacuated[t % BANKS]

            def spread(a, n):
                return a.unsqueeze(1).to_broadcast([a.shape[0], n, a.shape[1]])

            def norm_scale(name, cols):
                dve.wait_ge(rooted, norm_no[name] + 1)
                if norm_no[name]:
                    dve.wait_ge(normed, norm_out[name])
                link(nc.vector.reciprocal(rstd[:, 0:cols], rms[:, 0:cols]))

            def norm_apply(src, dst, gain, K, cols):
                for k in range(K):
                    stt(dst(k), src(k), gain(k), cols, ALU.mult, ALU.mult).then_inc(normed, 1)

            nc.vector.memset(eps_t[:, 0:1], RMS_EPS)
            nc.vector.memset(eps_t[:, 2:3], 1.0)
            nc.vector.memset(zero_w[:, :], 0.0)
            nc.vector.memset(eps_t[:, 1:2], GN_EPS).then_inc(S("eps_set"), 1)
            dve.wait_ge(tab_loaded, 16)
            dve.wait_ge(vec_loaded, 16)
            nc.vector.memset(small[:, 8:12], 0.0).then_inc(S("mod_stored"), 1)
            nc.vector.memset(small[:, 12:16], 0.0).then_inc(S("mod_stored"), 1)
            with dve.Fori(0, MODS * DT // (2 * SLOTS)) as r:
                for b in range(2):
                    dve.wait_ge(S("mod_summed"), r * 2 + b + 1)
                    col = r * (2 * SLOTS) + b * SLOTS
                    tt_(mod[:, bass.ds(col, SLOTS)], bank[b][:, 0:SLOTS], vec[:, bass.ds(col + VEC["b_mod"], SLOTS)],
                        ALU.add).then_inc(S("mod_stored"), 1)
            dve.wait_ge(S("mod_stored"), 2 + MODS * DT // SLOTS)
            for part, gain in ((1, "n1"), (4, "n2")):
                a = mod[:, part * DT:(part + 1) * DT]
                stt(a, a, 1.0, V(gain, 0, DT), ALU.add, ALU.mult).then_inc(S("mod_ready"), 1)
            for a in range(AH):
                dve.wait_ge(S("bias_sum"), a + 1)
                nc.vector.tensor_copy(bias_w[:, a, :], bank[4 + a % 2][:, :]).then_inc(S("bias_row"), 1)
            norm_scale("mix0", T0)
            norm_apply(lambda k: h[:, k, :], lambda k: hn[:, k, :], lambda k: V("mix0", k), DT, rstd[:, :])
            for pair in range(2 * RH):
                t = at["qk"] + 2 * pair
                a, free = take(t)
                if pair:
                    dve.wait_ge(S("roped"), pair)
                tt_(rope_t[:, 0, :], a[:, 0:T0], C("cos_r", 0, T0), ALU.mult)
                tt_(rope_t[:, 1, :], a[:, 0:T0], C("sin_r", 0, T0), ALU.mult).then_inc(free, 1)
                a, free = take(t + 1)
                tt_(rope_t[:, 2, :], a[:, 0:T0], C("sin_r", 0, T0), ALU.mult)
                tt_(rope_t[:, 3, :], a[:, 0:T0], C("cos_r", 0, T0), ALU.mult).then_inc(free, 1)
                wait_stored(dve, t + 1)
                tt_(qk[:, 2 * pair, :], rope_t[:, 0, :], rope_t[:, 2, :], ALU.subtract)
                tt_(qk[:, 2 * pair + 1, :], rope_t[:, 1, :], rope_t[:, 3, :], ALU.add).then_inc(S("roped"), 1)

            def gn_centre(hh):
                dve.wait_ge(S("gn_mean"), hh + 1)
                a = o_r[:, 4 * hh:4 * hh + 4, :]
                stt(a, spread(bank[6][:, 0:T0], 4), -1.0 / RDV, a, ALU.mult, ALU.add).then_inc(S("gn_centred"), 1)

            def gn_apply(hh):
                dve.wait_ge(S("gn_root"), hh + 1)
                link(nc.vector.reciprocal(rstd[:, :], rms[:, :]))
                a = o_r[:, 4 * hh:4 * hh + 4, :]
                dve.wait_ge(S("gn_squared"), hh + 1)
                link(tt_(a, a, spread(rstd[:, :], 4), ALU.mult))
                for d in range(4):
                    t = 4 * hh + d
                    wait_stored(dve, at["gate", hh] + d)
                    stt(o_r[:, t, :], o_r[:, t, :], V("gn", t), gate_r[:, t, :], ALU.mult,
                        ALU.mult).then_inc(S("ret_out"), 1)

            for hh in range(RH):
                dve.wait_ge(S("ret_scored"), hh + 1)
                if hh >= 2:
                    dve.wait_ge(tile_done, done(at["av", hh - 2] + 3))
                col = TAB["decay"] + hh * SC_W
                tt_(sc_r[0:META, hh % 2, 0:T0], bank[4][0:META, 0:T0], tab[0:META, col:col + T0], ALU.mult)
                tt_(sc_r[:, hh % 2, T0:], bank[5][:, 0:SEQ + P], tab[:, col + T0:col + SC_W],
                    ALU.mult).then_inc(S("decayed"), 1)
                if hh:
                    gn_centre(hh - 1)
                    gn_apply(hh - 1)
            gn_centre(RH - 1)
            gn_apply(RH - 1)

            def add_tiles(first, cols, dst):
                for k in range(DT):
                    src, free = take(first + k)
                    tt_(dst(k), dst(k), src[:, 0:cols], ALU.add).then_inc(free, 1)

            add_tiles(at["wo0"], T0, lambda k: h[:, k, :])

            def feed_forward(layer, cols, src, dst):
                name = f"ffn{layer}"
                norm_scale(name, cols)
                norm_apply(src, dst, lambda k: V(name, k), DT, rstd[:, 0:cols])
                first = at[name]
                turns = 2 * FT // SLOTS

                def product(pair, turn=None):
                    t = first + 2 * pair + 1
                    more = lambda n, per: n if turn is None else turn * per + n
                    dve.wait_ge(tile_done, more(done(t), SLOTS))
                    dve.wait_ge(evacuated[(t - 1) % BANKS], more(freed(t - 1), SLOTS // BANKS))
                    dst = ff_act[:, pair, 0:cols] if turn is None else \
                        ff_act[:, bass.ds(turn * (SLOTS // 2) + pair, 1), 0:cols].rearrange("p a b -> p (a b)")
                    tt_(dst, ff_gate[:, pair % 2, 0:cols], bank[t % BANKS][:, 0:cols],
                        ALU.mult).then_inc(evacuated[t % BANKS], 1)

                with dve.Fori(0, turns) as r:
                    for j in range(SLOTS // 2):
                        product(j, r)
                for pair in range(turns * SLOTS // 2, FT):
                    product(pair)

            feed_forward(0, T0, lambda k: h[:, k, :], lambda k: hn[:, k, :])
            add_tiles(at["down0"], T0, lambda k: h[:, k, :])

            norm_scale("mix1", T0)
            norm_apply(lambda k: h[:, k, :], lambda k: kvn[:, k, :], lambda k: V("kv", k), DT, rstd[:, :])
            norm_apply(lambda k: h[:, k, :], lambda k: hn[:, k, :], lambda k: V("mix1", k), DT, rstd[:, :])

            def rotate(src, free, dst, c0, cols):
                c, s = C("cos_m", c0, cols), C("sin_m", c0, cols)
                tt_(mrope_t[:, 0, 0:cols], src[:, 0:cols], c, ALU.mult)
                for q in range(4):
                    of, to = slice(32 * q, 32 * q + 32), slice(32 * (q ^ 1), 32 * (q ^ 1) + 32)
                    last = tt_(mrope_t[to, 1, 0:cols], src[of, 0:cols], s[of], ALU.mult)
                last.then_inc(free[0], 1)
                dve.wait_ge(*free)
                tt_(dst, mrope_t[:, 0, 0:cols], mrope_t[:, 1, 0:cols], ALU.add).then_inc(S("q_roped"), 1)
                rotated[0] += 1
                dve.wait_ge(S("q_roped"), rotated[0])

            rotated = [0]

            def rotate_tile(t, dst, c0, cols):
                src, sem_free = take(t)
                rotate(src, (sem_free, freed(t)), dst, c0, cols)

            rotate_tile(at["kva"] + KVT, krope[:, 0, :], 0, T0)
            norm_scale("ckv", T0)
            norm_apply(lambda k: ckv[:, k, :], lambda k: ckv[:, k, :], lambda k: V("kva", k), KVT, rstd[:, :])
            norm_scale("cq", SEQ)
            norm_apply(lambda k: cq[:, k, :], lambda k: cq[:, k, :], lambda k: V("qa", k), QT, rstd[:, 0:SEQ])
            for t in range(4):
                rotate_tile(at["qr"] + t, qrope[:, t, :], META, SEQ)

            def attention(tag, heads, front, probs, parts, stat, turned=None):
                for i in range(heads + 1):
                    if i < heads:
                        dve.wait_ge(S(tag + "_scored"), i + 1)
                        if i >= 2:
                            dve.wait_ge(S(tag + "_turned"), i - 1)
                        link(front(i, bank[4 + i % 2], probs[:, i % 2, :]))
                        s = stat(i)
                        for j, (lo, hi) in enumerate(parts):
                            last = nc.vector.tensor_reduce(s[:, j:j + 1], probs[:, i % 2, lo:hi], AX, ALU.max)
                        link(last)
                        ts_(s[:, 2:4], s[:, 0:2], -1.0, None, ALU.mult).then_inc(S(tag + "_max"), 1)
                    if i >= 1:
                        j = i - 1
                        dve.wait_ge(S(tag + "_exp"), i)
                        s = stat(j)
                        link(nc.vector.reciprocal(s[:, 6:8], s[:, 4:6]))
                        for n, (lo, hi) in enumerate(parts):
                            a = probs[:, j % 2, lo:hi]
                            last = ts_(a, a, s[:, 6 + n:7 + n], None, ALU.mult)
                        last.then_inc(S(tag + "_p"), 1)
                        if turned:
                            turned(j)

            scale = (NOPE + ROPE) ** -0.5

            def mla_front(i, src, dst):
                return stt(dst, src[:, 0:MLA_W], scale, C("mask", 0, MLA_W), ALU.mult, ALU.add)

            def mla_turned(j):
                dve.wait_ge(S("mla_turnedm"), j + 1)
                if j:
                    dve.wait_ge(tile_done, done(at["am"] + j - 1))
                nc.vector.tensor_copy(pt_meta[0:META, 0, :], bank[7][0:META, 0:SEQ]).then_inc(S("mla_ptm"), 1)

            attention("mla", MH, mla_front, p_m, [(0, META + P), (META + P, MLA_W)],
                      lambda i: stats[:, 8 * i:8 * i + 8], mla_turned)
            add_tiles(at["wo1"], SEQ, lambda k: h[:, k, XC])
            feed_forward(1, SEQ, lambda k: h[:, k, XC], lambda k: hn[:, k, XC])
            add_tiles(at["down1"], SEQ, lambda k: h[:, k, XC])
            norm_scale("final", SEQ)
            norm_apply(lambda k: h[:, k, XC], lambda k: h[:, k, XC], lambda k: V("final", k), DT, rstd[:, 0:SEQ])

            norm_scale("n1", SEQ)
            norm_apply(lambda k: h[:, k, XC], lambda k: hn[:, k, 0:SEQ],
                       lambda k: mod[:, DT + k:DT + k + 1], DT, rstd[:, 0:SEQ])
            nc.vector.memset(raw_b[:, :, 0:CONV - 1], 0.0)
            dve.wait_ge(S("ba_done"), 1)
            ba = bank[4][:, 0:16].rearrange("p (t c) -> p t c", t=2)
            two = lambda a: a.rearrange("p (t c) -> p t c", t=2)
            nc.vector.tensor_copy(two(M("b", 0, 8)), ba[:, :, 0:BH])
            link(tt_(two(M("a", 0, 8)), ba[:, :, BH:2 * BH], two(V("dt", 0, 8)), ALU.add))
            stt(M("abs", 0, 8), M("a", 0, 8), -1.0, M("a", 0, 8), ALU.mult, ALU.max).then_inc(S("ba_split"), 1)
            dve.wait_ge(S("beta_ready"), 1)
            dve.wait_ge(S("softplus_ln"), 1)
            link(stt(M("sp", 0, 8), M("a", 0, 8), 0.0, M("sp", 0, 8), ALU.max, ALU.add))
            stt(M("g", 0, 8), M("sp", 0, 8), -1.0, M("ea", 0, 8), ALU.mult, ALU.mult).then_inc(S("g_ready"), 1)
            dve.wait_ge(S("g_summed"), 1)
            link(nc.vector.tensor_copy(M("G", 0, 8), bank[5][:, 0:8]))
            tt_(M("R", 0, 8), bank[5][:, 8:16], M("G", 0, 8), ALU.subtract)
            nc.vector.tensor_copy(M("H", 0, 16), bank[5][:, 16:32]).then_inc(S("g_stored"), 1)
            dve.wait_ge(S("g_exp"), 1)
            link(tt_(M("bg", 0, 8), M("beta", 0, 8), M("eG", 0, 8), ALU.mult))
            dve.wait_ge(S("exp_rows"), 1)
            for p in range(NP):
                last = ts_(decT[:, p, :], bank[6 + p // 4][:, (p % 4) * P:(p % 4 + 1) * P], M("G", G_COL[p]), 0.0,
                           ALU.subtract, ALU.min)
            last.then_inc(S("dec_diff"), 1)
            dve.wait_ge(S("dec_exp"), 1)
            link(tt_(decT[:, :, :], decT[:, :, :], spread(C("upto"), NP), ALU.mult))
            dve.wait_ge(S("row_beta"), 1)

            def half(a, j):
                return a[:, 4 * j:4 * j + 4, :]

            def psum(b):
                return bank[b][:, :].rearrange("p (a b) -> p a b", a=4)

            for j in range(2):
                last = tt_(half(LT, j), half(decT, j), psum(4 + j), ALU.mult)
            last.then_inc(S("beta_rows"), 1)
            for t0 in range(0, 12, 4):
                for j in range(CONV):
                    for t in range(t0, t0 + 4):
                        if j == 0:
                            wait_stored(dve, at["qkvb"] + t)
                        x, w = raw_b[:, t, j:j + SEQ], V("conv", t * CONV + j)
                        if j == 0:
                            last = ts_(cb[:, t, :], x, w, None, ALU.mult)
                        else:
                            last = stt(cb[:, t, :], x, w, cb[:, t, :], ALU.mult, ALU.add)
                            if j == CONV - 1:
                                last.then_inc(S("conv_done"), 1)
                    if j < CONV - 1:
                        link(last)
            dve.wait_ge(S("l2_root"), 1)
            link(nc.vector.reciprocal(l2sq, l2sq))
            flat = cb.rearrange("p a b -> p (a b)")
            stt(flat[:, 0:BH * SEQ], flat[:, 0:BH * SEQ], BHD ** -0.5, l2sq[:, 0:BH * SEQ], ALU.mult, ALU.mult)
            tt_(flat[:, BH * SEQ:2 * BH * SEQ], flat[:, BH * SEQ:2 * BH * SEQ], l2sq[:, BH * SEQ:], ALU.mult)\
                .then_inc(S("l2_done"), 1)
            dve.wait_ge(S("gram_done"), 1)
            for j in range(2):
                last = tt_(half(LT, j), half(LT, j), psum(4 + j), ALU.mult)
            last.then_inc(S("lt_ready"), 1)
            dve.wait_ge(S("qk_done"), 1)
            for j in range(2):
                last = tt_(half(PT, j), half(decT, j), psum(6 + j), ALU.mult)
            last.then_inc(S("pt_ready"), 1)
            tt_(qg, qg, TM[:, :, :], ALU.mult)
            dve.wait_ge(S("k_turned"), 1)
            dve.wait_ge(S("v_turned"), 1)
            dve.wait_ge(S("conv_silu"), 12)
            for dst, first, name in ((k_tok, 4, "bg"), (kd, 4, "eR"), (v_tok, 6, "beta")):
                per = M(name, 0, 8).rearrange("p (t a) -> p a t", t=2)
                for j in range(2):
                    last = tt_(half(dst, j).rearrange("p (a t) b -> p a t b", t=2),
                               psum(first + j).rearrange("p (a t) b -> p a t b", t=2),
                               per[:, 2 * j:2 * j + 2, :].unsqueeze(3).to_broadcast([P, 2, 2, P]), ALU.mult)
            last.then_inc(S("tok_ready"), 1)

            def level(lv):
                tt_(ML[:, :, :], LT[:, :, :], spread(C("level", lv * P), NP), ALU.mult).then_inc(S("ml_ready"), 1)

            dve.wait_ge(S("lt_ready"), 1)
            level(0)
            for lv in range(6):
                dve.wait_ge(S("mx_done"), lv + 1)
                if lv == 0:
                    dve.wait_ge(S("ml_ready"), 1)
                    tt_(Y[:, :, :], spread(ident, NP), ML[:, :, :], ALU.subtract)
                    for j in range(2):
                        last = tt_(half(X, j), spread(ident, 4), psum(4 + j), ALU.subtract)
                    last.then_inc(S("inv_ready"), 1)
                    dve.wait_ge(S("inv_ready"), 1)
                    level(1)
                    continue
                if lv < 5:
                    level(lv + 1)
                dve.wait_ge(S("dy_done"), lv)
                if lv < 5:
                    dve.wait_ge(S("dx_done"), lv)
                for j in range(2):
                    last = tt_(half(Y, j), half(Y, j), psum(6 + j), ALU.subtract)
                if lv < 5:
                    for j in range(2):
                        last = tt_(half(X, j), half(X, j), psum(4 + j), ALU.subtract)
                last.then_inc(S("inv_ready"), 1)
            dve.wait_ge(S("u_stored"), 1)
            for c in range(4):
                R, tt = CHUNK * (c % 2), c // 2
                rows = slice(R, R + CHUNK)
                u = u_tok.rearrange("p (a t) b -> p a t b", t=2)[rows, :, tt, :]
                if c == 0:
                    nc.vector.tensor_copy(vn[rows], u).then_inc(S("vn_ready"), 1)
                else:
                    dve.wait_ge(S("ws_done"), c)
                    tt_(vn[rows], u, psum(4)[rows], ALU.subtract).then_inc(S("vn_ready"), 1)
                if c == 3:
                    break
                dve.wait_ge(S("ds_done"), c + 1)
                if c == 0:
                    nc.vector.tensor_copy(st, psum(6)).then_inc(S("state_ready"), 1)
                    continue
                for a in range(BH):
                    last = stt(st[:, a, :], st[:, a, :], M("eH", 8 * (c % 2) + tt * BH + a), psum(6)[:, a, :],
                               ALU.mult, ALU.add)
                last.then_inc(S("state_ready"), 1)
            dve.wait_ge(S("ob_rooted"), 1)
            ob = o_b.rearrange("p a b -> p (a b)")
            link(nc.vector.reciprocal(obsq, obsq))
            link(tt_(ob, ob, obsq, ALU.mult))
            wait_stored(dve, at["z"] + BH - 1)
            stt(ob, z_b.rearrange("p a b -> p (a b)"), V("onorm"), ob, ALU.mult, ALU.mult).then_inc(S("ob_ready"), 1)

            dve.wait_ge(S("bias_loaded"), 16 * 2 * AH)

            def moba_front(i, src, dst):
                return stt(dst, src[:, 0:MOBA_W], AHD ** -0.5, bias_a[:, i, :], ALU.mult, ALU.add)

            attention("moba", AH, moba_front, p_a, [(0, P), (P, MOBA_W)], lambda i: stats[:, 64 + 8 * i:72 + 8 * i])
            for k in range(DT):
                t = at["up"] + 2 * k
                src, free = take(t)
                if k == 0:
                    wait_stored(dve, at["gates"] + 15)
                else:
                    dve.wait_ge(S("m_ready"), k)
                tt_(up_t[:, 0, :], gates[:, k, :], src[:, 0:SEQ], ALU.mult).then_inc(free, 1)
                src, free = take(t + 1)
                tt_(up_t[:, 1, :], gates[:, DT + k, :], src[:, 0:SEQ], ALU.mult).then_inc(free, 1)
                wait_stored(dve, t + 1)
                tt_(m_up[:, k, :], up_t[:, 0, :], up_t[:, 1, :], ALU.add).then_inc(S("m_ready"), 1)
            for k in range(DT):
                src, free = take(at["wout"] + k)
                stt(h[:, k, XC], src[:, 0:SEQ], mod[:, 2 * DT + k:2 * DT + k + 1], h[:, k, XC],
                    ALU.mult, ALU.add).then_inc(free, 1)
            norm_scale("n2", SEQ)
            norm_apply(lambda k: h[:, k, XC], lambda k: hn[:, k, 0:SEQ],
                       lambda k: mod[:, 4 * DT + k:4 * DT + k + 1], DT, rstd[:, 0:SEQ])

            dve.wait_ge(S("logits_done"), 1)
            red = nc.vector.tensor_reduce

            def per_token(a, n):
                return a.unsqueeze(2).to_broadcast([P, 2, n])

            def first_of_max(values, n, top, hit, first, one, shape):
                link(red(router(top), values, AX, ALU.max))
                link(tt_(shape(hit), values, per_token(router(top), n), ALU.is_equal))
                iota = C("iota", 0, 16).rearrange("p (a b) -> p a b", a=2)[:, :, 0:n]
                link(stt(shape(hit), shape(hit), -64.0, iota, ALU.mult, ALU.add))
                link(red(router(first), shape(hit), AX, ALU.min))
                link(tt_(shape(one), shape(hit), per_token(router(first), n), ALU.is_equal))

            lg = router("logits", 2)
            link(tt_(lg, bank[4][:, 0:72].rearrange("p (a b) -> p a b", a=2),
                     V("b36", 0, 72).rearrange("p (a b) -> p a b", a=2), ALU.add))
            first_of_max(lg[:, :, 0:NG], NG, "gmax", "g_hit", "g_first", "g_one", lambda a: router(a, 2))
            tt_(router("g_diff", 2), lg[:, :, 0:NG], per_token(router("gmax"), NG), ALU.subtract)\
                .then_inc(S("group_diff"), 1)
            for tt in range(2):
                prod = router("prod")[:, tt * 32:tt * 32 + 32].rearrange("p (g e) -> p g e", g=NG)
                last = tt_(prod, lg[:, tt, NG:].rearrange("p (g e) -> p g e", g=NG),
                           router("g_one", 2)[:, tt, :].unsqueeze(2).to_broadcast([P, NG, EPG]), ALU.mult)
            link(last)
            for tt in range(2):
                prod = router("prod")[:, tt * 32:tt * 32 + 32].rearrange("p (g e) -> p e g", g=NG)
                last = red(router("le", 2)[:, tt, :], prod, AX, ALU.add)
            link(last)
            first_of_max(router("le", 2), EPG, "m1", "hit1", "first1", "one1", lambda a: router(a, 2))
            link(stt(router("le2"), router("one1"), NEG, router("le"), ALU.mult, ALU.add))
            first_of_max(router("le2", 2), EPG, "m2", "hit2", "first2", "one2", lambda a: router(a, 2))
            tt_(router("t_diff"), router("m2"), router("m1"), ALU.subtract).then_inc(S("top_diff"), 1)
            dve.wait_ge(S("group_exp"), 1)
            link(red(router("g_sum"), router("g_exp", 2), AX, ALU.add))
            nc.vector.reciprocal(router("g_top"), router("g_sum"))
            dve.wait_ge(S("top_exp"), 1)
            link(ts_(router("t_sum"), router("t_exp"), 1.0, None, ALU.add))
            link(nc.vector.reciprocal(router("t_sum"), router("t_sum")))
            link(tt_(router("w1"), router("t_sum"), router("g_top"), ALU.mult))
            link(tt_(router("w2"), router("w1"), router("t_exp"), ALU.mult))
            tt_(router("hit1", 2), router("one1", 2), per_token(router("w1"), EPG), ALU.mult)
            link(tt_(router("hit2", 2), router("one2", 2), per_token(router("w2"), EPG), ALU.mult))
            tt_(router("hit"), router("one1"), router("one2"), ALU.add)
            link(tt_(router("ce"), router("hit1"), router("hit2"), ALU.add))
            for tt in range(2):
                last = tt_(comb[:, tt, :].rearrange("p (g e) -> p g e", g=NG),
                           router("ce", 2)[:, tt, :].unsqueeze(1).to_broadcast([P, NG, EPG]),
                           router("g_one", 2)[:, tt, :].unsqueeze(2).to_broadcast([P, NG, EPG]), ALU.mult)
            for tt in range(2):
                last = tt_(router("used", 2)[:, tt, :].rearrange("p (g e) -> p g e", g=NG),
                           router("hit", 2)[:, tt, :].unsqueeze(1).to_broadcast([P, NG, EPG]),
                           router("g_one", 2)[:, tt, :].unsqueeze(2).to_broadcast([P, NG, EPG]), ALU.mult)
            last.then_inc(S("used_ready"), 1)
            dve.wait_ge(S("used_ready"), 1)
            dve.wait_ge(S("ranked"), 1)
            link(stt(router("rank"), bank[4][:, 0:2 * NE], FAR, router("used"), ALU.add, ALU.mult))
            ts_(router("rank"), router("rank"), FAR, None, ALU.subtract)
            link(red(router("most"), bank[4][:, 2 * NE:3 * NE], AX, ALU.max))
            link(ts_(router("over"), router("most"), float(CAP), 1.0, ALU.is_gt, ALU.add))
            for n in range(2, SEQ // CAP - 1):
                link(stt(router("over"), router("most"), float(n * CAP), router("over"), ALU.is_gt, ALU.add))
            nc.vector.memset(e_act[:, :, :], 0.0).then_inc(S("e_act_ready"), 1)
            nc.vector.memset(sel_t[:, :, :], 0.0).then_inc(S("sel_t_stored"), 1)
            stt(rounds_t[:, :], router("most"), float((SEQ // CAP - 1) * CAP), router("over"), ALU.is_gt,
                ALU.add).then_inc(S("rounds_ready"), 1)
            dve.wait_ge(S("rounds_ready"), 1)

            def four(a, at):
                return a[:, at:at + 4, :].rearrange("p a b -> p (a b)")

            def out_halves(g):
                dve.wait_ge(S("down_done"), g * 2 + 2)
                nc.vector.tensor_copy(four(e_out, 4), bank[3][:, :]).then_inc(S("out_stored_v"), 1)

            def turned_halves(g):
                dve.wait_ge(S("out_turned"), g + 1)
                nc.vector.tensor_copy(four(e_out_t, 4), bank[3][:, :]).then_inc(S("turned_stored_v"), 1)

            dve_rounds = dve.value_load(rounds_t[0:1, 0:1], min_val=1, max_val=SEQ // CAP)
            with dve.Fori(0, dve_rounds) as r:
                with dve.Fori(0, PAIRS) as pair:
                    g = r * PAIRS + pair
                    dve.wait_ge(S("sel_t_stored"), g + 1)
                    for tt in range(2):
                        for j in range(2):
                            col = pair * 2 + (tt * NE + j)
                            rank = rt[:, bass.ds(col + RT["rank"][0], 1)]
                            share = rt[:, bass.ds(col + RT["comb"][0], 1)]
                            out_cols = slice(j * CAP, (j + 1) * CAP)
                            ts_(sel[:, tt, out_cols], C("slot", 0, CAP), rank, None, ALU.is_equal)
                            last = ts_(sel_w[:, tt, out_cols], C("slot", 0, CAP), rank, share, ALU.is_equal, ALU.mult)
                    last.then_inc(S("sel_ready"), 1)
                    out_halves(g)
                    dve.wait_ge(S("gathered"), g * 2 + 2)
                    nc.vector.tensor_copy(four(e_in, 4), bank[1][:, :]).then_inc(S("in_stored_v"), 1)
                    turned_halves(g)
                    dve.wait_ge(S("e_gate_ready"), g + 1)
                    tt_(e_act[:, :, :], e_gate[:, :, :],
                        bank[0][:, :].rearrange("p (a b c) -> p a b c", a=4, b=2)[:, :, 1, :], ALU.mult)\
                        .then_inc(S("e_act_ready"), 1)
                    dve.wait_ge(S("sel_turned"), g + 1)
                    nc.vector.tensor_copy(sel_t[:, 0, :], bank[1][:, 0:SEQ]).then_inc(S("sel_t_stored"), 1)
                dve.wait_ge(S("sel_ready"), r * PAIRS + PAIRS)
                link_in_loop = ts_(router("rank"), router("rank"), float(CAP), None, ALU.subtract)
                link_in_loop.then_inc(S("rank_shifted"), 1)
                dve.wait_ge(S("rank_shifted"), r + 1)
            out_halves(dve_rounds * PAIRS)
            turned_halves(dve_rounds * PAIRS)
            dve.wait_ge(S("moe_done"), 1)
            for k in range(DT):
                stt(h[:, k, XC], bank[4 + k // 2][:, (k % 2) * SEQ:(k % 2 + 1) * SEQ],
                    mod[:, 5 * DT + k:5 * DT + k + 1], h[:, k, XC], ALU.mult, ALU.add).then_inc(S("moe_added"), 1)
            norm_scale("final2", SEQ)
            norm_apply(lambda k: h[:, k, XC], lambda k: hn[:, k, 0:SEQ], lambda k: V("final2", k), DT, rstd[:, 0:SEQ])


def kernel(**inputs):
    import concourse.bacc as bacc
    from concourse.bass_utils import run_bass_kernel_spmd

    i = {name: np.asarray(a) for name, a in inputs.items()}
    tokens = np.concatenate([i["meta"], i["x"][0]], axis=0)
    arrays = {
        "weights": weight_stream(i),
        "vectors": np.ascontiguousarray(vectors(i)),
        "tables": constants(),
        "tokens": np.ascontiguousarray(tokens.T.reshape(DT, P, T0).transpose(1, 0, 2)),
        "rel_bias": np.ascontiguousarray(i["rel_bias_2"]),
    }
    nc = bacc.Bacc("TRN2", target_bir_lowering=False, num_devices=1)
    args = [nc.dram_tensor(name, a.shape, F32, kind="ExternalInput").ap() for name, a in arrays.items()]
    skew = nc.dram_tensor("skew", (AH, P, 512), F32, kind="Internal").ap()
    out = nc.dram_tensor("out", (P, DT, SEQ), F32, kind="ExternalOutput").ap()
    build(nc, *args, skew, out)
    r = run_bass_kernel_spmd(nc, [arrays], core_ids=[0])
    got = np.asarray(r.results[0]["out"])
    return np.ascontiguousarray(got.transpose(2, 1, 0).reshape(1, SEQ, D))
```

```python
from contextlib import ExitStack

import numpy as np

import concourse.bass as bass
from concourse import mybir

F32 = mybir.dt.float32
F32R = mybir.dt.float32r
ALU = mybir.AluOpType
ACT = mybir.ActivationFunctionType
AX = mybir.AxisListType.X

P = 128
D = 1024
DT = D // P
META, SEQ = 16, 256
T0 = META + SEQ
TOK = [(0, META), (META, META + P), (META + P, T0)]
PAD = P - META
CHUNK = 64
RMS_EPS, GN_EPS = 1e-6, 1e-5
NEG = -1e30

RH, RDK, RDV = 4, 256, 512
MH, NOPE, ROPE = 8, 128, 64
QR, KVR = 768, 512
QT, KVT = QR // P, KVR // P
FF = 2816
FT = FF // P
AH, AHD = 8, 64
BH, BHD = 4, 128
CONV = 4
NG, EPG, EF = 4, 8, 256
NE = NG * EPG
BUCKETS = 32
CAP = 64
PAIRS = NE // 2
FAR = 1000.0
MODS = 6
MOD_GROUPS = 3

UB = 8
UNIT = UB * P
SLOTS = 12
BANKS = 4

VEC = {}
_at = 0
for _name, _n in [("c", DT), ("b_mod", MODS * DT), ("mix0", DT), ("ffn0", DT), ("gn", 16), ("kv", DT), ("mix1", DT),
                  ("kva", KVT), ("qa", QT), ("ffn1", DT), ("final", DT), ("n1", DT), ("n2", DT), ("final2", DT),
                  ("onorm", 1), ("conv", 12 * CONV), ("alog", 2 * BH), ("dt", 2 * BH), ("b36", 2 * 36),
                  ("wba", DT * 8), ("w36", DT * 36)]:
    VEC[_name] = _at
    _at += _n
NVEC = _at

TAB = {}
_at = 0
SC_W = T0 + SEQ + P
MLA_W = (META + P) + T0
MOBA_W = P + SEQ
for _name, _n in [("cos_r", T0), ("sin_r", T0), ("decay", RH * SC_W), ("cos_m", T0), ("sin_m", T0), ("mask", MLA_W),
                  ("ident", P), ("ones", P), ("upto", P), ("chunk", P), ("half0", P), ("half1", P),
                  ("level", 6 * P), ("bucket", 512), ("iota", 2 * 8), ("before", P), ("slot", CAP)]:
    TAB[_name] = _at
    _at += _n
NTAB = _at

UNITS = (MODS * D * D + D * (2 * RH * RDK + 2 * RH * RDV) + RH * RDV * D + D * (KVR + P) + D * QR + KVR * MH * 256
         + QR * MH * (NOPE + ROPE) + D * D + 2 * 3 * D * FF
         + D * (3 * 512 + 3 * 512 + 512 + 2 * D) + 2 * 512 * D + D * D + NE * 3 * D * EF) // (P * UNIT)

SPLITS = 4
FFN_UNITS = 3 * D * FF // (P * UNIT)
FFN_FIRST = [(MODS * D * D + D * (2 * RH * RDK + 2 * RH * RDV) + RH * RDV * D) // (P * UNIT)]
FFN_FIRST.append(FFN_FIRST[0] + FFN_UNITS + (D * (KVR + P) + D * QR + KVR * MH * 256 + QR * MH * (NOPE + ROPE)
                                             + D * D) // (P * UNIT))

PAIR_UNITS = 2 * 3 * D * EF // (P * UNIT)
GATE_UP_UNITS = 2 * PAIR_UNITS // 3
EXPERTS_FIRST = UNITS - PAIRS * PAIR_UNITS
AHEAD = SPLITS - 1
assert PAIR_UNITS == SLOTS


def constants():
    f = np.float32
    tab = np.zeros((P, NTAB), f)

    def put(name, a, rows=P):
        tab[:rows, TAB[name]:TAB[name] + a.shape[1]] = a

    def rope(dim):
        inv = f(1.0) / (f(10000.0) ** (np.arange(0, dim, 2, dtype=f) / f(dim)))
        ang = (np.arange(T0, dtype=f)[None, :] * inv[:, None].astype(f)).astype(f).astype(np.float64)
        return np.cos(ang).astype(f), np.sin(ang).astype(f)

    c, s = rope(RDK)
    put("cos_r", c)
    put("sin_r", s)
    c, s = rope(ROPE)
    put("cos_m", np.concatenate([c] * 4))
    put("sin_m", np.concatenate([s, -s, s, -s]))
    pos = np.arange(T0) + PAD
    seen = (pos[:, None] // CHUNK) <= (pos[None, :] // CHUNK)
    for h in range(RH):
        log_g = np.log1p(-np.exp2(-5.0 - h))
        m = np.where(seen, np.exp(log_g * np.abs(pos[:, None] - pos[None, :])), 0.0) * RDK ** -0.5
        at = TAB["decay"] + h * SC_W
        for lo, hi in TOK:
            tab[:hi - lo, at:at + T0 - lo] = m[lo:hi, lo:]
            at += T0 - lo
    m = np.where(seen.T, 0.0, NEG)
    put("mask", np.concatenate([m[META:META + P, :META + P], m[META + P:, :]], axis=1))
    i = np.arange(P)
    same = (i[:, None] // CHUNK) == (i[None, :] // CHUNK)
    put("ident", np.eye(P))
    put("ones", np.ones((P, P)))
    put("upto", same & (i[:, None] <= i[None, :]))
    put("chunk", same)
    put("half0", np.broadcast_to(i[:, None] < CHUNK, (P, P)))
    put("half1", np.broadcast_to(i[:, None] >= CHUNK, (P, P)))
    lv = [((i[None, :] >> n) & 1 == 1) & ((i[:, None] >> n) == (i[None, :] >> n) - 1) for n in range(6)]
    put("level", np.concatenate(lv, axis=1))
    d = 255 - np.arange(512)
    n = np.maximum(d, 0)
    large = 16 + (np.log(np.maximum(n, 1).astype(f) / f(16)) / f(np.log(8.0)) * f(16)).astype(np.int32)
    b = np.where(n < 16, n, np.minimum(large, BUCKETS - 1))
    b = np.where(d < 0, BUCKETS, b)
    put("bucket", np.arange(BUCKETS + 1)[:, None] == b[None, :], BUCKETS + 1)
    put("iota", np.broadcast_to(np.tile(np.arange(8), 2), (P, 16)))
    put("before", i[:, None] < i[None, :])
    put("slot", np.broadcast_to(np.arange(CAP), (P, CAP)))
    return tab


def narrow_units(w):
    k, f = w.shape
    b = w.reshape(k // P, P, f // P, P).transpose(2, 0, 1, 3).reshape(-1, UB, P, P)
    return b.transpose(0, 2, 1, 3).reshape(-1, P, UNIT)


def wide_units(w):
    k, f = w.shape
    b = w.reshape(k // P, P, f // 512, 512).transpose(2, 0, 1, 3).reshape(-1, UB // 4, P, 512)
    return b.transpose(0, 2, 1, 3).reshape(-1, P, UNIT)


def pair_units(a, b):
    k, f = a.shape
    both = np.stack([a.reshape(k, f // P, P), b.reshape(k, f // P, P)], axis=2)
    return narrow_units(both.reshape(k, 2 * f))


def weight_stream(i):
    r = i["ret_w_in"][0]
    qk = [r[:, base + h * RDK:base + (h + 1) * RDK] for h in range(RH) for base in (0, RH * RDK)]
    kva = i["mla_w_kv_a"]
    kvb = i["mla_w_kv_b"].reshape(KVR, MH, 2, P)
    qb = i["mla_w_q_b"][0].reshape(QR, MH, NOPE + ROPE)
    w = i["w_in_2"][0]
    out = [wide_units(i["w_mod_2"][0]), narrow_units(np.concatenate(qk, axis=1)), wide_units(r[:, 2048:4096]),
           narrow_units(r[:, 4096:]), narrow_units(i["ret_w_o"][0]),
           pair_units(i["ffn_w1"][0], i["ffn_w3"][0]), narrow_units(i["ffn_w2"][0]),
           narrow_units(np.concatenate([kva, kva[:, KVR:]], axis=1)), narrow_units(i["mla_w_q_a"][0]),
           narrow_units(kvb[:, :, 0].reshape(KVR, D)), wide_units(kvb[:, :, 1].reshape(KVR, D)),
           narrow_units(qb[:, :, :NOPE].reshape(QR, D)), narrow_units(qb[:, :, NOPE:].reshape(QR, MH * ROPE)),
           narrow_units(i["mla_w_o"][0]),
           pair_units(i["ffn_w1"][1], i["ffn_w3"][1]), narrow_units(i["ffn_w2"][1]),
           narrow_units(w[:, 1536:3072]), narrow_units(w[:, :1024]), wide_units(w[:, 1024:1536]),
           narrow_units(w[:, 3072:3584]), narrow_units(w[:, 3592:])]
    out.append(narrow_units(np.concatenate([i["w_up_a_2"][0].reshape(512, DT, P), i["w_up_b_2"][0].reshape(512, DT, P)],
                                           axis=0).reshape(D, D)))
    out.append(narrow_units(i["w_out_2"][0]))
    gate, up = i["w_e_gate_2"][0].reshape(NE, D, EF), i["w_e_up_2"][0].reshape(NE, D, EF)
    down = i["w_e_down_2"][0].reshape(NE, EF, D)
    for e in range(0, NE, 2):
        out += [wide_units(np.concatenate([gate[e + j], up[e + j]], axis=1)) for j in range(2)]
        both = down[e:e + 2].reshape(2, 2, P, 2, 512).transpose(3, 0, 1, 2, 4).reshape(-1, 2, P, 512)
        out.append(both.transpose(0, 2, 1, 3).reshape(-1, P, UNIT))
    return np.concatenate(out, axis=0)


def vectors(i):
    cols = lambda a: np.asarray(a).reshape(-1, P).T
    rep = lambda a: np.broadcast_to(np.asarray(a).reshape(1, -1), (P, np.asarray(a).size))
    conv = i["conv_w_2"][0].reshape(CONV, 12, P).transpose(2, 1, 0).reshape(P, 12 * CONV)
    rows = lambda w: w.reshape(DT, P, -1).transpose(1, 0, 2).reshape(P, -1)
    w36 = np.concatenate([i["w_rg_2"][0], i["w_re_2"][0]], axis=1)
    b36 = np.concatenate([i["b_rg_2"][0], i["b_re_2"][0]])
    parts = [cols(i["c_2"]), cols(i["b_mod_2"][0]), cols(i["norm_mix_g"][0]), cols(i["norm_ffn_g"][0]),
             cols(i["ret_gn_g"][0]), cols(i["mla_norm_kv_g"]), cols(i["norm_mix_g"][1]), cols(i["mla_kv_a_norm_g"]),
             cols(i["mla_q_a_norm_g"][0]), cols(i["norm_ffn_g"][1]), cols(i["final_g"]), cols(i["norm1_w_2"][0]),
             cols(i["norm2_w_2"][0]), cols(i["final_norm_w_2"]), cols(i["onorm_w_2"][0]), conv,
             rep(np.tile(i["a_log_2"][0], 2)), rep(np.tile(i["dt_bias_2"][0], 2)), rep(np.tile(b36, 2)),
             rows(i["w_in_2"][0][:, 3584:3592]), rows(w36)]
    return np.concatenate(parts, axis=1)


def build(nc, weights, vectors_in, tables_in, tokens_in, rel_bias, skew, out):
    with ExitStack() as ctx:
        def sb(name, *shape):
            return ctx.enter_context(nc.sbuf_tensor(name, list(shape), F32))

        def sem(name):
            return ctx.enter_context(nc.semaphore(name))

        ring = sb("ring", P, SLOTS, UNIT)
        vec = sb("vec", P, NVEC)
        tab = sb("tab", P, NTAB)
        h = sb("h", P, DT, T0)
        sq = sb("sq", P, DT, T0)
        rms = sb("rms", P, T0)
        rstd = sb("rstd", P, T0)
        mod = sb("mod", P, MODS * DT)
        relb = sb("relb", P, AH)
        small = sb("small", P, 160)
        stats = sb("stats", P, 8 * (MH + AH))
        eps_t = sb("eps_t", P, 4)
        zero_w = sb("zero_w", P, P)
        rt = sb("rt", P, 640)
        rounds_t = ctx.enter_context(nc.sbuf_tensor("rounds_t", [P, 1], mybir.dt.int32))
        with ExitStack() as twins:
            hn = twins.enter_context(nc.sbuf_tensor("hn", [P, DT, T0], F32))
            arena = twins.enter_context(nc.sbuf_tensor("arena", [P, 23400], F32))
        hn_lo = ctx.enter_context(nc.sbuf_tensor("hn_low", [P, DT, T0], F32R))
        arena_r = ctx.enter_context(nc.sbuf_tensor("arena_r", [P, 23400], F32R))

        cursor = [0]

        def carve_r(*shape, at=None):
            return carve(*shape, at=at, arena=arena_r)

        def carve(*shape, at=None, arena=arena):
            if at is not None:
                cursor[0] = at
            n = int(np.prod(shape))
            a = arena[:, cursor[0]:cursor[0] + n]
            cursor[0] += n
            assert cursor[0] <= 23400, cursor[0]
            if len(shape) == 2:
                a = a.rearrange("p (a b) -> p a b", a=shape[0])
            return a

        qk = carve(4 * RH, T0, at=0)
        gate_r = carve(4 * RH, T0)
        o_r = carve(4 * RH, T0)
        sc_r = carve(2, SC_W)
        rope_t = carve(4, T0)
        v_r = carve(3, RH * RDV)
        ff_hi = carve_r(FT, T0, at=0)
        ff_lo = carve_r(FT, T0)
        ff_gate = carve(2, T0)
        hn_hi = carve_r(DT, T0)
        assert cursor[0] <= 23400 - 2 * SPLITS * UNIT
        w_hi = carve_r(SPLITS, UNIT, at=23400 - 2 * SPLITS * UNIT)
        w_lo = carve_r(SPLITS, UNIT)
        o_m = carve(MH, SEQ, at=0)
        ckv = carve(KVT, T0)
        kvn = carve(DT, T0)
        krope = carve(1, T0)
        k_m = carve(MH, T0)
        v_m = carve(3, MH * P)
        cq = carve(QT, SEQ)
        q_m = carve(MH, SEQ)
        qrope = carve(4, SEQ)
        mrope_t = carve(2, T0)
        p_m = carve(2, MLA_W)
        pt_m = carve(1, 3 * P)
        pt_meta = carve(1, SEQ)
        raw_b = carve(12, SEQ + CONV - 1, at=0)
        cb = carve(12, SEQ)
        q_a = carve(8, SEQ)
        v_a = carve(2, 512)
        z_b = carve(BH, SEQ)
        gates = carve(16, SEQ)
        o_b = carve(BH, SEQ)
        delta_at = cursor[0]
        NP = 2 * BH
        LT = carve(NP, P)
        X = carve(NP, P)
        Y = carve(NP, P)
        TM = carve(NP, P)
        PT = carve(NP, P)
        decT = carve(NP, P)
        ML = carve(NP, P)

        def problems(a):
            return a.rearrange("p a (t b) -> p (a t) b", t=2)

        qg = problems(cb[:, 0:BH, :])
        k_tok = problems(cb[:, BH:2 * BH, :])
        kd = problems(cb[:, 2 * BH:3 * BH, :])
        wT = k_tok
        raw_flat = raw_b.rearrange("p a b -> p (a b)")
        v_tok = raw_flat[:, 0:NP * P].rearrange("p (a b) -> p a b", a=NP)
        u_tok = raw_flat[:, NP * P:2 * NP * P].rearrange("p (a b) -> p a b", a=NP)
        st = decT[:, 0:BH, :]
        vn = decT[:, BH:2 * BH, :]
        sq_flat = sq[:, :, :].rearrange("p a b -> p (a b)")
        l2sq = sq_flat[:, 0:8 * SEQ]
        obsq = sq_flat[:, 0:BH * SEQ]
        bias_a = tab[:, 0:AH * MOBA_W].rearrange("p (a b) -> p a b", a=AH)
        bias_w = v_r.rearrange("p a b -> p (a b)")[0:AH, 0:512]
        o_a = carve(4, SEQ, at=delta_at)
        p_a = carve(2, MOBA_W)
        pt_a = carve(1, 3 * P)
        m_up = carve(DT, SEQ)
        up_t = carve(2, SEQ)
        mod_diag = hn[:, :, :].rearrange("p a b -> p (a b)")[:, 0:512].rearrange("p (a b) -> p a b", a=4)
        h_tok = carve(2, D, at=0)
        sel = carve(2, P)
        sel_w = carve(2, P)
        sel_t = carve(1, SEQ)
        e_gate = carve(2, P)
        e_act = carve(2, P)
        e_out = carve(2, 512)
        e_in_hi, e_in_lo = (carve_r(DT, 3 * CAP) for _ in range(2))
        act_hi, act_lo = (carve_r(2, 3 * CAP) for _ in range(2))
        zeroed = arena_r[:, cursor[0] - 2 * (DT + 2) * 3 * CAP:cursor[0]].rearrange("p (a b) -> p a b", b=P)
        assert cursor[0] <= 23400 - 2 * SPLITS * UNIT

        RT, cur = {}, 0
        for name, k in [("logits", 2 * 36), ("gmax", 2), ("g_diff", 8), ("g_exp", 8), ("g_sum", 2), ("g_top", 2),
                        ("g_hit", 8), ("g_first", 2), ("g_one", 8), ("prod", 64), ("le", 16), ("m1", 2), ("hit1", 16),
                        ("first1", 2), ("one1", 16), ("le2", 16), ("m2", 2), ("hit2", 16), ("first2", 2), ("one2", 16),
                        ("t_diff", 2), ("t_exp", 2), ("t_sum", 2), ("w1", 2), ("w2", 2), ("ce", 16), ("comb", 64), ("hit", 16),
                        ("used", 64), ("rank", 64), ("most", 1), ("over", 1)]:
            RT[name] = (cur, k)
            cur += k

        def router(name, groups=None):
            a, k = RT[name]
            v = rt[:, a:a + k]
            return v if groups is None else v.rearrange("p (a b) -> p a b", a=groups)

        comb = router("comb", 2)

        def flat2(a):
            return a.rearrange("p a b -> p (a b)")

        def two_experts(a, k, n):
            return a[:, k:k + n, :].rearrange("p a (e c) -> p a e c", e=3)[:, :, 0::2, :]

        SM = dict(c=0, g=16, beta=24, b=40, a=48, sp=56, ea=64, G=72, R=80, H=88, eG=104, eR=112, eH=120, abs=136, bg=144)
        G_COL = [(p % 2) * BH + p // 2 for p in range(2 * BH)]

        def M(name, k=0, n=1):
            return small[:, SM[name] + k:SM[name] + k + n]

        bank = [ctx.enter_context(nc.psum_tensor(f"bank{n}", [P, 512], F32)) for n in range(8)]

        def gathered(part):
            return bank[3 * part][:, :].rearrange("p (a e c) -> p a e c", a=4, e=2)

        turned_act = bank[1][:, SEQ:2 * SEQ].rearrange("p (a e c) -> p a e c", a=2, e=2)

        def V(name, k=0, n=1):
            return vec[:, VEC[name] + k:VEC[name] + k + n]

        def C(name, k=0, n=P, rows=P):
            return tab[0:rows, TAB[name] + k:TAB[name] + k + n]

        ident, ones = C("ident"), C("ones")

        slot_loaded = [sem(f"slot_loaded{s}") for s in range(SLOTS)]
        unit_begun = sem("unit_begun")
        tile_done = sem("tile_done")
        evacuated = [sem(f"evacuated{b}") for b in range(BANKS)]
        vec_loaded, tab_loaded, tok_loaded = sem("vec_loaded"), sem("tab_loaded"), sem("tok_loaded")
        rel_loaded = sem("rel_loaded")
        squared, summed, rooted, normed = sem("squared"), sem("summed"), sem("rooted"), sem("normed")
        dve_step, act_step = sem("dve_step"), sem("act_step")

        made = {}

        def S(name):
            if name not in made:
                made[name] = sem(name)
            return made[name]

        def done(n):
            return n + 1

        def freed(n):
            return n // BANKS + 1

        def wait_stored(eng, n):
            eng.wait_ge(evacuated[n % BANKS], freed(n))

        at = {}
        n = 0
        for name, count in [("qk", 4 * RH)]:
            at[name] = n
            n += count
        at["v"] = n
        n += 3 * RH
        for hh in range(RH):
            at["gate", hh] = n
            at["av", hh] = n + 4
            n += 8
        for name, count in [("wo0", DT), ("ffn0", 2 * FT), ("down0", DT), ("kva", KVT + 1), ("qa", QT), ("kn", MH),
                            ("vm", 6), ("qn", MH), ("qr", 4), ("am", MH), ("wo1", DT), ("ffn1", 2 * FT),
                            ("down1", DT), ("qkvb", 12), ("qka", 8), ("va", 2), ("z", BH), ("gates", 16),
                            ("aa", AH), ("up", 2 * DT), ("wout", DT)]:
            at[name] = n
            n += count

        norm_k = [("mix0", DT), ("ffn0", DT), ("mix1", DT), ("ckv", KVT), ("cq", QT), ("ffn1", DT), ("final", DT),
                  ("n1", DT), ("n2", DT), ("final2", DT)]
        norm_no = {name: j for j, (name, _) in enumerate(norm_k)}
        norm_sq, norm_out = {}, {}
        a = b = 0
        for name, k in norm_k:
            norm_sq[name], norm_out[name] = a, b
            a += k
            b += k + (DT if name == "mix1" else 0)
        XC = slice(META, T0)
        ALL = slice(0, T0)

        block = ctx.enter_context(nc.Block())

        @block.sync
        def _(sp):
            def load(slot, unit):
                sp.dma_start(ring[:, slot, :], unit).then_inc(slot_loaded[slot], 16)

            for s in range(SLOTS):
                load(s, weights[s])
            rounds = UNITS // SLOTS
            with sp.Fori(1, rounds) as r:
                for s in range(SLOTS):
                    sp.wait_ge(unit_begun, (r - 1) * SLOTS + s + 2)
                    load(s, weights[bass.ds(r * SLOTS + s, 1)].rearrange("a p n -> (a p) n"))
            for u in range(rounds * SLOTS, UNITS):
                sp.wait_ge(unit_begun, u - SLOTS + 2)
                load(u % SLOTS, weights[u])
            sp.wait_ge(S("rounds_ready"), 1)
            more = sp.value_load(rounds_t[0:1, 0:1], min_val=1, max_val=SEQ // CAP)
            first = UNITS - PAIRS * SLOTS
            with sp.If(more > 1):
                with sp.Fori(1, more) as r:
                    with sp.Fori(0, PAIRS) as pair:
                        for s in range(SLOTS):
                            sp.wait_ge(unit_begun, (r * PAIRS + pair) * SLOTS + (first + s - SLOTS + 2))
                            load((first + s) % SLOTS,
                                 weights[bass.ds(pair * SLOTS + (first + s), 1)].rearrange("a p n -> (a p) n"))
            for k in range(DT):
                sp.wait_ge(normed, norm_out["final2"] + k + 1)
                sp.dma_start(out[:, k, :], hn[:, k, 0:SEQ]).then_inc(S("out_stored"), 16)
            sp.wait_ge(S("out_stored"), 16 * DT)

        @block.gpsimd
        def _(pool):
            nc.gpsimd.memset(relb[:, :], NEG).then_inc(S("rel_zeroed"), 1)
            pool.wait_ge(S("rel_zeroed"), 1)
            pool.dma_start(relb[0:BUCKETS, :], rel_bias).then_inc(rel_loaded, 16)
            pool.wait_ge(S("bias_row"), 1)
            pool.dma_start(skew, bias_w.unsqueeze(1).to_broadcast([AH, P, 512])).then_inc(S("skew_written"), 16)
            pool.wait_ge(S("skew_written"), 16)
            pool.wait_ge(S("ret_out"), 4 * RH)
            flat = P * 512
            for a in range(AH):
                for off, lo, n in ((255, 0, P), (127, P, SEQ)):
                    pool.dma_start(bias_a[:, a, lo:lo + n],
                                   bass.AP(skew.tensor, a * flat + off, [[511, P], [1, n]])).then_inc(S("bias_loaded"), 16)
            pool.wait_ge(S("bias_loaded"), 16 * 2 * AH)

            def low(layer, n, turn=None):
                count = layer * FFN_UNITS + n + 1
                pool.wait_ge(S("w_hi_ready"), count if turn is None else turn * SLOTS + count)
                nc.gpsimd.tensor_tensor(w_lo[:, n % SPLITS, :], ring[:, (FFN_FIRST[layer] + n) % SLOTS, :],
                                        w_hi[:, n % SPLITS, :], ALU.subtract).then_inc(S("w_lo_ready"), 1)

            for layer in range(2):
                turns = FFN_UNITS // SLOTS
                with pool.Fori(0, turns) as r:
                    for n in range(SLOTS):
                        low(layer, n, r)
                for n in range(turns * SLOTS, FFN_UNITS):
                    low(layer, n)

        @block.tensor
        def _(pe):
            mm = nc.tensor.matmul
            pos = [0, 0]

            def weight(turn=None, per_turn=0):
                blk = pos[0]
                pos[0] += 1
                unit, place = divmod(blk, UB)
                slot = unit % SLOTS
                if place == 0:
                    want = 16 * (unit // SLOTS + 1)
                    pe.wait_ge(slot_loaded[slot], want if turn is None else turn * (16 * per_turn) + want)
                return ring[:, slot, place * P:(place + 1) * P], place == 0

            def narrow(K, moving, cols, ready=None, turn=None, tiles_per_turn=0, rounds_per_turn=0):
                t = pos[1]
                pos[1] += 1
                dst = bank[t % BANKS]
                if t >= BANKS:
                    want = freed(t - BANKS)
                    pe.wait_ge(evacuated[t % BANKS],
                               want if turn is None else turn * (tiles_per_turn // BANKS) + want)
                for k in range(K):
                    if ready:
                        ready(k)
                    w, first = weight(turn=turn, per_turn=rounds_per_turn)
                    last = mm(dst[:, 0:cols], w, moving(k), start=k == 0, stop=k == K - 1)
                    if first:
                        last.then_inc(unit_begun, 1)
                last.then_inc(tile_done, 1)

            def wide(K, stationary, tiles, ready=None):
                t = pos[1]
                pos[1] += len(tiles)
                for j in range(len(tiles)):
                    if t + j >= BANKS:
                        wait_stored(pe, t + j - BANKS)
                for k in range(K):
                    if ready:
                        ready(k)
                    unit, half = divmod(pos[0] // 4, 2)
                    pos[0] += 4
                    slot = unit % SLOTS
                    if half == 0:
                        pe.wait_ge(slot_loaded[slot], 16 * (unit // SLOTS + 1))
                    for j, (lo, hi) in enumerate(tiles):
                        last = mm(bank[(t + j) % BANKS][0:hi - lo, :], stationary(k)[:, lo:hi],
                                  ring[:, slot, half * 512:(half + 1) * 512], start=k == 0, stop=k == K - 1)
                        if half == 0 and j == 0:
                            last.then_inc(unit_begun, 1)
                        if k == K - 1:
                            last.then_inc(tile_done, 1)

            def norm_sum(name, K, cols):
                for k in range(K):
                    pe.wait_ge(squared, norm_sq[name] + k + 1)
                    last = mm(bank[7][:, 0:cols], ones, sq[:, k, 0:cols], start=k == 0, stop=k == K - 1)
                last.then_inc(summed, 1)

            def normed_ready(name, extra=0):
                return lambda k: pe.wait_ge(normed, norm_out[name] + extra + k + 1)

            pe.wait_ge(S("c_silu"), 1)
            with pe.Fori(0, MODS * DT // SLOTS) as r:
                for b in range(MOD_GROUPS):
                    pe.wait_ge(S("mod_read"), r * MOD_GROUPS + b + 1)
                    for k in range(DT):
                        slot, part = divmod(b * DT + k, 2)
                        if part == 0:
                            pe.wait_ge(slot_loaded[slot], r * 16 + 16)
                        last = mm(bank[b][:, :], small[:, k:k + 1].to_broadcast([P, P]),
                                  ring[:, slot, part * 512:(part + 1) * 512], start=k == 0, stop=k == DT - 1)
                        if part == 0:
                            last.then_inc(unit_begun, 1)
                    last.then_inc(S("mod_summed"), 1)
            pos[0] += MODS * DT * UB

            pe.wait_ge(rel_loaded, 16)
            pe.wait_ge(tab_loaded, 16)
            mm(bank[4][0:AH, :], relb[0:BUCKETS + 1, :], C("bucket", 0, 512, BUCKETS + 1), start=True,
               stop=True).then_inc(S("bias_sum"), 1)

            norm_sum("mix0", DT, T0)
            ready = normed_ready("mix0")
            for t in range(4 * RH):
                narrow(DT, lambda k: hn[:, k, :], T0, ready if t == 0 else None)
            for g in range(RH):
                wide(DT, lambda k: hn[:, k, :], TOK)

            def ret_mean(hh):
                for d in range(4):
                    wait_stored(pe, at["av", hh] + d)
                    last = mm(bank[6][:, 0:T0], ones, o_r[:, 4 * hh + d, :], start=d == 0, stop=d == 3)
                last.then_inc(S("gn_mean"), 1)

            def ret_var(hh):
                pe.wait_ge(S("gn_squared"), hh + 1)
                for d in range(4):
                    last = mm(bank[7][:, 0:T0], ones, sq[:, d, :], start=d == 0, stop=d == 3)
                last.then_inc(S("gn_var"), 1)

            for hh in range(RH):
                pe.wait_ge(S("roped"), 2 * hh + 2)
                if hh:
                    pe.wait_ge(S("decayed"), hh)
                for half in range(2):
                    mm(bank[4][0:META, 0:T0], qk[:, 4 * hh + 2 + half, 0:META], qk[:, 4 * hh + half, :],
                       start=half == 0, stop=half == 1)
                for j, (lo, hi) in enumerate(TOK[1:]):
                    for half in range(2):
                        last = mm(bank[5][:, j * SEQ:j * SEQ + T0 - lo], qk[:, 4 * hh + 2 + half, lo:hi],
                                  qk[:, 4 * hh + half, lo:T0], start=half == 0, stop=half == 1)
                last.then_inc(S("ret_scored"), 1)
                if hh:
                    ret_mean(hh - 1)
                for t in range(4):
                    if hh and t == 2:
                        ret_var(hh - 1)
                    narrow(DT, lambda k: hn[:, k, :], T0)
                pe.wait_ge(S("decayed"), hh + 1)
                if hh == 0:
                    wait_stored(pe, at["v"] + 3 * RH - 1)
                for d in range(4):
                    t = pos[1]
                    pos[1] += 1
                    wait_stored(pe, t - BANKS)
                    dst, col, c0 = bank[t % BANKS], hh * RDV + d * P, 0
                    for j, (lo, hi) in enumerate(TOK):
                        last = mm(dst[:, lo:T0], v_r[0:hi - lo, j, col:col + P], sc_r[0:hi - lo, hh % 2, c0:c0 + T0 - lo],
                                  start=j == 0, stop=j == 2, skip_group_check=True)
                        c0 += T0 - lo
                    last.then_inc(tile_done, 1)
            ret_mean(RH - 1)
            ret_var(RH - 1)
            for t in range(DT):
                narrow(4 * RH, lambda k: o_r[:, k, :], T0,
                       (lambda k: pe.wait_ge(S("ret_out"), k + 1)) if t == 0 else None)

            def split_tile(layer, first, K, high, low, cols, ready=None, turn=None):
                t = pos[1]
                pos[1] += 1
                dst = bank[t % BANKS]
                want = freed(t - BANKS)
                pe.wait_ge(evacuated[t % BANKS], want if turn is None else turn * (SLOTS // BANKS) + want)
                for k in range(K):
                    if ready:
                        ready(k)
                    blk = pos[0] - first
                    pos[0] += 1
                    n, place = divmod(blk, UB)
                    if place == 0:
                        count = layer * FFN_UNITS + n + 1
                        pe.wait_ge(S("w_lo_ready"), count if turn is None else turn * SLOTS + count)
                    cut = slice(place * P, (place + 1) * P)
                    wh, wl = w_hi[:, n % SPLITS, cut], w_lo[:, n % SPLITS, cut]
                    begun = mm(dst[:, 0:cols], wh, high(k), start=k == 0, stop=False)
                    if place == 0:
                        begun.then_inc(unit_begun, 1)
                    mm(dst[:, 0:cols], wh, low(k), start=False, stop=False)
                    last = mm(dst[:, 0:cols], wl, high(k), start=False, stop=k == K - 1)
                last.then_inc(tile_done, 1)

            def feed_forward(layer, src, cols):
                norm_sum(f"ffn{layer}", DT, cols)
                turns = 2 * FT // SLOTS
                start = list(pos)
                first = FFN_FIRST[layer] * UB
                assert pos[0] == first
                high, low = (lambda k: src(hn_hi, k)), (lambda k: src(hn_lo, k))
                for t in range(SLOTS):
                    split_tile(layer, first, DT, high, low, cols,
                               (lambda k: pe.wait_ge(S("hn_split"), layer * DT + k + 1)) if t == 0 else None)
                pos[0], pos[1] = start
                with pe.Fori(1, turns) as r:
                    for t in range(SLOTS):
                        split_tile(layer, first, DT, high, low, cols, turn=r)
                pos[0] = start[0] + turns * SLOTS * UB
                pos[1] = start[1] + turns * SLOTS
                for t in range(turns * SLOTS, 2 * FT):
                    split_tile(layer, first, DT, high, low, cols)
                for t in range(DT):
                    split_tile(layer, first, FT, lambda k: ff_hi[:, k, 0:cols], lambda k: ff_lo[:, k, 0:cols], cols,
                               (lambda k: pe.wait_ge(S("ff_split"), 2 + layer * FT + k + 1)) if t == 0 else None)

            feed_forward(0, lambda a, k: a[:, k, :], T0)

            norm_sum("mix1", DT, T0)
            for t in range(KVT + 1):
                narrow(DT, lambda k: kvn[:, k, :], T0, normed_ready("mix1") if t == 0 else None)
            for t in range(QT):
                narrow(DT, lambda k: hn[:, k, XC], SEQ, normed_ready("mix1", DT) if t == 0 else None)
            norm_sum("ckv", KVT, T0)
            norm_sum("cq", QT, SEQ)
            for t in range(MH):
                narrow(KVT, lambda k: ckv[:, k, :], T0, normed_ready("ckv") if t == 0 else None)
            for g in range(2):
                wide(KVT, lambda k: ckv[:, k, :], TOK)
            for t in range(MH + 4):
                narrow(QT, lambda k: cq[:, k, :], SEQ, normed_ready("cq") if t == 0 else None)

            def attention(tag, heads, score, put):
                def scores(i):
                    if i < heads:
                        score(i, bank[4 + i % 2]).then_inc(S(tag + "_scored"), 1)

                scores(0)
                scores(1)
                for j in range(heads):
                    pe.wait_ge(S(tag + "_p"), j + 1)
                    if j:
                        pe.wait_ge(S(tag + "_pt"), j)
                    put(j, lambda: scores(j + 2))

            def mla_score(i, dst):
                if i == 0:
                    pe.wait_ge(S("q_roped"), 5)
                    wait_stored(pe, at["qn"] + MH - 1)
                if i >= 2:
                    pe.wait_ge(S("mla_p"), i - 1)
                r = 64 * (i % 2)
                for lo, hi, q0 in [(0, META + P, 0), (META + P, MLA_W, P)]:
                    w = hi - lo
                    mm(dst[:, lo:hi], q_m[:, i, q0:q0 + P], k_m[:, i, 0:w], start=True, stop=False)
                    last = mm(dst[:, lo:hi], qrope[r:r + ROPE, i // 2, q0:q0 + P], krope[r:r + ROPE, 0, 0:w],
                              start=False, stop=True)
                return last

            def values(tag, j, pv, v_cols, meta, rows, between):
                key0 = META if meta else 0
                second = key0 + P
                nc.tensor.transpose(bank[6][:, 0:P], pv[:, key0:key0 + P], ident)
                nc.tensor.transpose(bank[6][:, P:2 * P], pv[:, second + key0:second + key0 + P], ident)
                last = nc.tensor.transpose(bank[6][:, 2 * P:3 * P], pv[:, second + key0 + P:second + key0 + 2 * P], ident)
                last.then_inc(S(tag + "_turned"), 1)
                if meta:
                    if j:
                        pe.wait_ge(S(tag + "_ptm"), j)
                    nc.tensor.transpose(bank[7][0:META, 0:P], pv[:, 0:META], ident)
                    nc.tensor.transpose(bank[7][0:META, P:2 * P], pv[:, second:second + META],
                                        ident).then_inc(S(tag + "_turnedm"), 1)
                between()
                t = pos[1]
                pos[1] += 1
                wait_stored(pe, t - BANKS)
                dst = bank[t % BANKS]
                pe.wait_ge(S(tag + "_pt"), j + 1)
                pt = pt_m if meta else pt_a
                v = v_m if meta else v_a
                o = 1 if meta else 0
                mm(dst[rows, 0:SEQ], v[:, o, v_cols], pt[:, 0, 0:SEQ], start=True, stop=False, skip_group_check=True)
                last = mm(dst[rows, P:SEQ], v[:, o + 1, v_cols], pt[:, 0, SEQ:3 * P], start=False, stop=not meta,
                          skip_group_check=True)
                if meta:
                    pe.wait_ge(S(tag + "_ptm"), j + 1)
                    last = mm(dst[rows, 0:SEQ], v[0:META, 0, v_cols], pt_meta[0:META, 0, :], start=False, stop=True,
                              skip_group_check=True)
                last.then_inc(tile_done, 1)

            def mla_values(j, between):
                if j == 0:
                    wait_stored(pe, at["vm"] + 5)
                values("mla", j, p_m[:, j % 2, :], slice(j * P, (j + 1) * P), True, slice(0, P), between)

            attention("mla", MH, mla_score, mla_values)
            for t in range(DT):
                narrow(MH, lambda k: o_m[:, k, :], SEQ,
                       (lambda k: wait_stored(pe, at["am"] + k)) if t == 0 else None)
            feed_forward(1, lambda a, k: a[:, k, XC], SEQ)
            norm_sum("final", DT, SEQ)

            norm_sum("n1", DT, SEQ)
            hb = lambda k: hn[:, k, 0:SEQ]
            narrow(DT, hb, SEQ, lambda k: pe.wait_ge(S("hb_ready"), k + 1))
            for tt in range(2):
                for k in range(DT):
                    last = mm(bank[4][:, 8 * tt:8 * tt + 8], hn[:, k, tt * P:(tt + 1) * P], V("wba", 8 * k, 8),
                              start=k == 0, stop=k == DT - 1)
            last.then_inc(S("ba_done"), 1)
            for t in range(1, 12):
                narrow(DT, hb, SEQ)
            pe.wait_ge(S("g_ready"), 1)
            g = M("g", 0, 8)
            for j, name in enumerate(("upto", "chunk", "half0", "half1")):
                last = mm(bank[5][:, 8 * j:8 * j + 8], C(name), g, start=True, stop=True)
            last.then_inc(S("g_summed"), 1)
            pe.wait_ge(S("g_stored"), 1)
            for p in range(NP):
                last = mm(bank[6 + p // 4][:, (p % 4) * P:(p % 4 + 1) * P],
                          M("g", G_COL[p]).to_broadcast([P, P]), C("upto"), start=True, stop=True)
            last.then_inc(S("row_g"), 1)
            for p in range(NP):
                last = mm(bank[4 + p // 4][:, (p % 4) * P:(p % 4 + 1) * P],
                          M("beta", G_COL[p]).to_broadcast([P, P]), ident, start=True, stop=True)
            last.then_inc(S("row_beta"), 1)
            for t in range(8):
                narrow(DT, hb, SEQ)
            pe.wait_ge(S("l2_squared"), 8)
            pe.wait_ge(S("beta_rows"), 1)
            pe.wait_ge(S("exp_rows"), 1)
            for j in range(4):
                last = mm(bank[4 + j][:, :], ones, l2sq[:, j * 512:(j + 1) * 512], start=True, stop=True)
            last.then_inc(S("l2_summed"), 1)
            wide(DT, hb, [(0, P), (P, SEQ)])
            for t in range(BH):
                narrow(DT, hb, SEQ)
            pe.wait_ge(S("l2_done"), 1)
            for p in range(NP):
                kp = cb[:, BH + p // 2, (p % 2) * P:(p % 2 + 1) * P]
                last = mm(bank[4 + p // 4][:, (p % 4) * P:(p % 4 + 1) * P], kp, kp, start=True, stop=True)
            last.then_inc(S("gram_done"), 1)
            for p in range(NP):
                kp = cb[:, BH + p // 2, (p % 2) * P:(p % 2 + 1) * P]
                last = mm(bank[6 + p // 4][:, (p % 4) * P:(p % 4 + 1) * P], kp,
                          cb[:, p // 2, (p % 2) * P:(p % 2 + 1) * P], start=True, stop=True)
            last.then_inc(S("qk_done"), 1)
            narrow(DT, hb, SEQ)
            narrow(DT, hb, SEQ)
            pe.wait_ge(S("lt_ready"), 1)
            for p in range(NP):
                last = nc.tensor.transpose(bank[4 + p // 4][:, (p % 4) * P:(p % 4 + 1) * P],
                                           cb[:, BH + p // 2, (p % 2) * P:(p % 2 + 1) * P], ident)
            last.then_inc(S("k_turned"), 1)
            pe.wait_ge(S("pt_ready"), 1)
            for p in range(NP):
                last = nc.tensor.transpose(bank[6 + p // 4][:, (p % 4) * P:(p % 4 + 1) * P],
                                           cb[:, 2 * BH + p // 2, (p % 2) * P:(p % 2 + 1) * P], ident)
            last.then_inc(S("v_turned"), 1)
            narrow(DT, hb, SEQ)
            narrow(DT, hb, SEQ)
            pe.wait_ge(S("tok_ready"), 1)
            for lv in range(6):
                pe.wait_ge(S("ml_ready"), lv + 1)
                for half in range(2):
                    if lv and half == 0:
                        pe.wait_ge(S("inv_ready"), lv)
                    for p in range(4 * half, 4 * half + 4):
                        last = mm(bank[4 + half][:, (p % 4) * P:(p % 4 + 1) * P], ML[:, p, :],
                                  X[:, p, :] if lv else ident, start=True, stop=True)
                last.then_inc(S("mx_done"), 1)
                narrow(DT, hb, SEQ)
                if lv == 0:
                    continue
                pe.wait_ge(S("t_stored"), lv)
                for half in range(2):
                    for p in range(4 * half, 4 * half + 4):
                        last = mm(bank[6 + half][:, (p % 4) * P:(p % 4 + 1) * P], TM[:, p, :], Y[:, p, :],
                                  start=True, stop=True)
                last.then_inc(S("dy_done"), 1)
                if lv < 5:
                    for half in range(2):
                        for p in range(4 * half, 4 * half + 4):
                            last = mm(bank[4 + half][:, (p % 4) * P:(p % 4 + 1) * P], Y[:, p, :], TM[:, p, :],
                                      start=True, stop=True)
                    last.then_inc(S("dx_done"), 1)
                narrow(DT, hb, SEQ)
            pe.wait_ge(S("inv_ready"), 6)
            for p in range(NP):
                last = mm(bank[4 + p // 4][:, (p % 4) * P:(p % 4 + 1) * P], Y[:, p, :], v_tok[:, p, :],
                          start=True, stop=True)
            last.then_inc(S("u_done"), 1)
            for p in range(NP):
                last = mm(bank[6 + p // 4][:, (p % 4) * P:(p % 4 + 1) * P], k_tok[:, p, :], Y[:, p, :],
                          start=True, stop=True)
            last.then_inc(S("w_done"), 1)
            narrow(DT, hb, SEQ)
            for c in range(4):
                R, tt = CHUNK * (c % 2), c // 2
                rows = slice(R, R + CHUNK)
                if c == 0:
                    pe.wait_ge(S("u_stored"), 1)
                    pe.wait_ge(S("w_stored"), 1)
                if c:
                    pe.wait_ge(S("state_ready"), c)
                    for a in range(BH):
                        last = mm(bank[4][rows, a * P:(a + 1) * P], wT[:, 2 * a + tt, rows], st[:, a, :],
                                  start=True, stop=True)
                    last.then_inc(S("ws_done"), 1)
                pe.wait_ge(S("vn_ready"), c + 1)
                if c:
                    pe.wait_ge(S("ob_stored"), c)
                for a in range(BH):
                    dst = bank[5][:, a * CHUNK:(a + 1) * CHUNK]
                    if c:
                        mm(dst, st[:, a, :], qg[:, 2 * a + tt, rows], start=True, stop=False)
                    last = mm(dst, vn[rows, a, :], PT[rows, 2 * a + tt, rows], start=c == 0, stop=True)
                last.then_inc(S("ob_done"), 1)
                if c < 3:
                    for a in range(BH):
                        last = mm(bank[6][:, a * P:(a + 1) * P], kd[rows, 2 * a + tt, :], vn[rows, a, :],
                                  start=True, stop=True)
                    last.then_inc(S("ds_done"), 1)
            assert pos[1] == at["aa"]
            pe.wait_ge(S("ob_squared"), 1)
            for j in range(2):
                last = mm(bank[4 + j][:, :], ones, obsq[:, j * 512:(j + 1) * 512], start=True, stop=True)
            last.then_inc(S("ob_summed"), 1)

            def moba_score(i, dst):
                if i == 0:
                    wait_stored(pe, at["qka"] + 7)
                    pe.wait_ge(S("ob_rooted"), 1)
                if i >= 2:
                    pe.wait_ge(S("moba_p"), i - 1)
                r = slice(AHD * (i % 2), AHD * (i % 2) + AHD)
                mm(dst[:, 0:P], q_a[r, i // 2, 0:P], q_a[r, 4 + i // 2, 0:P], start=True, stop=True)
                return mm(dst[:, P:MOBA_W], q_a[r, i // 2, P:SEQ], q_a[r, 4 + i // 2, :], start=True, stop=True)

            def moba_values(j, between):
                if j == 0:
                    wait_stored(pe, at["va"] + 1)
                values("moba", j, p_a[:, j % 2, :], slice(j // 2 * P, (j // 2 + 1) * P), False, slice(0, P), between)

            attention("moba", AH, moba_score, moba_values)
            for k in range(4):
                wait_stored(pe, at["aa"] + 2 * k + 1)
            for t in range(DT):
                narrow(4, lambda k: o_a[:, k, :], SEQ)
                narrow(4, lambda k: o_b[:, k, :], SEQ,
                       (lambda k: pe.wait_ge(S("ob_ready"), 1)) if t == 0 else None)
            for t in range(DT):
                narrow(DT, lambda k: m_up[:, k, :], SEQ,
                       (lambda k: pe.wait_ge(S("m_ready"), k + 1)) if t == 0 else None)

            norm_sum("n2", DT, SEQ)
            for tt in range(2):
                for k in range(DT):
                    if tt == 0:
                        pe.wait_ge(S("hb_ready"), DT + k + 1)
                    last = mm(bank[4][:, 36 * tt:36 * tt + 36], hn[:, k, tt * P:(tt + 1) * P], V("w36", 36 * k, 36),
                              start=k == 0, stop=k == DT - 1)
            last.then_inc(S("logits_done"), 1)

            for t in range(pos[1] - BANKS, pos[1]):
                wait_stored(pe, t)
            for tt in range(2):
                for k in range(DT):
                    last = nc.tensor.transpose(bank[2 * tt + k // 4][:, (k % 4) * P:(k % 4 + 1) * P],
                                               hn[:, k, tt * P:(tt + 1) * P], ident)
                last.then_inc(S("h_turned"), 1)
            def zero_bank(b):
                mm(bank[b][:, :], zero_w[:, :], C("bucket", 0, 512), start=True, stop=False, skip_group_check=True)

            for b in range(5, 8):
                zero_bank(b)
            pe.wait_ge(S("used_ready"), 1)
            used = router("used", 2)
            mm(bank[4][:, 0:NE], C("before"), used[:, 0, :], start=True, stop=True)
            mm(bank[4][:, NE:2 * NE], C("before"), used[:, 1, :], start=True, stop=False)
            mm(bank[4][:, NE:2 * NE], ones, used[:, 0, :], start=False, stop=True)
            for tt in range(2):
                last = mm(bank[4][:, 2 * NE:3 * NE], ones, used[:, tt, :], start=tt == 0, stop=tt == 1)
            last.then_inc(S("ranked"), 1)
            pe.wait_ge(S("h_tok_stored"), 4)
            pe.wait_ge(S("rounds_ready"), 1)
            zero_bank(4)

            def gather(g, part):
                if part == 0:
                    pe.wait_ge(S("sel_ready"), g + 1)
                for k in range(4):
                    for tt in range(2):
                        last = mm(bank[3 * part][:, k * P:(k + 1) * P],
                                  h_tok[:, tt, (4 * part + k) * P:(4 * part + k + 1) * P], sel[:, tt, :],
                                  start=tt == 0, stop=tt == 1)
                last.then_inc(S("gathered"), 1)

            def scatter(g):
                pe.wait_ge(S("out_stored_a"), g)
                pe.wait_ge(S("out_stored_v"), g)
                pe.wait_ge(S("sel_t_stored"), g)
                for t in range(DT):
                    last = mm(bank[4 + t // 2][:, (t % 2) * SEQ:(t % 2 + 1) * SEQ],
                              e_out[:, t // 4, (t % 4) * P:(t % 4 + 1) * P], sel_t[:, 0, :],
                              start=False, stop=t % 2 == 1, skip_group_check=True)
                return last

            def expert_unit(g, m, dst, high, low, start, stop):
                pe.wait_ge(S("e_lo_ready"), g * PAIR_UNITS + (m + 1))
                for k in range(2):
                    wh, wl = (a[:, m % SPLITS, k * 512:(k + 1) * 512] for a in (w_hi, w_lo))
                    begun = mm(dst, high(k), wh, start=start and k == 0, stop=False)
                    if k == 0:
                        begun.then_inc(unit_begun, 1)
                    mm(dst, low(k), wh, start=False, stop=False)
                    last = mm(dst, high(k), wl, start=False, stop=stop and k == 1)
                return last

            def expert_pair(g, first, final):
                pe.wait_ge(S("in_split"), g * 2 + 2)
                if not first:
                    pe.wait_ge(S("out_stored_a"), g)
                for m in range(GATE_UP_UNITS):
                    e, k0 = m // 4, m % 4 * 2
                    last = expert_unit(g, m, bank[2][:, :], lambda k: e_in_hi[:, k0 + k, e * CAP:e * CAP + P],
                                       lambda k: e_in_lo[:, k0 + k, e * CAP:e * CAP + P], m == 0, m == GATE_UP_UNITS - 1)
                last.then_inc(S("gate_up_done"), 1)
                if not final:
                    gather(g + 1, 0)
                if not first:
                    scatter(g)
                pe.wait_ge(S("sel_w_ready"), g + 1)
                pe.wait_ge(S("e_act_ready"), g + 1)
                for tt in range(2):
                    nc.tensor.transpose(bank[1][:, tt * P:(tt + 1) * P], sel_w[:, tt, :], ident)
                for k in range(2):
                    last = nc.tensor.transpose(bank[1][:, (2 + k) * P:(3 + k) * P], e_act[:, k, :], ident)
                last.then_inc(S("act_turned"), 1)
                if not final:
                    gather(g + 1, 1)
                pe.wait_ge(S("act_split"), g + 1)
                for half in range(2):
                    if half and not final:
                        pe.wait_ge(S("in_split"), g * 2 + 4)
                    for e in range(2):
                        last = expert_unit(g, GATE_UP_UNITS + 2 * half + e, bank[2 + half][:, :],
                                           lambda k: act_hi[:, k, e * CAP:e * CAP + P],
                                           lambda k: act_lo[:, k, e * CAP:e * CAP + P], e == 0, e == 1)
                    last.then_inc(S("down_done"), 1)

            pe_rounds = pe.value_load(rounds_t[0:1, 0:1], min_val=1, max_val=SEQ // CAP)
            with pe.Fori(0, pe_rounds) as r:
                gather(r * PAIRS, 0)
                gather(r * PAIRS, 1)
                expert_pair(r * PAIRS, True, False)
                with pe.Fori(1, PAIRS - 1) as pair:
                    expert_pair(r * PAIRS + pair, False, False)
                expert_pair(r * PAIRS + (PAIRS - 1), False, True)
                scatter(r * PAIRS + PAIRS).then_inc(S("moe_done"), 1)
            pe.wait_ge(S("moe_added"), DT)
            norm_sum("final2", DT, SEQ)

        @block.scalar
        def _(act):
            fn = nc.scalar.activation
            act.dma_start(vec[:, :], vectors_in).then_inc(vec_loaded, 16)
            tile = [0]

            def take():
                t = tile[0]
                tile[0] += 1
                act.wait_ge(tile_done, done(t))
                return bank[t % BANKS], evacuated[t % BANKS]

            def norm(name, src, K, cols, width, ready, eps=RMS_EPS):
                for k in range(K):
                    ready(k)
                    fn(sq[:, k, 0:cols], src(k), ACT.Square).then_inc(squared, 1)
                act.wait_ge(summed, norm_no[name] + 1)
                if norm_no[name]:
                    act.wait_ge(normed, norm_out[norm_k[norm_no[name] - 1][0]] + 1)
                fn(rms[:, 0:cols], bank[7][:, 0:cols], ACT.Sqrt, bias=eps_col(eps), scale=1.0 / width).then_inc(rooted, 1)

            def eps_col(eps):
                return eps_t[:, 0:1] if eps == RMS_EPS else eps_t[:, 1:2]

            act.wait_ge(vec_loaded, 16)
            fn(small[:, 0:DT], V("c", 0, DT), ACT.Silu).then_inc(S("c_silu"), 1)
            act.wait_ge(slot_loaded[SLOTS // 3], 16)
            act.dma_start(tab[:, :], tables_in).then_inc(tab_loaded, 16)
            act.wait_ge(slot_loaded[SLOTS - 1], 16)
            act.dma_start(h[:, :, :], tokens_in).then_inc(tok_loaded, 16)
            act.wait_ge(tok_loaded, 16)
            act.wait_ge(S("eps_set"), 1)
            norm("mix0", lambda k: h[:, k, :], DT, T0, D, lambda k: None)
            tile[0] = at["v"]
            act.wait_ge(S("skew_written"), 16)
            for g in range(RH):
                for j, (lo, hi) in enumerate(TOK):
                    src, free = take()
                    fn(v_r[0:hi - lo, j, g * RDV:(g + 1) * RDV], src[0:hi - lo, :], ACT.Copy).then_inc(free, 1)

            def gn_root(hh):
                act.wait_ge(S("gn_var"), hh + 1)
                fn(rms[:, :], bank[7][:, 0:T0], ACT.Sqrt, bias=eps_col(GN_EPS), scale=1.0 / RDV).then_inc(S("gn_root"), 1)

            def gn_square(hh):
                act.wait_ge(S("gn_centred"), hh + 1)
                fn(sq[:, 0:4, :], o_r[:, 4 * hh:4 * hh + 4, :], ACT.Square).then_inc(S("gn_squared"), 1)

            for hh in range(RH):
                if hh:
                    gn_square(hh - 1)
                for t in range(4):
                    if hh and t == 2:
                        gn_root(hh - 1)
                    src, free = take()
                    fn(gate_r[:, 4 * hh + t, :], src[:, 0:T0], ACT.Silu).then_inc(free, 1)
                for d in range(4):
                    src, free = take()
                    fn(o_r[:, 4 * hh + d, :], src[:, 0:T0], ACT.Copy).then_inc(free, 1)
            gn_square(RH - 1)
            gn_root(RH - 1)

            def high(layer, n, turn=None):
                more = lambda v, per: v if turn is None else turn * per + v
                u = FFN_FIRST[layer] + n
                act.wait_ge(slot_loaded[u % SLOTS], more(16 * (u // SLOTS + 1), 16))
                if n >= SPLITS:
                    act.wait_ge(unit_begun, more(u - SPLITS + 2, SLOTS))
                fn(w_hi[:, n % SPLITS, :], ring[:, u % SLOTS, :], ACT.Copy).then_inc(S("w_hi_ready"), 1)

            def feed_forward(layer, first_tile, cols, src):
                name = f"ffn{layer}"
                res = at["wo0"] if layer == 0 else at["wo1"]
                act.wait_ge(tile_done, done(at["av", RH - 1] + 3 if layer == 0 else at["am"] + MH - 1))
                for n in range(SPLITS):
                    high(layer, n)
                norm(name, src, DT, cols, D, lambda k: wait_stored(act, res + k))
                for k in range(DT):
                    act.wait_ge(normed, norm_out[name] + k + 1)
                    x = (lambda a: a[:, k, :]) if layer == 0 else (lambda a: a[:, k, XC])
                    fn(x(hn_hi), x(hn), ACT.Copy).then_inc(S("hn_hi_ready"), 1)
                turns = 2 * FT // SLOTS

                def gate(pair, turn=None):
                    t = first_tile + 2 * pair
                    more = lambda n, per: n if turn is None else turn * per + n
                    act.wait_ge(tile_done, more(done(t), SLOTS))
                    act.wait_ge(S("ff_split"), more(layer * FT + pair + 1, SLOTS // 2))
                    fn(ff_gate[:, pair % 2, 0:cols], bank[t % BANKS][:, 0:cols], ACT.Silu).then_inc(evacuated[t % BANKS], 1)
                    for n in (2 * pair + SPLITS, 2 * pair + 1 + SPLITS):
                        high(layer, n, turn)

                with act.Fori(0, turns) as r:
                    for j in range(SLOTS // 2):
                        gate(j, r)
                for pair in range(turns * SLOTS // 2, FT):
                    gate(pair)

            def with_high(layer, first):
                at_unit = [2 * FT + SPLITS]

                def ready(k):
                    need = min(FFN_UNITS, 2 * FT + -(-(k + 1) * FT // UB) + SPLITS - 1)
                    while at_unit[0] < need:
                        high(layer, at_unit[0])
                        at_unit[0] += 1
                    wait_stored(act, first + k)

                return ready

            feed_forward(0, at["ffn0"], T0, lambda k: h[:, k, :])

            norm("mix1", lambda k: h[:, k, :], DT, T0, D, with_high(0, at["down0"]))
            tile[0] = at["kva"]
            for t in range(KVT):
                src, free = take()
                fn(ckv[:, t, :], src[:, 0:T0], ACT.Copy).then_inc(free, 1)
            tile[0] = at["qa"]
            for t in range(QT):
                src, free = take()
                fn(cq[:, t, :], src[:, 0:SEQ], ACT.Copy).then_inc(free, 1)
            norm("ckv", lambda k: ckv[:, k, :], KVT, T0, KVR, lambda k: wait_stored(act, at["kva"] + k))
            norm("cq", lambda k: cq[:, k, :], QT, SEQ, QR, lambda k: wait_stored(act, at["qa"] + k))
            for t in range(MH):
                src, free = take()
                fn(k_m[:, t, :], src[:, 0:T0], ACT.Copy).then_inc(free, 1)
            for g in range(2):
                for j, (lo, hi) in enumerate(TOK):
                    src, free = take()
                    fn(v_m[0:hi - lo, j, g * 512:(g + 1) * 512], src[0:hi - lo, :], ACT.Copy).then_inc(free, 1)
            for t in range(MH):
                src, free = take()
                fn(q_m[:, t, :], src[:, 0:SEQ], ACT.Copy).then_inc(free, 1)

            def attention(tag, heads, probs, parts, stat, pt, store):
                for i in range(heads + 1):
                    if i < heads:
                        act.wait_ge(S(tag + "_max"), i + 1)
                        s = stat(i)
                        for j, (lo, hi) in enumerate(parts):
                            a = probs[:, i % 2, lo:hi]
                            last = fn(a, a, ACT.Exp, bias=s[:, 2 + j:3 + j], accum_out=s[:, 4 + j:5 + j])
                        last.then_inc(S(tag + "_exp"), 1)
                    if i >= 1:
                        j = i - 1
                        act.wait_ge(S(tag + "_turned"), j + 1)
                        fn(pt[:, 0, :], bank[6][:, 0:3 * P], ACT.Copy).then_inc(S(tag + "_pt"), 1)
                        store(j)

            tile[0] = at["am"]

            def mla_store(j):
                src, free = take()
                fn(o_m[:, j, :], src[:, 0:SEQ], ACT.Copy).then_inc(free, 1)

            attention("mla", MH, p_m, [(0, META + P), (META + P, MLA_W)], lambda i: stats[:, 8 * i:8 * i + 8],
                      pt_m, mla_store)
            feed_forward(1, at["ffn1"], SEQ, lambda k: h[:, k, XC])
            norm("final", lambda k: h[:, k, XC], DT, SEQ, D, with_high(1, at["down1"]))

            def shifted(name, shift, ready):
                norm(name, lambda k: h[:, k, XC], DT, SEQ, D, ready)
                for k in range(DT):
                    act.wait_ge(normed, norm_out[name] + k + 1)
                    fn(hn[:, k, 0:SEQ], hn[:, k, 0:SEQ], ACT.Identity,
                       bias=mod[:, shift * DT + k:shift * DT + k + 1]).then_inc(S("hb_ready"), 1)

            act.wait_ge(S("mod_ready"), 2)
            shifted("n1", 0, lambda k: act.wait_ge(normed, norm_out["final"] + k + 1))
            act.wait_ge(S("ba_split"), 1)
            fn(M("beta", 0, 8), M("b", 0, 8), ACT.Sigmoid).then_inc(S("beta_ready"), 1)
            fn(M("sp", 0, 8), M("abs", 0, 8), ACT.Exp, scale=-1.0)
            fn(M("ea", 0, 8), V("alog", 0, 8), ACT.Exp).then_inc(act_step, 1)
            act.wait_ge(act_step, 1)
            fn(M("sp", 0, 8), M("sp", 0, 8), ACT.Ln, bias=eps_t[:, 2:3]).then_inc(S("softplus_ln"), 1)
            tile[0] = at["qkvb"]

            def conv_silu(first):
                for t in range(first, first + 4):
                    act.wait_ge(S("conv_done"), t + 1)
                    fn(cb[:, t, :], cb[:, t, :], ACT.Silu).then_inc(S("conv_silu"), 1)

            for t in range(12):
                src, free = take()
                fn(raw_b[:, t, CONV - 1:], src[:, 0:SEQ], ACT.Copy).then_inc(free, 1)
            conv_silu(0)
            conv_silu(4)
            for t in range(8):
                act.wait_ge(S("conv_silu"), t + 1)
                fn(l2sq[:, t * SEQ:(t + 1) * SEQ], cb[:, t, :], ACT.Square).then_inc(S("l2_squared"), 1)
            act.wait_ge(S("g_stored"), 1)
            fn(M("eG", 0, 32), M("G", 0, 32), ACT.Exp).then_inc(S("g_exp"), 1)
            act.wait_ge(S("row_g"), 1)
            for j in range(2):
                last = fn(TM[:, 4 * j:4 * j + 4, :], bank[6 + j][:, :].rearrange("p (a b) -> p a b", a=4), ACT.Exp)
            last.then_inc(S("exp_rows"), 1)
            act.wait_ge(S("dec_diff"), 1)
            fn(decT[:, :, :], decT[:, :, :], ACT.Exp).then_inc(S("dec_exp"), 1)
            tile[0] = at["qka"]
            for t in range(8):
                src, free = take()
                fn(q_a[:, t, :], src[:, 0:SEQ], ACT.Copy).then_inc(free, 1)
            conv_silu(8)
            act.wait_ge(S("l2_summed"), 1)
            for j in range(4):
                last = fn(l2sq[:, j * 512:(j + 1) * 512], bank[4 + j][:, :], ACT.Sqrt, bias=eps_t[:, 0:1])
            last.then_inc(S("l2_root"), 1)
            for t in range(2):
                src, free = take()
                fn(v_a[:, t, :], src[:, :], ACT.Copy).then_inc(free, 1)
            for t in range(BH):
                src, free = take()
                fn(z_b[:, t, :], src[:, 0:SEQ], ACT.Silu).then_inc(free, 1)

            def gate():
                t = tile[0] - at["gates"]
                src, free = take()
                fn(gates[:, t, :], src[:, 0:SEQ], ACT.Sigmoid).then_inc(free, 1)

            gate()
            gate()
            gate()
            gate()
            for lv in range(6):
                if lv:
                    act.wait_ge(S("mx_done"), lv + 1)
                    for j in range(2):
                        last = fn(TM[:, 4 * j:4 * j + 4, :], bank[4 + j][:, :].rearrange("p (a b) -> p a b", a=4),
                                  ACT.Copy)
                    last.then_inc(S("t_stored"), 1)
                gate()
                if lv:
                    gate()
            act.wait_ge(S("u_done"), 1)
            for j in range(2):
                last = fn(u_tok[:, 4 * j:4 * j + 4, :], bank[4 + j][:, :].rearrange("p (a b) -> p a b", a=4), ACT.Copy)
            last.then_inc(S("u_stored"), 1)
            act.wait_ge(S("w_done"), 1)
            for j in range(2):
                last = fn(wT[:, 4 * j:4 * j + 4, :], bank[6 + j][:, :].rearrange("p (a b) -> p a b", a=4), ACT.Copy)
            last.then_inc(S("w_stored"), 1)
            gate()
            assert tile[0] == at["aa"]
            for c in range(4):
                act.wait_ge(S("ob_done"), c + 1)
                fn(o_b[:, :, c * CHUNK:(c + 1) * CHUNK], bank[5][:, 0:BH * CHUNK].rearrange("p (a b) -> p a b", a=BH),
                   ACT.Copy).then_inc(S("ob_stored"), 1)
            act.wait_ge(S("ob_stored"), 4)
            fn(obsq, o_b.rearrange("p a b -> p (a b)"), ACT.Square).then_inc(S("ob_squared"), 1)
            act.wait_ge(S("ob_summed"), 1)
            for j in range(2):
                last = fn(obsq[:, j * 512:(j + 1) * 512], bank[4 + j][:, :], ACT.Sqrt, bias=eps_t[:, 0:1], scale=1.0 / BHD)
            last.then_inc(S("ob_rooted"), 1)
            tile[0] = at["aa"]

            def moba_store(j):
                src, free = take()
                r = slice(AHD * (j % 2), AHD * (j % 2) + AHD)
                fn(o_a[r, j // 2, :], src[r, 0:SEQ], ACT.Copy).then_inc(free, 1)

            attention("moba", AH, p_a, [(0, P), (P, MOBA_W)], lambda i: stats[:, 64 + 8 * i:72 + 8 * i], pt_a, moba_store)

            shifted("n2", 3, lambda k: wait_stored(act, at["wout"] + k))

            act.wait_ge(S("group_diff"), 1)
            fn(router("g_exp"), router("g_diff"), ACT.Exp).then_inc(S("group_exp"), 1)
            act.wait_ge(S("top_diff"), 1)
            fn(router("t_exp"), router("t_diff"), ACT.Exp).then_inc(S("top_exp"), 1)
            for b in range(4):
                act.wait_ge(S("h_turned"), b // 2 + 1)
                fn(h_tok[:, b // 2, (b % 2) * 512:(b % 2 + 1) * 512], bank[b][:, :], ACT.Copy)\
                    .then_inc(S("h_tok_stored"), 1)

            act.wait_ge(S("rounds_ready"), 1)

            def expert_high(g, m):
                u = EXPERTS_FIRST + m
                act.wait_ge(slot_loaded[u % SLOTS], g * 16 + 16 * (u // SLOTS + 1))
                act.wait_ge(unit_begun, g * PAIR_UNITS + (u - SPLITS + 2))
                fn(w_hi[:, m % SPLITS, :], ring[:, u % SLOTS, :], ACT.Copy).then_inc(S("e_hi_ready"), 1)

            def in_high(g, part):
                act.wait_ge(S("gathered"), g * 2 + (part + 1))
                fn(two_experts(e_in_hi, 4 * part, 4), gathered(part), ACT.Copy).then_inc(S("in_hi_ready"), 1)

            def expert_pair(g, final):
                for m in range(AHEAD, GATE_UP_UNITS + AHEAD):
                    expert_high(g, m)
                act.wait_ge(S("gate_up_done"), g + 1)
                fn(flat2(e_gate), bank[2][:, 0:EF], ACT.Silu).then_inc(S("e_gate_ready"), 1)
                if not final:
                    in_high(g + 1, 0)
                act.wait_ge(S("act_turned"), g + 1)
                fn(two_experts(act_hi, 0, 2), turned_act, ACT.Copy).then_inc(S("act_hi_ready"), 1)
                if not final:
                    in_high(g + 1, 1)
                expert_high(g, PAIR_UNITS - 1)
                if not final:
                    expert_high(g + 1, 0)
                    expert_high(g + 1, 1)
                act.wait_ge(S("down_done"), g * 2 + 1)
                fn(e_out[:, 0, :], bank[2][:, :], ACT.Copy).then_inc(S("out_stored_a"), 1)
                if not final:
                    expert_high(g + 1, 2)

            act_rounds = act.value_load(rounds_t[0:1, 0:1], min_val=1, max_val=SEQ // CAP)
            with act.Fori(0, act_rounds) as r:
                for m in range(AHEAD):
                    expert_high(r * PAIRS, m)
                in_high(r * PAIRS, 0)
                in_high(r * PAIRS, 1)
                with act.Fori(0, PAIRS - 1) as pair:
                    expert_pair(r * PAIRS + pair, False)
                expert_pair(r * PAIRS + (PAIRS - 1), True)
            norm("final2", lambda k: h[:, k, XC], DT, SEQ, D, lambda k: act.wait_ge(S("moe_added"), k + 1))

        @block.vector
        def _(dve):
            tt_, ts_, stt = nc.vector.tensor_tensor, nc.vector.tensor_scalar, nc.vector.scalar_tensor_tensor
            steps = [0]

            def link(ins):
                steps[0] += 1
                ins.then_inc(dve_step, 1)
                dve.wait_ge(dve_step, steps[0])

            def take(t):
                dve.wait_ge(tile_done, done(t))
                return bank[t % BANKS], evacuated[t % BANKS]

            def spread(a, n):
                return a.unsqueeze(1).to_broadcast([a.shape[0], n, a.shape[1]])

            def norm_scale(name, cols):
                dve.wait_ge(rooted, norm_no[name] + 1)
                if norm_no[name]:
                    dve.wait_ge(normed, norm_out[name])
                link(nc.vector.reciprocal(rstd[:, 0:cols], rms[:, 0:cols]))

            def norm_apply(src, dst, gain, K, cols):
                for k in range(K):
                    stt(dst(k), src(k), gain(k), cols, ALU.mult, ALU.mult).then_inc(normed, 1)

            nc.vector.memset(eps_t[:, 0:1], RMS_EPS)
            nc.vector.memset(zero_w[:, :], 0.0)
            for n in range(2):
                nc.vector.memset(eps_t[:, 2 + n:3 + n], 1.0).then_inc(S("ff_split"), 1)
            nc.vector.memset(eps_t[:, 1:2], GN_EPS).then_inc(S("eps_set"), 1)
            dve.wait_ge(vec_loaded, 16)
            for b in range(MOD_GROUPS):
                nc.vector.memset(small[:, DT + b:DT + b + 1], 0.0).then_inc(S("mod_read"), 1)
            dve.wait_ge(tab_loaded, 16)
            with dve.Fori(0, MODS * DT // SLOTS) as r:
                for b in range(MOD_GROUPS):
                    turn = r * MOD_GROUPS + b
                    dve.wait_ge(S("mod_summed"), turn + 1)
                    tt_(mod_diag, bank[b][:, :].rearrange("p (a b) -> p a b", a=4), spread(ident, 4),
                        ALU.mult).then_inc(S("mod_read"), 1)
                    dve.wait_ge(S("mod_read"), turn + (MOD_GROUPS + 1))
                    nc.vector.tensor_reduce(mod[:, bass.ds(turn * 4, 4)], mod_diag, AX, ALU.add)\
                        .then_inc(S("mod_reduced"), 1)
                    dve.wait_ge(S("mod_reduced"), turn + 1)
            link(tt_(mod[:, :], mod[:, :], V("b_mod", 0, MODS * DT), ALU.add))
            for part, gain in ((1, "n1"), (4, "n2")):
                a = mod[:, part * DT:(part + 1) * DT]
                stt(a, a, 1.0, V(gain, 0, DT), ALU.add, ALU.mult).then_inc(S("mod_ready"), 1)
            dve.wait_ge(S("bias_sum"), 1)
            nc.vector.tensor_copy(bias_w, bank[4][0:AH, :]).then_inc(S("bias_row"), 1)
            norm_scale("mix0", T0)
            norm_apply(lambda k: h[:, k, :], lambda k: hn[:, k, :], lambda k: V("mix0", k), DT, rstd[:, :])
            for pair in range(2 * RH):
                t = at["qk"] + 2 * pair
                a, free = take(t)
                if pair:
                    dve.wait_ge(S("roped"), pair)
                tt_(rope_t[:, 0, :], a[:, 0:T0], C("cos_r", 0, T0), ALU.mult)
                tt_(rope_t[:, 1, :], a[:, 0:T0], C("sin_r", 0, T0), ALU.mult).then_inc(free, 1)
                a, free = take(t + 1)
                tt_(rope_t[:, 2, :], a[:, 0:T0], C("sin_r", 0, T0), ALU.mult)
                tt_(rope_t[:, 3, :], a[:, 0:T0], C("cos_r", 0, T0), ALU.mult).then_inc(free, 1)
                wait_stored(dve, t + 1)
                tt_(qk[:, 2 * pair, :], rope_t[:, 0, :], rope_t[:, 2, :], ALU.subtract)
                tt_(qk[:, 2 * pair + 1, :], rope_t[:, 1, :], rope_t[:, 3, :], ALU.add).then_inc(S("roped"), 1)

            def gn_centre(hh):
                dve.wait_ge(S("gn_mean"), hh + 1)
                a = o_r[:, 4 * hh:4 * hh + 4, :]
                stt(a, spread(bank[6][:, 0:T0], 4), -1.0 / RDV, a, ALU.mult, ALU.add).then_inc(S("gn_centred"), 1)

            def gn_apply(hh):
                dve.wait_ge(S("gn_root"), hh + 1)
                link(nc.vector.reciprocal(rstd[:, :], rms[:, :]))
                a = o_r[:, 4 * hh:4 * hh + 4, :]
                dve.wait_ge(S("gn_squared"), hh + 1)
                link(tt_(a, a, spread(rstd[:, :], 4), ALU.mult))
                for d in range(4):
                    t = 4 * hh + d
                    wait_stored(dve, at["gate", hh] + d)
                    stt(o_r[:, t, :], o_r[:, t, :], V("gn", t), gate_r[:, t, :], ALU.mult,
                        ALU.mult).then_inc(S("ret_out"), 1)

            for hh in range(RH):
                dve.wait_ge(S("ret_scored"), hh + 1)
                if hh >= 2:
                    dve.wait_ge(tile_done, done(at["av", hh - 2] + 3))
                col = TAB["decay"] + hh * SC_W
                tt_(sc_r[0:META, hh % 2, 0:T0], bank[4][0:META, 0:T0], tab[0:META, col:col + T0], ALU.mult)
                tt_(sc_r[:, hh % 2, T0:], bank[5][:, 0:SEQ + P], tab[:, col + T0:col + SC_W],
                    ALU.mult).then_inc(S("decayed"), 1)
                if hh:
                    gn_centre(hh - 1)
                    gn_apply(hh - 1)
            gn_centre(RH - 1)
            gn_apply(RH - 1)

            def add_tiles(first, cols, dst):
                for k in range(DT):
                    src, free = take(first + k)
                    tt_(dst(k), dst(k), src[:, 0:cols], ALU.add).then_inc(free, 1)

            add_tiles(at["wo0"], T0, lambda k: h[:, k, :])

            def feed_forward(layer, cols, src, dst):
                name = f"ffn{layer}"
                norm_scale(name, cols)
                for k in range(DT + 1):
                    if k < DT:
                        stt(dst(hn, k), src(k), V(name, k), rstd[:, 0:cols], ALU.mult, ALU.mult).then_inc(normed, 1)
                    if k:
                        dve.wait_ge(S("hn_hi_ready"), layer * DT + k)
                        tt_(dst(hn_lo, k - 1), dst(hn, k - 1), dst(hn_hi, k - 1), ALU.subtract).then_inc(S("hn_split"), 1)
                first = at[name]
                turns = 2 * FT // SLOTS

                def product(pair, turn=None):
                    t = first + 2 * pair + 1
                    more = lambda n, per: n if turn is None else turn * per + n
                    dve.wait_ge(tile_done, more(done(t), SLOTS))
                    dve.wait_ge(evacuated[(t - 1) % BANKS], more(freed(t - 1), SLOTS // BANKS))
                    place = pair if turn is None else turn * (SLOTS // 2) + pair
                    tile = lambda a: a[:, bass.ds(place, 1), 0:cols].rearrange("p a b -> p (a b)")
                    x = ff_gate[:, pair % 2, 0:cols]
                    tt_(x, x, bank[t % BANKS][:, 0:cols], ALU.mult).then_inc(evacuated[t % BANKS], 1)
                    dve.wait_ge(evacuated[t % BANKS], more(freed(t), SLOTS // BANKS))
                    nc.vector.tensor_copy(tile(ff_hi), x).then_inc(S("ff_hi_ready"), 1)
                    dve.wait_ge(S("ff_hi_ready"), more(layer * FT + pair + 1, SLOTS // 2))
                    tt_(tile(ff_lo), x, tile(ff_hi), ALU.subtract).then_inc(S("ff_split"), 1)

                with dve.Fori(0, turns) as r:
                    for j in range(SLOTS // 2):
                        product(j, r)
                for pair in range(turns * SLOTS // 2, FT):
                    product(pair)

            feed_forward(0, T0, lambda k: h[:, k, :], lambda a, k: a[:, k, :])
            add_tiles(at["down0"], T0, lambda k: h[:, k, :])

            norm_scale("mix1", T0)
            norm_apply(lambda k: h[:, k, :], lambda k: kvn[:, k, :], lambda k: V("kv", k), DT, rstd[:, :])
            norm_apply(lambda k: h[:, k, :], lambda k: hn[:, k, :], lambda k: V("mix1", k), DT, rstd[:, :])

            def rotate(src, free, dst, c0, cols):
                c, s = C("cos_m", c0, cols), C("sin_m", c0, cols)
                tt_(mrope_t[:, 0, 0:cols], src[:, 0:cols], c, ALU.mult)
                for q in range(4):
                    of, to = slice(32 * q, 32 * q + 32), slice(32 * (q ^ 1), 32 * (q ^ 1) + 32)
                    last = tt_(mrope_t[to, 1, 0:cols], src[of, 0:cols], s[of], ALU.mult)
                last.then_inc(free[0], 1)
                dve.wait_ge(*free)
                tt_(dst, mrope_t[:, 0, 0:cols], mrope_t[:, 1, 0:cols], ALU.add).then_inc(S("q_roped"), 1)
                rotated[0] += 1
                dve.wait_ge(S("q_roped"), rotated[0])

            rotated = [0]

            def rotate_tile(t, dst, c0, cols):
                src, sem_free = take(t)
                rotate(src, (sem_free, freed(t)), dst, c0, cols)

            rotate_tile(at["kva"] + KVT, krope[:, 0, :], 0, T0)
            norm_scale("ckv", T0)
            norm_apply(lambda k: ckv[:, k, :], lambda k: ckv[:, k, :], lambda k: V("kva", k), KVT, rstd[:, :])
            norm_scale("cq", SEQ)
            norm_apply(lambda k: cq[:, k, :], lambda k: cq[:, k, :], lambda k: V("qa", k), QT, rstd[:, 0:SEQ])
            for t in range(4):
                rotate_tile(at["qr"] + t, qrope[:, t, :], META, SEQ)

            def attention(tag, heads, front, probs, parts, stat, turned=None):
                for i in range(heads + 1):
                    if i < heads:
                        dve.wait_ge(S(tag + "_scored"), i + 1)
                        if i >= 2:
                            dve.wait_ge(S(tag + "_turned"), i - 1)
                        link(front(i, bank[4 + i % 2], probs[:, i % 2, :]))
                        s = stat(i)
                        for j, (lo, hi) in enumerate(parts):
                            last = nc.vector.tensor_reduce(s[:, j:j + 1], probs[:, i % 2, lo:hi], AX, ALU.max)
                        link(last)
                        ts_(s[:, 2:4], s[:, 0:2], -1.0, None, ALU.mult).then_inc(S(tag + "_max"), 1)
                    if i >= 1:
                        j = i - 1
                        dve.wait_ge(S(tag + "_exp"), i)
                        s = stat(j)
                        link(nc.vector.reciprocal(s[:, 6:8], s[:, 4:6]))
                        for n, (lo, hi) in enumerate(parts):
                            a = probs[:, j % 2, lo:hi]
                            last = ts_(a, a, s[:, 6 + n:7 + n], None, ALU.mult)
                        last.then_inc(S(tag + "_p"), 1)
                        if turned:
                            turned(j)

            scale = (NOPE + ROPE) ** -0.5

            def mla_front(i, src, dst):
                return stt(dst, src[:, 0:MLA_W], scale, C("mask", 0, MLA_W), ALU.mult, ALU.add)

            def mla_turned(j):
                dve.wait_ge(S("mla_turnedm"), j + 1)
                if j:
                    dve.wait_ge(tile_done, done(at["am"] + j - 1))
                nc.vector.tensor_copy(pt_meta[0:META, 0, :], bank[7][0:META, 0:SEQ]).then_inc(S("mla_ptm"), 1)

            attention("mla", MH, mla_front, p_m, [(0, META + P), (META + P, MLA_W)],
                      lambda i: stats[:, 8 * i:8 * i + 8], mla_turned)
            add_tiles(at["wo1"], SEQ, lambda k: h[:, k, XC])
            feed_forward(1, SEQ, lambda k: h[:, k, XC], lambda a, k: a[:, k, XC])
            add_tiles(at["down1"], SEQ, lambda k: h[:, k, XC])
            norm_scale("final", SEQ)
            norm_apply(lambda k: h[:, k, XC], lambda k: h[:, k, XC], lambda k: V("final", k), DT, rstd[:, 0:SEQ])

            norm_scale("n1", SEQ)
            norm_apply(lambda k: h[:, k, XC], lambda k: hn[:, k, 0:SEQ],
                       lambda k: mod[:, DT + k:DT + k + 1], DT, rstd[:, 0:SEQ])
            nc.vector.memset(raw_b[:, :, 0:CONV - 1], 0.0)
            dve.wait_ge(S("ba_done"), 1)
            ba = bank[4][:, 0:16].rearrange("p (t c) -> p t c", t=2)
            two = lambda a: a.rearrange("p (t c) -> p t c", t=2)
            nc.vector.tensor_copy(two(M("b", 0, 8)), ba[:, :, 0:BH])
            link(tt_(two(M("a", 0, 8)), ba[:, :, BH:2 * BH], two(V("dt", 0, 8)), ALU.add))
            stt(M("abs", 0, 8), M("a", 0, 8), -1.0, M("a", 0, 8), ALU.mult, ALU.max).then_inc(S("ba_split"), 1)
            dve.wait_ge(S("beta_ready"), 1)
            dve.wait_ge(S("softplus_ln"), 1)
            link(stt(M("sp", 0, 8), M("a", 0, 8), 0.0, M("sp", 0, 8), ALU.max, ALU.add))
            stt(M("g", 0, 8), M("sp", 0, 8), -1.0, M("ea", 0, 8), ALU.mult, ALU.mult).then_inc(S("g_ready"), 1)

            def conv(t0):
                for j in range(CONV):
                    for t in range(t0, t0 + 4):
                        if j == 0:
                            wait_stored(dve, at["qkvb"] + t)
                        x, w = raw_b[:, t, j:j + SEQ], V("conv", t * CONV + j)
                        if j == 0:
                            last = ts_(cb[:, t, :], x, w, None, ALU.mult)
                        else:
                            last = stt(cb[:, t, :], x, w, cb[:, t, :], ALU.mult, ALU.add)
                            if j == CONV - 1:
                                last.then_inc(S("conv_done"), 1)
                    if j < CONV - 1:
                        link(last)

            conv(0)
            conv(4)
            dve.wait_ge(S("g_summed"), 1)
            link(nc.vector.tensor_copy(M("G", 0, 8), bank[5][:, 0:8]))
            tt_(M("R", 0, 8), bank[5][:, 8:16], M("G", 0, 8), ALU.subtract)
            nc.vector.tensor_copy(M("H", 0, 16), bank[5][:, 16:32]).then_inc(S("g_stored"), 1)
            dve.wait_ge(S("g_exp"), 1)
            link(tt_(M("bg", 0, 8), M("beta", 0, 8), M("eG", 0, 8), ALU.mult))
            dve.wait_ge(S("exp_rows"), 1)
            for p in range(NP):
                last = ts_(decT[:, p, :], bank[6 + p // 4][:, (p % 4) * P:(p % 4 + 1) * P], M("G", G_COL[p]), 0.0,
                           ALU.subtract, ALU.min)
            last.then_inc(S("dec_diff"), 1)
            dve.wait_ge(S("dec_exp"), 1)
            link(tt_(decT[:, :, :], decT[:, :, :], spread(C("upto"), NP), ALU.mult))
            dve.wait_ge(S("row_beta"), 1)

            def half(a, j):
                return a[:, 4 * j:4 * j + 4, :]

            def psum(b):
                return bank[b][:, :].rearrange("p (a b) -> p a b", a=4)

            for j in range(2):
                last = tt_(half(LT, j), half(decT, j), psum(4 + j), ALU.mult)
            last.then_inc(S("beta_rows"), 1)
            conv(8)
            dve.wait_ge(S("l2_root"), 1)
            link(nc.vector.reciprocal(l2sq, l2sq))
            flat = cb.rearrange("p a b -> p (a b)")
            stt(flat[:, 0:BH * SEQ], flat[:, 0:BH * SEQ], BHD ** -0.5, l2sq[:, 0:BH * SEQ], ALU.mult, ALU.mult)
            tt_(flat[:, BH * SEQ:2 * BH * SEQ], flat[:, BH * SEQ:2 * BH * SEQ], l2sq[:, BH * SEQ:], ALU.mult)\
                .then_inc(S("l2_done"), 1)
            dve.wait_ge(S("gram_done"), 1)
            for j in range(2):
                last = tt_(half(LT, j), half(LT, j), psum(4 + j), ALU.mult)
            last.then_inc(S("lt_ready"), 1)
            dve.wait_ge(S("qk_done"), 1)
            for j in range(2):
                last = tt_(half(PT, j), half(decT, j), psum(6 + j), ALU.mult)
            last.then_inc(S("pt_ready"), 1)
            tt_(qg, qg, TM[:, :, :], ALU.mult)
            dve.wait_ge(S("k_turned"), 1)
            dve.wait_ge(S("v_turned"), 1)
            dve.wait_ge(S("conv_silu"), 12)
            for dst, first, name in ((k_tok, 4, "bg"), (kd, 4, "eR"), (v_tok, 6, "beta")):
                per = M(name, 0, 8).rearrange("p (t a) -> p a t", t=2)
                for j in range(2):
                    last = tt_(half(dst, j).rearrange("p (a t) b -> p a t b", t=2),
                               psum(first + j).rearrange("p (a t) b -> p a t b", t=2),
                               per[:, 2 * j:2 * j + 2, :].unsqueeze(3).to_broadcast([P, 2, 2, P]), ALU.mult)
            last.then_inc(S("tok_ready"), 1)

            def level(lv):
                tt_(ML[:, :, :], LT[:, :, :], spread(C("level", lv * P), NP), ALU.mult).then_inc(S("ml_ready"), 1)

            dve.wait_ge(S("lt_ready"), 1)
            level(0)
            for lv in range(6):
                dve.wait_ge(S("mx_done"), lv + 1)
                if lv == 0:
                    dve.wait_ge(S("ml_ready"), 1)
                    tt_(Y[:, :, :], spread(ident, NP), ML[:, :, :], ALU.subtract)
                    for j in range(2):
                        last = tt_(half(X, j), spread(ident, 4), psum(4 + j), ALU.subtract)
                    last.then_inc(S("inv_ready"), 1)
                    dve.wait_ge(S("inv_ready"), 1)
                    level(1)
                    continue
                if lv < 5:
                    level(lv + 1)
                dve.wait_ge(S("dy_done"), lv)
                if lv < 5:
                    dve.wait_ge(S("dx_done"), lv)
                for j in range(2):
                    last = tt_(half(Y, j), half(Y, j), psum(6 + j), ALU.subtract)
                if lv < 5:
                    for j in range(2):
                        last = tt_(half(X, j), half(X, j), psum(4 + j), ALU.subtract)
                last.then_inc(S("inv_ready"), 1)
            dve.wait_ge(S("u_stored"), 1)
            for c in range(4):
                R, tt = CHUNK * (c % 2), c // 2
                rows = slice(R, R + CHUNK)
                u = u_tok.rearrange("p (a t) b -> p a t b", t=2)[rows, :, tt, :]
                if c == 0:
                    nc.vector.tensor_copy(vn[rows], u).then_inc(S("vn_ready"), 1)
                else:
                    dve.wait_ge(S("ws_done"), c)
                    tt_(vn[rows], u, psum(4)[rows], ALU.subtract).then_inc(S("vn_ready"), 1)
                if c == 3:
                    break
                dve.wait_ge(S("ds_done"), c + 1)
                if c == 0:
                    nc.vector.tensor_copy(st, psum(6)).then_inc(S("state_ready"), 1)
                    continue
                for a in range(BH):
                    last = stt(st[:, a, :], st[:, a, :], M("eH", 8 * (c % 2) + tt * BH + a), psum(6)[:, a, :],
                               ALU.mult, ALU.add)
                last.then_inc(S("state_ready"), 1)

            def ob_norm(j):
                ob = o_b.rearrange("p a b -> p (a b)")
                if j < 4:
                    if j == 0:
                        dve.wait_ge(S("ob_rooted"), 1)
                    part = obsq[:, j * SEQ:(j + 1) * SEQ]
                    nc.vector.reciprocal(part, part).then_inc(S("ob_inverted"), 1)
                elif j == 4:
                    dve.wait_ge(S("ob_inverted"), 4)
                    tt_(ob, ob, obsq, ALU.mult).then_inc(S("ob_normed"), 1)
                elif j == 5:
                    dve.wait_ge(S("ob_normed"), 1)
                    wait_stored(dve, at["z"] + BH - 1)
                    stt(ob, z_b.rearrange("p a b -> p (a b)"), V("onorm"), ob, ALU.mult, ALU.mult)\
                        .then_inc(S("ob_ready"), 1)

            dve.wait_ge(S("bias_loaded"), 16 * 2 * AH)

            def moba_front(i, src, dst):
                return stt(dst, src[:, 0:MOBA_W], AHD ** -0.5, bias_a[:, i, :], ALU.mult, ALU.add)

            attention("moba", AH, moba_front, p_a, [(0, P), (P, MOBA_W)], lambda i: stats[:, 64 + 8 * i:72 + 8 * i],
                      ob_norm)
            for k in range(DT):
                t = at["up"] + 2 * k
                src, free = take(t)
                if k == 0:
                    wait_stored(dve, at["gates"] + 15)
                else:
                    dve.wait_ge(S("m_ready"), k)
                tt_(up_t[:, 0, :], gates[:, k, :], src[:, 0:SEQ], ALU.mult).then_inc(free, 1)
                src, free = take(t + 1)
                tt_(up_t[:, 1, :], gates[:, DT + k, :], src[:, 0:SEQ], ALU.mult).then_inc(free, 1)
                wait_stored(dve, t + 1)
                tt_(m_up[:, k, :], up_t[:, 0, :], up_t[:, 1, :], ALU.add).then_inc(S("m_ready"), 1)
            for k in range(DT):
                src, free = take(at["wout"] + k)
                stt(h[:, k, XC], src[:, 0:SEQ], mod[:, 2 * DT + k:2 * DT + k + 1], h[:, k, XC],
                    ALU.mult, ALU.add).then_inc(free, 1)
            norm_scale("n2", SEQ)
            norm_apply(lambda k: h[:, k, XC], lambda k: hn[:, k, 0:SEQ],
                       lambda k: mod[:, 4 * DT + k:4 * DT + k + 1], DT, rstd[:, 0:SEQ])

            dve.wait_ge(S("logits_done"), 1)
            red = nc.vector.tensor_reduce

            def per_token(a, n):
                return a.unsqueeze(2).to_broadcast([P, 2, n])

            def first_of_max(values, n, top, hit, first, one, shape):
                link(red(router(top), values, AX, ALU.max))
                link(tt_(shape(hit), values, per_token(router(top), n), ALU.is_equal))
                iota = C("iota", 0, 16).rearrange("p (a b) -> p a b", a=2)[:, :, 0:n]
                link(stt(shape(hit), shape(hit), -64.0, iota, ALU.mult, ALU.add))
                link(red(router(first), shape(hit), AX, ALU.min))
                link(tt_(shape(one), shape(hit), per_token(router(first), n), ALU.is_equal))

            lg = router("logits", 2)
            link(tt_(lg, bank[4][:, 0:72].rearrange("p (a b) -> p a b", a=2),
                     V("b36", 0, 72).rearrange("p (a b) -> p a b", a=2), ALU.add))
            first_of_max(lg[:, :, 0:NG], NG, "gmax", "g_hit", "g_first", "g_one", lambda a: router(a, 2))
            tt_(router("g_diff", 2), lg[:, :, 0:NG], per_token(router("gmax"), NG), ALU.subtract)\
                .then_inc(S("group_diff"), 1)
            for tt in range(2):
                prod = router("prod")[:, tt * 32:tt * 32 + 32].rearrange("p (g e) -> p g e", g=NG)
                last = tt_(prod, lg[:, tt, NG:].rearrange("p (g e) -> p g e", g=NG),
                           router("g_one", 2)[:, tt, :].unsqueeze(2).to_broadcast([P, NG, EPG]), ALU.mult)
            link(last)
            for tt in range(2):
                prod = router("prod")[:, tt * 32:tt * 32 + 32].rearrange("p (g e) -> p e g", g=NG)
                last = red(router("le", 2)[:, tt, :], prod, AX, ALU.add)
            link(last)
            first_of_max(router("le", 2), EPG, "m1", "hit1", "first1", "one1", lambda a: router(a, 2))
            link(stt(router("le2"), router("one1"), NEG, router("le"), ALU.mult, ALU.add))
            first_of_max(router("le2", 2), EPG, "m2", "hit2", "first2", "one2", lambda a: router(a, 2))
            tt_(router("t_diff"), router("m2"), router("m1"), ALU.subtract).then_inc(S("top_diff"), 1)
            dve.wait_ge(S("group_exp"), 1)
            link(red(router("g_sum"), router("g_exp", 2), AX, ALU.add))
            nc.vector.reciprocal(router("g_top"), router("g_sum"))
            dve.wait_ge(S("top_exp"), 1)
            link(ts_(router("t_sum"), router("t_exp"), 1.0, None, ALU.add))
            link(nc.vector.reciprocal(router("t_sum"), router("t_sum")))
            link(tt_(router("w1"), router("t_sum"), router("g_top"), ALU.mult))
            link(tt_(router("w2"), router("w1"), router("t_exp"), ALU.mult))
            tt_(router("hit1", 2), router("one1", 2), per_token(router("w1"), EPG), ALU.mult)
            link(tt_(router("hit2", 2), router("one2", 2), per_token(router("w2"), EPG), ALU.mult))
            tt_(router("hit"), router("one1"), router("one2"), ALU.add)
            link(tt_(router("ce"), router("hit1"), router("hit2"), ALU.add))
            for tt in range(2):
                last = tt_(comb[:, tt, :].rearrange("p (g e) -> p g e", g=NG),
                           router("ce", 2)[:, tt, :].unsqueeze(1).to_broadcast([P, NG, EPG]),
                           router("g_one", 2)[:, tt, :].unsqueeze(2).to_broadcast([P, NG, EPG]), ALU.mult)
            for tt in range(2):
                last = tt_(router("used", 2)[:, tt, :].rearrange("p (g e) -> p g e", g=NG),
                           router("hit", 2)[:, tt, :].unsqueeze(1).to_broadcast([P, NG, EPG]),
                           router("g_one", 2)[:, tt, :].unsqueeze(2).to_broadcast([P, NG, EPG]), ALU.mult)
            last.then_inc(S("used_ready"), 1)
            dve.wait_ge(S("used_ready"), 1)
            dve.wait_ge(S("ranked"), 1)
            link(stt(router("rank"), bank[4][:, 0:2 * NE], FAR, router("used"), ALU.add, ALU.mult))
            ts_(router("rank"), router("rank"), FAR, None, ALU.subtract)
            link(red(router("most"), bank[4][:, 2 * NE:3 * NE], AX, ALU.max))
            link(ts_(router("over"), router("most"), float(CAP), 1.0, ALU.is_gt, ALU.add))
            for n in range(2, SEQ // CAP - 1):
                link(stt(router("over"), router("most"), float(n * CAP), router("over"), ALU.is_gt, ALU.add))
            nc.vector.tensor_copy(zeroed, zero_w[:, :].unsqueeze(1).to_broadcast([P, 2 * (DT + 2) * 3 * CAP // P, P]))
            stt(rounds_t[:, :], router("most"), float((SEQ // CAP - 1) * CAP), router("over"), ALU.is_gt,
                ALU.add).then_inc(S("rounds_ready"), 1)
            dve.wait_ge(S("rounds_ready"), 1)

            def expert_low(g, m):
                dve.wait_ge(S("e_hi_ready"), g * PAIR_UNITS + (m + 1))
                tt_(w_lo[:, m % SPLITS, :], ring[:, (EXPERTS_FIRST + m) % SLOTS, :], w_hi[:, m % SPLITS, :],
                    ALU.subtract).then_inc(S("e_lo_ready"), 1)

            def in_low(g, part):
                dve.wait_ge(S("in_hi_ready"), g * 2 + (part + 1))
                tt_(two_experts(e_in_lo, 4 * part, 4), gathered(part), two_experts(e_in_hi, 4 * part, 4),
                    ALU.subtract).then_inc(S("in_split"), 1)

            def select(a, pair, weighted):
                for tt in range(2):
                    for j in range(2):
                        col = pair * 2 + (tt * NE + j)
                        rank = rt[:, bass.ds(col + RT["rank"][0], 1)]
                        dst = a[:, tt, j * CAP:(j + 1) * CAP]
                        if weighted:
                            share = rt[:, bass.ds(col + RT["comb"][0], 1)]
                            last = ts_(dst, C("slot", 0, CAP), rank, share, ALU.is_equal, ALU.mult)
                        else:
                            last = ts_(dst, C("slot", 0, CAP), rank, None, ALU.is_equal)
                last.then_inc(S("sel_w_ready" if weighted else "sel_ready"), 1)

            def expert_pair(r, pair, final):
                g = r * PAIRS + pair
                for m in range(AHEAD, GATE_UP_UNITS):
                    expert_low(g, m)
                if not final:
                    select(sel, pair + 1, False)
                for m in range(GATE_UP_UNITS, GATE_UP_UNITS + AHEAD):
                    expert_low(g, m)
                dve.wait_ge(S("e_gate_ready"), g + 1)
                tt_(flat2(e_act), flat2(e_gate), bank[2][:, EF:2 * EF], ALU.mult).then_inc(S("e_act_ready"), 1)
                if not final:
                    in_low(g + 1, 0)
                select(sel_w, pair, True)
                dve.wait_ge(S("act_hi_ready"), g + 1)
                tt_(two_experts(act_lo, 0, 2), turned_act, two_experts(act_hi, 0, 2), ALU.subtract)\
                    .then_inc(S("act_split"), 1)
                nc.vector.tensor_copy(sel_t[:, 0, :], bank[1][:, 0:SEQ]).then_inc(S("sel_t_stored"), 1)
                if not final:
                    in_low(g + 1, 1)
                expert_low(g, PAIR_UNITS - 1)
                if not final:
                    for m in range(AHEAD):
                        expert_low(g + 1, m)
                dve.wait_ge(S("down_done"), g * 2 + 2)
                nc.vector.tensor_copy(e_out[:, 1, :], bank[3][:, :]).then_inc(S("out_stored_v"), 1)

            dve_rounds = dve.value_load(rounds_t[0:1, 0:1], min_val=1, max_val=SEQ // CAP)
            with dve.Fori(0, dve_rounds) as r:
                select(sel, 0, False)
                for m in range(AHEAD):
                    expert_low(r * PAIRS, m)
                in_low(r * PAIRS, 0)
                in_low(r * PAIRS, 1)
                with dve.Fori(0, PAIRS - 1) as pair:
                    expert_pair(r, pair, False)
                expert_pair(r, PAIRS - 1, True)
                dve.wait_ge(S("sel_w_ready"), r * PAIRS + PAIRS)
                ts_(router("rank"), router("rank"), float(CAP), None, ALU.subtract).then_inc(S("rank_shifted"), 1)
                dve.wait_ge(S("rank_shifted"), r + 1)
            dve.wait_ge(S("moe_done"), dve_rounds)
            for k in range(DT):
                stt(h[:, k, XC], bank[4 + k // 2][:, (k % 2) * SEQ:(k % 2 + 1) * SEQ],
                    mod[:, 5 * DT + k:5 * DT + k + 1], h[:, k, XC], ALU.mult, ALU.add).then_inc(S("moe_added"), 1)
            norm_scale("final2", SEQ)
            norm_apply(lambda k: h[:, k, XC], lambda k: hn[:, k, 0:SEQ], lambda k: V("final2", k), DT, rstd[:, 0:SEQ])


def kernel(**inputs):
    import concourse.bacc as bacc
    from concourse.bass_utils import run_bass_kernel_spmd

    i = {name: np.asarray(a) for name, a in inputs.items()}
    tokens = np.concatenate([i["meta"], i["x"][0]], axis=0)
    arrays = {
        "weights": weight_stream(i),
        "vectors": np.ascontiguousarray(vectors(i)),
        "tables": constants(),
        "tokens": np.ascontiguousarray(tokens.T.reshape(DT, P, T0).transpose(1, 0, 2)),
        "rel_bias": np.ascontiguousarray(i["rel_bias_2"]),
    }
    nc = bacc.Bacc("TRN2", target_bir_lowering=False, num_devices=1)
    args = [nc.dram_tensor(name, a.shape, F32, kind="ExternalInput").ap() for name, a in arrays.items()]
    skew = nc.dram_tensor("skew", (AH, P, 512), F32, kind="Internal").ap()
    out = nc.dram_tensor("out", (P, DT, SEQ), F32, kind="ExternalOutput").ap()
    build(nc, *args, skew, out)
    r = run_bass_kernel_spmd(nc, [arrays], core_ids=[0])
    got = np.asarray(r.results[0]["out"])
    return np.ascontiguousarray(got.transpose(2, 1, 0).reshape(1, SEQ, D))
```
